# Optimizing a Trainium2 kernel written in Bass

```python
import math, functools
import jax, jax.numpy as jnp
from jax import lax
import numpy as np

D_MODEL = 1024
BATCH = 1
SEQ = 1024
DEPTH = 1
DEC_BATCH = 8
DEC_SEQ = 1
PAST_LEN = 4096
PAGE_SIZE = 128

N_HEADS = 16
HEAD_DIM = 64
N_KV_HEADS = 4
N_IDX_HEADS = 8
IDX_DIM = 64
TOPK_MAX = 256
Q_BLOCK = 128
N_BUCKETS = 32
MAX_DISTANCE = 128
SSD_EXPAND = 2
D_INNER = SSD_EXPAND * D_MODEL
SSD_HEAD_DIM = 64
SSD_HEADS = D_INNER // SSD_HEAD_DIM
SSD_GROUPS = 4
D_STATE = 128
CONV_WIDTH = 4
SSD_CHUNK = 128
CONV_DIM = D_INNER + 2 * SSD_GROUPS * D_STATE
D_FF = 2816
N_SUBLAYERS = 3
EPS = 1e-6
ATT_Q = N_HEADS * HEAD_DIM
ATT_KV = N_KV_HEADS * HEAD_DIM
IDX_Q = N_IDX_HEADS * IDX_DIM
IN_WIDTHS = (ATT_Q, ATT_KV, ATT_KV, IDX_Q, IDX_DIM, N_IDX_HEADS, D_INNER, CONV_DIM, SSD_HEADS, D_MODEL, D_MODEL)
IN_DIM = ATT_Q + 2 * ATT_KV + IDX_Q + IDX_DIM + N_IDX_HEADS + D_INNER + CONV_DIM + SSD_HEADS + 2 * D_MODEL

kernel_name = 'hybrid_dsa_ssd_macaron_decoder_step'

def split_points():
    return np.cumsum(np.array(IN_WIDTHS))[:-1].tolist()

def rmsnorm(x, g):
    xf = x.astype(jnp.float32)
    y = xf * lax.rsqrt(jnp.mean(xf * xf, axis=-1, keepdims=True) + EPS)
    return (y * g.astype(jnp.float32)).astype(x.dtype)

def modulate(h, shift, scale):
    return h * (1.0 + scale) + shift

def swiglu(h, w_in, w_out):
    gate, up = jnp.split(h @ w_in, 2, axis=-1)
    return (jax.nn.silu(gate) * up) @ w_out

def t5_bucket(dist):
    n = jnp.maximum(dist, 0)
    max_exact = N_BUCKETS // 2
    nf = jnp.maximum(n, 1).astype(jnp.float32)
    large = max_exact + (jnp.log(nf / max_exact) / math.log(MAX_DISTANCE / max_exact)
                         * (N_BUCKETS - max_exact)).astype(jnp.int32)
    large = jnp.minimum(large, N_BUCKETS - 1)
    return jnp.where(n < max_exact, n, large)

def dsa_queries(q, qi, wi, qpos, ki_all, fetch_kv, n_top, rel_bias):
    L = ki_all.shape[0]
    T = q.shape[0]
    kpos = jnp.arange(L, dtype=jnp.int32)
    dots = jnp.einsum('thd,sd->ths', qi, ki_all).astype(jnp.float32)
    score = jnp.einsum('ths,th->ts', jax.nn.relu(dots), wi.astype(jnp.float32)) * ((N_IDX_HEADS * IDX_DIM) ** -0.5)
    score = jnp.where(kpos[None, :] <= qpos[:, None], score, -jnp.inf)
    _, idx = lax.top_k(score, n_top)
    valid = idx <= qpos[:, None]
    k_sel, v_sel = fetch_kv(idx)
    qg = q.reshape(T, N_KV_HEADS, N_HEADS // N_KV_HEADS, HEAD_DIM)
    logits = jnp.einsum('tngd,tjnd->tngj', qg, k_sel).astype(jnp.float32) * (HEAD_DIM ** -0.5)
    bias = rel_bias[t5_bucket(qpos[:, None] - idx)]
    bias = jnp.transpose(bias, (0, 2, 1)).reshape(T, N_KV_HEADS, N_HEADS // N_KV_HEADS, n_top)
    logits = jnp.where(valid[:, None, None, :], logits + bias.astype(jnp.float32), -jnp.inf)
    p = jax.nn.softmax(logits, axis=-1).astype(v_sel.dtype)
    o = jnp.einsum('tngj,tjnd->tngd', p, v_sel)
    return o.reshape(T, N_HEADS * HEAD_DIM)

def dsa_prompt(q, k, v, qi, ki, wi, rel_bias):
    S = q.shape[1]
    n_top = min(TOPK_MAX, S // 4)
    nblk = S // Q_BLOCK
    qpos = jnp.arange(S, dtype=jnp.int32).reshape(nblk, Q_BLOCK)

    def per_seq(args):
        q_b, k_b, v_b, qi_b, ki_b, wi_b = args
        fetch = lambda idx: (k_b[idx], v_b[idx])

        def per_block(bargs):
            qq, qqi, ww, pp = bargs
            return dsa_queries(qq, qqi, ww, pp, ki_b, fetch, n_top, rel_bias)

        out = lax.map(per_block, (q_b.reshape(nblk, Q_BLOCK, N_HEADS, HEAD_DIM),
                                  qi_b.reshape(nblk, Q_BLOCK, N_IDX_HEADS, IDX_DIM),
                                  wi_b.reshape(nblk, Q_BLOCK, N_IDX_HEADS), qpos))
        return out.reshape(S, N_HEADS * HEAD_DIM)

    return lax.map(per_seq, (q, k, v, qi, ki, wi))

def dsa_sample(q, k_new, v_new, qi, ki_new, wi, cache_k, cache_v, cache_kidx, page_table, rel_bias):
    T = q.shape[1]
    n_pages = page_table.shape[1]
    past = n_pages * PAGE_SIZE
    n_top = min(TOPK_MAX, (past + T) // 4)
    qpos = past + jnp.arange(T, dtype=jnp.int32)

    def per_seq(args):
        q_b, kn, vn, qi_b, kin, wi_b, pt = args
        ki_all = jnp.concatenate([cache_kidx[pt].reshape(past, IDX_DIM), kin], axis=0)

        def fetch(idx):
            in_past = (idx < past)[..., None, None]
            page = pt[jnp.minimum(idx // PAGE_SIZE, n_pages - 1)]
            off = idx % PAGE_SIZE
            j = jnp.clip(idx - past, 0, T - 1)
            return (jnp.where(in_past, cache_k[page, off], kn[j]),
                    jnp.where(in_past, cache_v[page, off], vn[j]))

        return dsa_queries(q_b, qi_b, wi_b, qpos, ki_all, fetch, n_top, rel_bias)

    return lax.map(per_seq, (q, k_new, v_new, qi, ki_new, wi, page_table))

def causal_conv(xbc, conv_state, w, bias):
    full = jnp.concatenate([conv_state.astype(xbc.dtype), xbc], axis=1)
    out = lax.conv_general_dilated(full, w.astype(full.dtype)[:, None, :], window_strides=(1,), padding='VALID',
                                   dimension_numbers=('NWC', 'WIO', 'NWC'), feature_group_count=CONV_DIM)
    return jax.nn.silu(out + bias), full[:, -(CONV_WIDTH - 1):]

def ssd_scan(x, dt, A, Bm, Cm, h0):
    b, T = x.shape[:2]
    R = SSD_HEADS // SSD_GROUPS
    cl = min(SSD_CHUNK, T)
    nc = -(-T // cl)
    pad = nc * cl - T
    if pad:
        padT = lambda a: jnp.pad(a, [(0, 0), (0, pad)] + [(0, 0)] * (a.ndim - 2))
        x, dt, Bm, Cm = padT(x), padT(dt), padT(Bm), padT(Cm)
    Tp = nc * cl
    to_chunks = lambda a: jnp.moveaxis(a.reshape(b, nc, cl, *a.shape[2:]), 1, 0)
    xs = to_chunks(x.reshape(b, Tp, SSD_GROUPS, R, SSD_HEAD_DIM))
    dts = to_chunks(dt.reshape(b, Tp, SSD_GROUPS, R))
    Bs, Cs = to_chunks(Bm), to_chunks(Cm)
    Ar = A.reshape(SSD_GROUPS, R)
    tril = jnp.tril(jnp.ones((cl, cl), dtype=bool))[None, :, :, None, None]

    def step(h, inp):
        xc, dtc, Bc, Cc = inp
        acs = jnp.cumsum(dtc * Ar, axis=1)
        seg = acs[:, :, None] - acs[:, None, :]
        decay = jnp.exp(jnp.where(tril, seg, -jnp.inf))
        xdt = xc * dtc[..., None]
        cb = jnp.einsum('blgn,bsgn->blsg', Cc, Bc)
        y_diag = jnp.einsum('blsg,blsgr,bsgrp->blgrp', cb, decay, xdt)
        y_off = jnp.einsum('blgn,bgrpn,blgr->blgrp', Cc, h, jnp.exp(acs))
        to_end = jnp.exp(acs[:, -1:] - acs)
        h_new = jnp.exp(acs[:, -1])[..., None, None] * h + jnp.einsum('bsgn,bsgr,bsgrp->bgrpn', Bc, to_end, xdt)
        return h_new, y_diag + y_off

    h_fin, ys = lax.scan(step, h0.reshape(b, SSD_GROUPS, R, SSD_HEAD_DIM, D_STATE), (xs, dts, Bs, Cs))
    y = jnp.moveaxis(ys, 0, 1).reshape(b, Tp, SSD_HEADS, SSD_HEAD_DIM)[:, :T]
    return y, h_fin.reshape(b, SSD_HEADS, SSD_HEAD_DIM, D_STATE)

def ssd_branch(z, xbc, dt_raw, conv_state, ssm_state, p):
    b, T = z.shape[:2]
    xbc_c, conv_new = causal_conv(xbc, conv_state, p['conv_w'], p['conv_b'])
    xs, Bm, Cm = jnp.split(xbc_c.astype(jnp.float32), [D_INNER, D_INNER + SSD_GROUPS * D_STATE], axis=-1)
    xs = xs.reshape(b, T, SSD_HEADS, SSD_HEAD_DIM)
    Bm = Bm.reshape(b, T, SSD_GROUPS, D_STATE)
    Cm = Cm.reshape(b, T, SSD_GROUPS, D_STATE)
    dt = jax.nn.softplus(dt_raw.astype(jnp.float32) + p['dt_bias'].astype(jnp.float32))
    A = -jnp.exp(p['a_log'].astype(jnp.float32))
    y, h_new = ssd_scan(xs, dt, A, Bm, Cm, ssm_state.astype(jnp.float32))
    y = y + p['d_skip'].astype(jnp.float32)[:, None] * xs
    y = y.reshape(b, T, D_INNER) * jax.nn.silu(z.astype(jnp.float32))
    yg = y.reshape(b, T, SSD_GROUPS, D_INNER // SSD_GROUPS)
    yg = yg * lax.rsqrt(jnp.mean(yg * yg, axis=-1, keepdims=True) + EPS)
    y = yg.reshape(b, T, D_INNER) * p['norm_ssd'].astype(jnp.float32)
    return y.astype(z.dtype), h_new, conv_new

def trunk_layer(x, c, p, attend, conv_state, ssm_state):
    ada = jax.nn.silu(c) @ p['w_ada'] + p['b_ada']
    sh1, sc1, g1, sh2, sc2, g2, sh3, sc3, g3 = [a[:, None, :] for a in jnp.split(ada, 3 * N_SUBLAYERS, axis=-1)]
    h = modulate(rmsnorm(x, p['norm_ffn1']), sh1, sc1)
    x = x + 0.5 * g1 * swiglu(h, p['w_ffn1_in'], p['w_ffn1_out'])
    h = modulate(rmsnorm(x, p['norm_mix']), sh2, sc2)
    b, T, _ = h.shape
    q, k, v, qi, ki, wi, z, xbc, dt_raw, gate_a, gate_s = jnp.split(h @ p['w_in'], split_points(), axis=-1)
    q = q.reshape(b, T, N_HEADS, HEAD_DIM)
    k = k.reshape(b, T, N_KV_HEADS, HEAD_DIM)
    v = v.reshape(b, T, N_KV_HEADS, HEAD_DIM)
    qi = qi.reshape(b, T, N_IDX_HEADS, IDX_DIM)
    att = attend(q, k, v, qi, ki, wi)
    ssd_y, ssm_new, conv_new = ssd_branch(z, xbc, dt_raw, conv_state, ssm_state, p)
    merged = jax.nn.sigmoid(gate_a) * (att @ p['w_attn_out']) + jax.nn.sigmoid(gate_s) * (ssd_y @ p['w_ssd_out'])
    x = x + g2 * (merged @ p['w_out'])
    h = modulate(rmsnorm(x, p['norm_ffn2']), sh3, sc3)
    x = x + 0.5 * g3 * swiglu(h, p['w_ffn2_in'], p['w_ffn2_out'])
    return x, (k, v, ki, ssm_new, conv_new)

def setup_inputs(seed: int = 0) -> dict:
    key = jax.random.key(seed)
    ks = jax.random.split(key, 32)
    f32 = jnp.float32
    nrm = lambda kk, shape, scale: jax.random.normal(kk, shape, f32) * scale
    n_pages = PAST_LEN // PAGE_SIZE
    n_pool = (DEC_BATCH * n_pages * 5) // 4
    page_table = jax.random.permutation(ks[0], n_pool)[:DEC_BATCH * n_pages].reshape(DEC_BATCH, n_pages).astype(jnp.int32)
    dt0 = jnp.exp(jax.random.uniform(ks[1], (DEPTH, SSD_HEADS), f32) * (math.log(0.1) - math.log(0.001)) + math.log(0.001))
    dt_bias = dt0 + jnp.log(-jnp.expm1(-dt0))
    a_log = jnp.log(jax.random.uniform(ks[2], (DEPTH, SSD_HEADS), f32, 1.0, 16.0))
    gain = lambda kk, n: 1.0 + nrm(kk, (DEPTH, n), 0.02)
    return {
        'x_prompt': nrm(ks[3], (BATCH, SEQ, D_MODEL), 1.0),
        'x_sample': nrm(ks[4], (DEC_BATCH, DEC_SEQ, D_MODEL), 1.0),
        'c_prompt': nrm(ks[5], (BATCH, D_MODEL), 1.0),
        'c_sample': nrm(ks[6], (DEC_BATCH, D_MODEL), 1.0),
        'cache_k': nrm(ks[7], (DEPTH, n_pool, PAGE_SIZE, N_KV_HEADS, HEAD_DIM), 1.0),
        'cache_v': nrm(ks[8], (DEPTH, n_pool, PAGE_SIZE, N_KV_HEADS, HEAD_DIM), 1.0),
        'cache_kidx': nrm(ks[9], (DEPTH, n_pool, PAGE_SIZE, IDX_DIM), 1.0),
        'state_ssm': nrm(ks[10], (DEPTH, DEC_BATCH, SSD_HEADS, SSD_HEAD_DIM, D_STATE), 0.1),
        'state_conv': nrm(ks[11], (DEPTH, DEC_BATCH, CONV_WIDTH - 1, CONV_DIM), 1.0),
        'page_table': page_table,
        'w_ada': nrm(ks[12], (DEPTH, D_MODEL, 3 * N_SUBLAYERS * D_MODEL), D_MODEL ** -0.5),
        'b_ada': nrm(ks[13], (DEPTH, 3 * N_SUBLAYERS * D_MODEL), 0.02),
        'norm_ffn1': gain(ks[14], D_MODEL),
        'w_ffn1_in': nrm(ks[15], (DEPTH, D_MODEL, 2 * D_FF), D_MODEL ** -0.5),
        'w_ffn1_out': nrm(ks[16], (DEPTH, D_FF, D_MODEL), D_FF ** -0.5),
        'norm_mix': gain(ks[17], D_MODEL),
        'w_in': nrm(ks[18], (DEPTH, D_MODEL, IN_DIM), D_MODEL ** -0.5),
        'rel_bias': nrm(ks[19], (N_BUCKETS, N_HEADS), 0.5),
        'conv_w': nrm(ks[20], (DEPTH, CONV_WIDTH, CONV_DIM), CONV_WIDTH ** -0.5),
        'conv_b': nrm(ks[21], (DEPTH, CONV_DIM), 0.02),
        'a_log': a_log,
        'dt_bias': dt_bias,
        'd_skip': 1.0 + nrm(ks[22], (DEPTH, SSD_HEADS), 0.1),
        'norm_ssd': gain(ks[23], D_INNER),
        'w_attn_out': nrm(ks[24], (DEPTH, ATT_Q, D_MODEL), ATT_Q ** -0.5),
        'w_ssd_out': nrm(ks[25], (DEPTH, D_INNER, D_MODEL), D_INNER ** -0.5),
        'w_out': nrm(ks[26], (DEPTH, D_MODEL, D_MODEL), D_MODEL ** -0.5),
        'norm_ffn2': gain(ks[27], D_MODEL),
        'w_ffn2_in': nrm(ks[28], (DEPTH, D_MODEL, 2 * D_FF), D_MODEL ** -0.5),
        'w_ffn2_out': nrm(ks[29], (DEPTH, D_FF, D_MODEL), D_FF ** -0.5),
        'norm_final': 1.0 + nrm(ks[30], (D_MODEL,), 0.02),
    }

def reference(x_prompt, x_sample, c_prompt, c_sample, cache_k, cache_v, cache_kidx, state_ssm, state_conv, page_table,
              w_ada, b_ada, norm_ffn1, w_ffn1_in, w_ffn1_out, norm_mix, w_in, rel_bias, conv_w, conv_b, a_log, dt_bias,
              d_skip, norm_ssd, w_attn_out, w_ssd_out, w_out, norm_ffn2, w_ffn2_in, w_ffn2_out, norm_final):
    yp, ys = x_prompt, x_sample
    bp = x_prompt.shape[0]
    zero_conv = jnp.zeros((bp, CONV_WIDTH - 1, CONV_DIM), x_prompt.dtype)
    zero_ssm = jnp.zeros((bp, SSD_HEADS, SSD_HEAD_DIM, D_STATE), jnp.float32)
    outs_p, outs_s = [], []
    for l in range(DEPTH):
        p = {'w_ada': w_ada[l], 'b_ada': b_ada[l], 'norm_ffn1': norm_ffn1[l], 'w_ffn1_in': w_ffn1_in[l],
             'w_ffn1_out': w_ffn1_out[l], 'norm_mix': norm_mix[l], 'w_in': w_in[l], 'conv_w': conv_w[l],
             'conv_b': conv_b[l], 'a_log': a_log[l], 'dt_bias': dt_bias[l], 'd_skip': d_skip[l],
             'norm_ssd': norm_ssd[l], 'w_attn_out': w_attn_out[l], 'w_ssd_out': w_ssd_out[l], 'w_out': w_out[l],
             'norm_ffn2': norm_ffn2[l], 'w_ffn2_in': w_ffn2_in[l], 'w_ffn2_out': w_ffn2_out[l]}
        attend_p = functools.partial(dsa_prompt, rel_bias=rel_bias)
        attend_s = functools.partial(dsa_sample, cache_k=cache_k[l], cache_v=cache_v[l], cache_kidx=cache_kidx[l],
                                     page_table=page_table, rel_bias=rel_bias)
        yp, st_p = trunk_layer(yp, c_prompt, p, attend_p, zero_conv, zero_ssm)
        ys, st_s = trunk_layer(ys, c_sample, p, attend_s, state_conv[l], state_ssm[l])
        outs_p.append(st_p)
        outs_s.append(st_s)
    y_prompt = rmsnorm(yp, norm_final)
    y_sample = rmsnorm(ys, norm_final)
    stack = lambda outs, i: jnp.stack([o[i] for o in outs], axis=0)
    k_prompt, v_prompt, kidx_prompt = stack(outs_p, 0), stack(outs_p, 1), stack(outs_p, 2)
    ssm_prompt, conv_prompt = stack(outs_p, 3), stack(outs_p, 4)
    k_sample, v_sample, kidx_sample = stack(outs_s, 0), stack(outs_s, 1), stack(outs_s, 2)
    ssm_sample, conv_sample = stack(outs_s, 3), stack(outs_s, 4)
    return (y_prompt, y_sample, k_prompt, v_prompt, kidx_prompt, ssm_prompt, conv_prompt,
            k_sample, v_sample, kidx_sample, ssm_sample, conv_sample)


_drawn_inputs = setup_inputs


def setup_inputs(seed=0):
    import zlib

    import numpy as np

    out = dict(_drawn_inputs(seed))
    spreads = {}
    factors = {'norm_ffn1': 4.707,
     'd_skip': 3.982,
     'norm_ssd': 43.44,
     'norm_ffn2': 22.68,
     'norm_final': 19.891,
     'cache_k': 6.795,
     'cache_v': 5.887,
     'cache_kidx': 6.042,
     'rel_bias': 8.0}
    for name, (base, spread) in spreads.items():
        noise = np.random.default_rng([zlib.crc32(name.encode()), seed]).standard_normal(out[name].shape)
        drawn = base * np.exp(spread * noise) if base else spread * noise
        out[name] = __import__('jax').numpy.asarray(drawn.astype(out[name].dtype))
    for name, factor in factors.items():
        out[name] = (out[name] * factor).astype(out[name].dtype)
    return out
```

```python
from contextlib import ExitStack

import numpy as np

import concourse.bass as bass
from concourse import mybir

P = 128
DM, SEQ, NB = 1024, 1024, 8
TOK = SEQ + NB
NCH = 3
NC = TOK // NCH
LASTP = NC - NB
KT = DM // P
TB = SEQ // P
DFF = 2816
FT = DFF // P
NH, HD, NKV = 16, 64, 4
NIH, ID = 8, 64
TOPK = 256
PAST, PAGE, NPAGE, NPOOL = 4096, 128, 32, 320
NBUCKET, MAXD = 32, 128
DI, SH, SG, DS, CW = 2048, 32, 4, 128, 4
CONVD = DI + 2 * SG * DS
XT = 6
EPS = 1e-6
AT = 15
QT0, KT0, QI0, KI0 = 0, 8, 10, 14
VW = NKV * HD + NIH + SH
BIG = 1.0e30
CAUSAL, TAKEN = -3.0e38, -3.3e38
WIN = 2 * P
NA = 9 * KT
NCOND = 1 + NB

F32 = mybir.dt.float32
F16 = mybir.dt.float16
I32 = mybir.dt.int32
U32 = mybir.dt.uint32
ALU = mybir.AluOpType
ACT = mybir.ActivationFunctionType
AX = mybir.AxisListType.X


class Chain:

    def __init__(self, eng, sem, tick=None):
        self.eng, self.sem, self.tick, self.n, self.off = eng, sem, tick, 0, 0

    def link(self, ins):
        self.n += 1
        ins.then_inc(self.sem, 1)
        self.eng.wait_ge(self.sem, self.off + self.n)
        if self.tick is not None:
            self.eng.sem_inc(self.tick, 1)

    def loop(self, i, per):
        self.off, self.start, self.per = i * per, self.n, per

    def done(self, times):
        assert self.n - self.start == self.per, (self.n - self.start, self.per)
        self.off, self.n = 0, self.start + self.per * times


def carve(arena, at, shape):
    n = int(np.prod(shape[1:]))
    a = arena[0:shape[0], at:at + n]
    assert at + n <= arena.shape[1], (at, n)
    names = "abcd"[:len(shape) - 1]
    if len(names) > 1:
        a = a.rearrange(f"p ({' '.join(names)}) -> p {' '.join(names)}", **dict(zip(names, shape[1:])))
    return at + n, a


class Phase:

    def __init__(self, nc, name, arena=None, start=0, banks=None):
        self.nc, self.name, self.ctx, self.arena, self.at = nc, name, ExitStack(), arena, start
        self.banks, self.bank, self.sems, self.blocks = banks, 0, [], ExitStack()

    def __enter__(self):
        return self

    def __exit__(self, *a):
        self.blocks.__exit__(*a)
        for s in self.sems:
            self.nc.gpsimd.sem_clear(s)
        self.nc.all_engine_barrier()
        return self.ctx.__exit__(*a)

    def sem(self, name):
        s = self.ctx.enter_context(self.nc.semaphore(f"{self.name}_{name}"))
        self.sems.append(s)
        return s

    def sb(self, name, shape, dt=F32):
        if self.arena is not None:
            self.at, a = carve(self.arena, self.at, shape)
            return a
        return self.ctx.enter_context(self.nc.sbuf_tensor(f"{self.name}_{name}", shape, dt))

    def ps(self, name, shape, dt=F32):
        if self.banks is not None:
            n, a = carve(self.banks, self.bank, shape)
            self.bank = -(-n // 512) * 512
            return a
        return self.ctx.enter_context(self.nc.psum_tensor(f"{self.name}_{name}", shape, dt))

    def block(self):
        return self.blocks.enter_context(self.nc.Block())


def adaln(nc, d, ada, sg):
    SLOTS = 4
    with Phase(nc, "ada") as ph:
        w = ph.sb("w", [P, SLOTS, KT, P])
        c = ph.sb("c", [P, KT, NCOND])
        b = ph.sb("b", [P, NA])
        gains = ph.sb("gains", [P, 3, KT])
        ps = [ph.ps(f"ps{s}", [P, 512]) for s in range(2 * SLOTS)]
        w_in = [ph.sem(f"w_in{s}") for s in range(SLOTS)]
        c_in, c_act, mm, evac, fix = (ph.sem(n) for n in ("c_in", "c_act", "mm", "evac", "fix"))
        block = ph.block()
        ROUNDS = NA // SLOTS
        assert ROUNDS % 2 == 0

        @block.sync
        def _(sp):
            for s in range(SLOTS):
                sp.dma_start(w[:, s], d["w_ada"][s]).then_inc(w_in[s], 16)
            with sp.Fori(1, ROUNDS) as i:
                for s in range(SLOTS):
                    sp.wait_ge(mm, SLOTS * (i - 1) + s + 1)
                    sp.dma_start(w[:, s], d["w_ada"][SLOTS * i + s]).then_inc(w_in[s], 16)

        @block.scalar
        def _(act):
            act.dma_start(c[:], d["c"]).then_inc(c_in, 16)
            act.dma_start(b[:], d["b_ada"]).then_inc(c_in, 16)
            act.dma_start(gains[:], d["gains"]).then_inc(c_in, 16)
            act.wait_ge(c_in, 48)
            nc.scalar.activation(c[:], c[:], ACT.Silu).then_inc(c_act, 1)

        @block.tensor
        def _(pe):
            pe.wait_ge(c_act, 1)
            with pe.Fori(0, ROUNDS // 2) as r:
                for half in range(2):
                    for s in range(SLOTS):
                        pe.wait_ge(w_in[s], 32 * r + 16 * (half + 1))
                        if s == 0 and half == 0:
                            pe.wait_ge(evac, 2 * r)
                        for k in range(KT):
                            m = nc.tensor.matmul(ps[SLOTS * half + s][:, 0:NCOND], w[:, s, k], c[:, k],
                                                 start=k == 0, stop=k == KT - 1)
                        m.then_inc(mm, 1)

        @block.vector
        def _(dve):
            dve.wait_ge(c_in, 48)
            with dve.Fori(0, ROUNDS // 2) as r:
                for half in range(2):
                    for s in range(SLOTS):
                        dve.wait_ge(mm, (2 * r + half) * SLOTS + s + 1)
                        t = (2 * r + half) * SLOTS + s
                        v = nc.vector.tensor_scalar(ada[:, t], ps[SLOTS * half + s][:, 0:NCOND],
                                                    b[:, bass.ds(t, 1)], None, ALU.add)
                    v.then_inc(evac, 1)
            dve.wait_ge(evac, ROUNDS)
            n = 0
            for s in range(3):
                scale = ada[:, (3 * s + 1) * KT:(3 * s + 2) * KT]
                gate = ada[:, (3 * s + 2) * KT:(3 * s + 3) * KT]
                nc.vector.tensor_scalar(sg[:, s], scale, 1.0, None, ALU.add).then_inc(fix, 1)
                n += 1
                if s != 1:
                    nc.vector.tensor_scalar(gate, gate, 0.5, None, ALU.mult).then_inc(fix, 1)
                    n += 1
                dve.wait_ge(fix, n)
                nc.vector.tensor_tensor(sg[:, s], sg[:, s],
                                        gains[:, s].unsqueeze(2).to_broadcast([P, KT, NCOND]), ALU.mult).then_inc(fix, 1)
                n += 1
            dve.wait_ge(fix, n)


def norm_mod(nc, name, x, h, ones, ada, sg, s, load=None, store=None):
    with Phase(nc, name) as ph:
        sq = ph.sb("sq", [P, 2, TOK])
        rstd = ph.sb("rstd", [P, TOK])
        smp = ph.sb("smp", [P, KT, NB])
        eps = ph.sb("eps", [P, 1])
        ps = ph.ps("ps", [P, NCH, 512])
        x_in = [ph.sem(f"x_in{k}") for k in range(KT)] if load is not None else None
        squared, summed, root, inv, scaled, modded, smp_mod, eps_set, saved = (
            ph.sem(n) for n in ("squared", "summed", "root", "inv", "scaled", "modded", "smp_mod", "eps_set", "saved"))
        block = ph.block()

        @block.sync
        def _(sp):
            if load is not None:
                for k in range(KT):
                    sp.dma_start(x[:, k], load[:, k]).then_inc(x_in[k], 16)
            if store is not None:
                sp.dma_start(store, x[:]).then_inc(saved, 16)
                sp.wait_ge(saved, 16)

        @block.scalar
        def _(act):
            for k in range(KT):
                if load is not None:
                    act.wait_ge(x_in[k], 16)
                if k >= 2:
                    act.wait_ge(summed, k - 1)
                nc.scalar.activation(sq[:, k % 2], x[:, k], ACT.Square).then_inc(squared, 1)
            act.wait_ge(summed, KT)
            act.wait_ge(eps_set, 1)
            nc.scalar.activation(rstd[:].rearrange("p (n c) -> p n c", n=NCH), ps[:, :, 0:NC], ACT.Sqrt,
                                 scale=1.0 / DM, bias=eps[:]).then_inc(root, 1)
            for k in range(KT):
                act.wait_ge(scaled, k + 1)
                nc.scalar.activation(h[:, k, 0:SEQ], h[:, k, 0:SEQ], ACT.Identity,
                                     scale=sg[:, s, k, 0:1], bias=ada[:, 3 * s * KT + k, 0:1]).then_inc(modded, 1)
            act.wait_ge(modded, KT)

        @block.tensor
        def _(pe):
            for k in range(KT):
                pe.wait_ge(squared, k + 1)
                for n in range(NCH):
                    m = nc.tensor.matmul(ps[:, n, 0:NC], ones[:], sq[:, k % 2, n * NC:(n + 1) * NC],
                                         start=k == 0, stop=k == KT - 1)
                m.then_inc(summed, 1)

        @block.vector
        def _(dve):
            nc.vector.memset(eps[:], EPS).then_inc(eps_set, 1)
            dve.wait_ge(root, 1)
            nc.vector.reciprocal(rstd[:], rstd[:]).then_inc(inv, 1)
            dve.wait_ge(inv, 1)
            for k in range(KT):
                nc.vector.tensor_tensor(h[:, k], x[:, k], rstd[:], ALU.mult).then_inc(scaled, 1)
            dve.wait_ge(scaled, KT)
            nc.vector.tensor_tensor(smp[:], h[:, :, SEQ:TOK], sg[:, s, :, 1:NCOND], ALU.mult).then_inc(smp_mod, 1)
            dve.wait_ge(smp_mod, 1)
            nc.vector.tensor_tensor(h[:, :, SEQ:TOK], smp[:], ada[:, 3 * s * KT:(3 * s + 1) * KT, 1:NCOND],
                                    ALU.add).then_inc(smp_mod, 1)
            dve.wait_ge(smp_mod, 2)


def ffn(nc, name, w_in_d, w_out_d, x, h, ada, s):
    with Phase(nc, name) as ph:
        a = ph.sb("a", [P, FT, TOK])
        w = ph.sb("w", [P, 2, 2 * KT * P])
        wo = ph.sb("wo", [P, 2, FT // 2, P])
        g = ph.sb("g", [P, NCH, NC])
        smp = ph.sb("smp", [P, 2, NB])
        ps = [ph.ps(f"ps{n}", [P, 2, 512]) for n in range(NCH)]
        w_in = [ph.sem(f"w_in{q}") for q in range(2)]
        wo_in = [ph.sem(f"wo_in{q}") for q in range(2)]
        mm, silued, acted, wo_used, mo, added, smped, smpadd = (
            ph.sem(n) for n in ("mm", "silued", "acted", "wo_used", "mo", "added", "smped", "smpadd"))
        wv = w[:].rearrange("p q (u k m) -> p q u k m", u=2, k=KT)
        block = ph.block()
        HK = FT // 2

        @block.sync
        def _(sp):
            for q in range(2):
                sp.dma_start(w[:, q], w_in_d[q]).then_inc(w_in[q], 16)
            for q in range(2):
                sp.dma_start(wo[:, q], w_out_d[q]).then_inc(wo_in[q], 16)
            with sp.Fori(1, FT // 2) as i:
                for q in range(2):
                    sp.wait_ge(mm, NCH * (2 * (i - 1) + q + 1))
                    sp.dma_start(w[:, q], w_in_d[2 * i + q]).then_inc(w_in[q], 16)
            with sp.Fori(1, KT) as i:
                for q in range(2):
                    sp.wait_ge(wo_used, 2 * (i - 1) + q + 1)
                    sp.dma_start(wo[:, q], w_out_d[2 * i + q]).then_inc(wo_in[q], 16)

        @block.tensor
        def _(pe):
            with pe.Fori(0, FT // 2) as i:
                for q in range(2):
                    pe.wait_ge(w_in[q], 16 * (i + 1))
                    for n in range(NCH):
                        pe.wait_ge(acted, 2 * NCH * i + (n + 1 if q else 0))
                        for u in range(2):
                            for k in range(KT):
                                m = nc.tensor.matmul(ps[n][:, u, 0:NC], wv[:, q, u, k], h[:, k, n * NC:(n + 1) * NC],
                                                     start=k == 0, stop=k == KT - 1)
                        m.then_inc(mm, 1)
            pe.wait_ge(acted, FT * NCH)
            with pe.Fori(0, KT // 2) as i:
                for q in range(2):
                    pe.wait_ge(added, 2 * i)
                    for hf in range(2):
                        pe.wait_ge(wo_in[hf], 32 * i + 16 * (q + 1))
                        for n in range(NCH):
                            for k in range(HK):
                                m = nc.tensor.matmul(ps[n][:, q, 0:NC], wo[:, hf, k], a[:, hf * HK + k, n * NC:(n + 1) * NC],
                                                     start=hf == 0 and k == 0, stop=hf == 1 and k == HK - 1)
                        m.then_inc(wo_used, 1)

        @block.scalar
        def _(act):
            with act.Fori(0, FT) as i:
                for n in range(NCH):
                    act.wait_ge(mm, NCH * i + n + 1)
                    act.wait_ge(acted, NCH * i)
                    nc.scalar.activation(g[:, n], ps[n][:, 0, 0:NC], ACT.Silu).then_inc(silued, 1)

        @block.vector
        def _(dve):
            with dve.Fori(0, FT) as i:
                for n in range(NCH):
                    dve.wait_ge(silued, NCH * i + n + 1)
                    nc.vector.tensor_tensor(a[:, i, n * NC:(n + 1) * NC], g[:, n], ps[n][:, 1, 0:NC],
                                            ALU.mult).then_inc(acted, 1)
            gate = (3 * s + 2) * KT
            with dve.Fori(0, KT // 2) as i:
                for q in range(2):
                    t = 2 * i + q
                    dve.wait_ge(wo_used, 4 * i + 2 * q + 2)
                    nc.vector.tensor_tensor(smp[:, q], ps[2][:, q, LASTP:NC], ada[:, gate + t, 1:NCOND],
                                            ALU.mult).then_inc(smped, 1)
                    for n in range(NCH):
                        c = NC if n < NCH - 1 else LASTP
                        v = nc.vector.scalar_tensor_tensor(
                            out=x[:, t, n * NC:n * NC + c], in0=ps[n][:, q, 0:c], scalar=ada[:, bass.ds(gate + t, 1), 0:1].rearrange("p a b -> p (a b)"),
                            in1=x[:, t, n * NC:n * NC + c], op0=ALU.mult, op1=ALU.add)
                    dve.wait_ge(smped, 2 * i + q + 1)
                    nc.vector.tensor_tensor(x[:, t, SEQ:TOK], x[:, t, SEQ:TOK], smp[:, q], ALU.add).then_inc(added, 1)
            dve.wait_ge(added, KT)


def load_tiles(eng, slots, w_in, used, per, src, n):
    for q in range(2):
        eng.dma_start(slots[:, q], src[q]).then_inc(w_in[q], 16)
    with eng.Fori(1, n // 2) as i:
        for q in range(2):
            eng.wait_ge(used, per * (2 * (i - 1) + q + 1))
            eng.dma_start(slots[:, q], src[2 * i + q]).then_inc(w_in[q], 16)
    if n % 2:
        eng.wait_ge(used, per * (n - 2))
        eng.dma_start(slots[:, 0], src[n - 1]).then_inc(w_in[0], 16)


def project_tiles(pe, nc, slots, ps, rhs, w_in, mm, read, n, kt=KT):
    def tile(i, q):
        pe.wait_ge(w_in[q], 16 * (i + 1))
        for c in range(NCH):
            if c == 0:
                pe.wait_ge(read[q], NCH * i)
            for k in range(kt):
                m = nc.tensor.matmul(ps[q][:, c, 0:NC], slots[:, q, k], rhs[:, k, c * NC:(c + 1) * NC],
                                     start=k == 0, stop=k == kt - 1)
            m.then_inc(mm, 1)

    with pe.Fori(0, n // 2) as i:
        for q in range(2):
            tile(i, q)
    if n % 2:
        tile(n // 2, 0)


def copy_tiles(act, nc, dst, ps, mm, read, n, before=0, func=ACT.Copy):
    def tile(i, q):
        for c in range(NCH):
            act.wait_ge(mm, NCH * (2 * i + q + before) + c + 1)
            nc.scalar.activation(dst[:, 2 * i + q, c * NC:(c + 1) * NC], ps[q][:, c, 0:NC], func).then_inc(read[q], 1)

    with act.Fori(0, n // 2) as i:
        for q in range(2):
            tile(i, q)
    if n % 2:
        tile(n // 2, 0)


def project_attention(nc, d, o, h, pj, tok):
    with Phase(nc, "pja") as ph:
        w = ph.sb("w", [P, 2, KT, P])
        wt = ph.sb("wt", [P, KT, VW])
        ps = [ph.ps(f"ps{q}", [P, NCH, 512]) for q in range(2)]
        pt = ph.ps("pt", [P, 2, 512])
        w_in = [ph.sem(f"w_in{q}") for q in range(2)]
        read = [ph.sem(f"read{q}") for q in range(2)]
        mm, wt_in, tmm, tread, saved = (ph.sem(n) for n in ("mm", "wt_in", "tmm", "tread", "saved"))
        block = ph.block()

        @block.sync
        def _(sp):
            sp.dma_start(wt[:], d["w_tok"]).then_inc(wt_in, 16)
            load_tiles(sp, w, w_in, mm, NCH, d["w_att"], AT)
            sp.wait_ge(read[0], NCH * (AT - AT // 2))
            sp.wait_ge(read[1], NCH * (AT // 2))
            sp.wait_ge(tread, TB + 1)
            sp.dma_start(o["k"], pj[:, KT0:KT0 + 2]).then_inc(saved, 16)
            sp.dma_start(o["kidx"], pj[0:ID, KI0]).then_inc(saved, 16)
            sp.dma_start(o["v_p"], tok[:, 0:TB, 0:NKV * HD]).then_inc(saved, 16)
            sp.dma_start(o["v_s"], tok[0:NB, TB, 0:NKV * HD]).then_inc(saved, 16)
            sp.wait_ge(saved, 64)

        @block.tensor
        def _(pe):
            project_tiles(pe, nc, w, ps, h, w_in, mm, read, AT)
            pe.wait_ge(wt_in, 16)
            for t in range(TB + 1):
                rows = P if t < TB else NB
                if t >= 2:
                    pe.wait_ge(tread, t - 1)
                for k in range(KT):
                    m = nc.tensor.matmul(pt[0:rows, t % 2, 0:VW], h[:, k, t * P:t * P + rows], wt[:, k],
                                         start=k == 0, stop=k == KT - 1)
                m.then_inc(tmm, 1)

        @block.scalar
        def _(act):
            copy_tiles(act, nc, pj, ps, mm, read, AT)

        @block.vector
        def _(dve):
            for t in range(TB + 1):
                rows = P if t < TB else NB
                dve.wait_ge(tmm, t + 1)
                nc.vector.tensor_copy(tok[0:rows, t], pt[0:rows, t % 2, 0:VW]).then_inc(tread, 1)


def mask_at(b):
    return P * (b * (b + 1) // 2)


def select_keys(nc, pj, tok, mask):
    with Phase(nc, "sel") as ph:
        r = ph.sb("r", [P, 2, SEQ])
        sc = ph.sb("sc", [P, 2, SEQ])
        wis = ph.sb("wis", [P, TB, NIH])
        m8 = ph.sb("m8", [P, 8])
        ps = ph.ps("ps", [P, 2, SEQ])
        mm, relu, acc, zeroed, causal, scored, masked, topk, free, tick = (
            ph.sem(n) for n in ("mm", "relu", "acc", "zeroed", "causal", "scored", "masked", "topk", "free", "tick"))
        block = ph.block()
        first = TOPK // P
        blocks = range(first, TB)

        @block.tensor
        def _(pe):
            n = 0
            for b in blocks:
                for hd in range(NIH):
                    lo = 64 * (hd % 2)
                    if n >= 2:
                        pe.wait_ge(relu, n - 1)
                    for c in range(0, (b + 1) * P, 512):
                        e = min(c + 512, (b + 1) * P)
                        m = nc.tensor.matmul(ps[:, n % 2, c:e], pj[lo:lo + ID, QI0 + hd // 2, b * P:(b + 1) * P],
                                             pj[lo:lo + ID, KI0, c:e], start=True, stop=True)
                    m.then_inc(mm, 1)
                    n += 1

        @block.scalar
        def _(act):
            n = 0
            for b in blocks:
                for hd in range(NIH):
                    act.wait_ge(mm, n + 1)
                    if n >= 2:
                        act.wait_ge(acc, n - 1)
                    nc.scalar.activation(r[:, n % 2, 0:(b + 1) * P], ps[:, n % 2, 0:(b + 1) * P], ACT.Relu).then_inc(relu, 1)
                    n += 1

        @block.gpsimd
        def _(pool):
            nc.gpsimd.memset(mask[:, 0:mask_at(first)], 0.0).then_inc(zeroed, 1)
            pool.wait_ge(zeroed, 1)
            for b in range(first):
                part = mask[:, mask_at(b) + b * P:mask_at(b + 1)]
                nc.gpsimd.affine_select(out=part, in_=part, compare_op=ALU.is_ge, fill=-BIG, base=0,
                                        pattern=[[-1, P]], channel_multiplier=1).then_inc(masked, 1)
            for i, b in enumerate(blocks):
                pool.wait_ge(scored, i + 1)
                part = sc[:, i % 2, b * P:(b + 1) * P]
                nc.gpsimd.affine_select(out=part, in_=part, compare_op=ALU.is_ge, fill=CAUSAL, base=0,
                                        pattern=[[-1, P]], channel_multiplier=1).then_inc(causal, 1)

        @block.vector
        def _(dve):
            nc.vector.tensor_scalar(wis[:], tok[:, 0:TB, NKV * HD:NKV * HD + NIH], float((NIH * ID) ** -0.5), None,
                                    ALU.mult).then_inc(free, 1)
            dve.wait_ge(free, 1)
            n = 0
            ch = Chain(dve, topk, tick)

            def score(i, b):
                nonlocal n
                for hd in range(NIH):
                    s = sc[:, i % 2, 0:(b + 1) * P]
                    dve.wait_ge(relu, n + 1)
                    if hd == 0:
                        v = nc.vector.tensor_scalar(s, r[:, n % 2, 0:(b + 1) * P], wis[:, b, 0:1], None, ALU.mult)
                    else:
                        dve.wait_ge(acc, n)
                        v = nc.vector.scalar_tensor_tensor(out=s, in0=r[:, n % 2, 0:(b + 1) * P], scalar=wis[:, b, hd:hd + 1],
                                                           in1=s, op0=ALU.mult, op1=ALU.add)
                    v.then_inc(acc, 1)
                    n += 1
                dve.wait_ge(acc, n)
                dve.sem_inc(scored, 1)

            score(0, first)
            for i, b in enumerate(blocks):
                if b + 1 < TB:
                    score(i + 1, b + 1)
                dve.wait_ge(causal, i + 1)
                s = sc[:, i % 2, 0:(b + 1) * P]
                ROUNDS, U = TOPK // 8, 4
                with dve.Fori(0, ROUNDS // U) as j:
                    ch.loop(j, 2 * U)
                    for _ in range(U):
                        ch.link(nc.vector.max(m8[:], s))
                        ch.link(nc.vector.match_replace(s, m8[:], s, TAKEN))
                ch.done(ROUNDS // U)
                ch.link(nc.vector.tensor_scalar(mask[:, mask_at(b):mask_at(b + 1)], s, -3.2e38, -BIG, ALU.is_gt, ALU.mult))


def attend(nc, pj, tok, mask, bias, ident, att):
    with Phase(nc, "att") as ph:
        q = ph.sb("q", [P, P])
        L = ph.sb("L", [P, 2, SEQ])
        ET = ph.sb("ET", [P, 2, SEQ])
        nm = ph.sb("nm", [P, 2])
        den = ph.sb("den", [P, 2])
        rd = ph.sb("rd", [P, 2])
        pair = ph.sb("pair", [P, P])
        pS = ph.ps("pS", [P, 2, SEQ])
        pT = ph.ps("pT", [P, SEQ])
        pO = ph.ps("pO", [P, 2, 512])
        staged, mm, logit, rmax, exped, trans, copied, pv, scaled, recip, turned, done, dchain = (
            ph.sem(n) for n in ("staged", "mm", "logit", "rmax", "exped", "trans", "copied", "pv", "scaled", "recip",
                                "turned", "done", "dchain"))
        block = ph.block()
        PAIRS = NH // 2
        G = NH // NKV

        def loops(eng, body):
            for b in range(TB):
                for m in range(2):
                    with eng.Fori(0, G) as g:
                        body(b * PAIRS + m * G + g, b, m, m * G + g)

        @block.gpsimd
        def _(pool):
            def body(t, b, m, j):
                pool.wait_ge(mm, 2 * t)
                nc.gpsimd.tensor_copy(q[:], pj[:, QT0 + j, b * P:(b + 1) * P]).then_inc(staged, 1)
            loops(pool, body)

        @block.tensor
        def _(pe):
            def body(t, b, m, j):
                W = (b + 1) * P
                pe.wait_ge(staged, t + 1)
                pe.wait_ge(rmax, 2 * t)
                for u in range(2):
                    for c in range(0, W, 512):
                        e = min(c + 512, W)
                        x = nc.tensor.matmul(pS[:, u, c:e], q[64 * u:64 * u + 64, :],
                                             pj[64 * u:64 * u + 64, KT0 + m, c:e], start=True, stop=True)
                    x.then_inc(mm, 1)
                for u in range(2):
                    pe.wait_ge(exped, 2 * t + u + 1)
                    pe.wait_ge(copied, 2 * t + u)
                    for c in range(b + 1):
                        x = nc.tensor.transpose(pT[:, c * P:(c + 1) * P], L[:, u, c * P:(c + 1) * P], ident[:])
                    x.then_inc(trans, 1)
                    pe.wait_ge(copied, 2 * t + u + 1)
                    if u == 0:
                        pe.wait_ge(done, t)
                    for c in range(b + 1):
                        x = nc.tensor.matmul(pO[:, 0, u * HD:(u + 1) * HD], ET[:, u, c * P:(c + 1) * P],
                                             tok[:, c, (2 * m + u) * HD:(2 * m + u + 1) * HD], start=c == 0, stop=c == b)
                    x.then_inc(pv, 1)
                pe.wait_ge(scaled, t + 1)
                nc.tensor.transpose(pO[:, 1, 0:P], pair[:], ident[:]).then_inc(turned, 1)
            loops(pe, body)

        @block.scalar
        def _(act):
            def body(t, b, m, j):
                W = (b + 1) * P
                for u in range(2):
                    act.wait_ge(rmax, 2 * t + u + 1)
                    nc.scalar.activation(L[:, u, 0:W], L[:, u, 0:W], ACT.Exp, bias=nm[:, u:u + 1],
                                         accum_out=den[:, u:u + 1]).then_inc(exped, 1)
                for u in range(2):
                    act.wait_ge(trans, 2 * t + u + 1)
                    nc.scalar.activation(ET[:, u, 0:W], pT[:, 0:W], ACT.Copy).then_inc(copied, 1)
                act.wait_ge(turned, t + 1)
                nc.scalar.activation(att[:, j, b * P:(b + 1) * P], pO[:, 1, 0:P], ACT.Copy).then_inc(done, 1)
            loops(act, body)

        @block.vector
        def _(dve):
            def body(t, b, m, j):
                W = (b + 1) * P
                lo = max(W - WIN, 0)
                for u in range(2):
                    dve.wait_ge(mm, 2 * t + u + 1)
                    dve.wait_ge(trans, 2 * t)
                    nc.vector.scalar_tensor_tensor(out=L[:, u, 0:W], in0=pS[:, u, 0:W], scalar=float(HD ** -0.5),
                                                   in1=mask[:, mask_at(b):mask_at(b + 1)], op0=ALU.mult,
                                                   op1=ALU.add).then_inc(logit, 1)
                    dve.wait_ge(logit, 4 * t + 2 * u + 1)
                    nc.vector.tensor_tensor(L[:, u, lo:W], L[:, u, lo:W], bias[:, 2 * j + u, WIN - (W - lo):WIN],
                                            ALU.add).then_inc(logit, 1)
                    dve.wait_ge(logit, 4 * t + 2 * u + 2)
                    nc.vector.tensor_reduce(nm[:, u:u + 1], L[:, u, 0:W], AX, ALU.max, negate=True).then_inc(rmax, 1)
                dve.wait_ge(exped, 2 * t + 2)
                nc.vector.reciprocal(rd[:], den[:]).then_inc(recip, 1)
                dve.wait_ge(recip, t + 1)
                dve.wait_ge(pv, 2 * t + 2)
                nc.vector.tensor_tensor(pair[:].rearrange("p (u d) -> p u d", u=2),
                                        pO[:, 0, 0:2 * HD].rearrange("p (u d) -> p u d", u=2),
                                        rd[:].unsqueeze(2).to_broadcast([P, 2, HD]), ALU.mult).then_inc(scaled, 1)
            loops(dve, body)


def tables(nc, d, s, ident, bias):
    with Phase(nc, "tab") as ph:
        hot = ph.sb("hot", [NBUCKET, 512])
        rb = ph.sb("rb", [NBUCKET, NH])
        byh = ph.sb("byh", [NH, 512])
        rows = ph.sb("rows", [P, 2, NH])
        flip = ph.sb("flip", [P, P])
        up = ph.sb("up", [P, NH, WIN])
        pf = ph.ps("pf", [P, 4, 2 * WIN])
        ps = ph.ps("ps", [P, 512])
        pr = ph.ps("pr", [P, 2, NH])
        flipped, loaded, mm, moved, sub, stored, back = (
            ph.sem(n) for n in ("flipped", "loaded", "mm", "moved", "sub", "stored", "back"))
        block = ph.block()

        @block.sync
        def _(sp):
            sp.dma_start(ident[:], d["ident"]).then_inc(loaded, 16)
            sp.dma_start(hot[:], d["hot"]).then_inc(loaded, 16)
            sp.dma_start(rb[:], d["rel_bias"]).then_inc(loaded, 16)
            sp.dma_start(flip[:], d["flip"]).then_inc(loaded, 16)
            sp.wait_ge(sub, 1)
            sp.dma_start(s["byh"], byh[:]).then_inc(stored, 16)
            sp.wait_ge(moved, 2)
            sp.dma_start(s["brow"].rearrange("(c p) h -> p c h", c=2), rows[:]).then_inc(stored, 16)
            sp.wait_ge(stored, 32)
            win = bass.AP(s["byh"].tensor, 0, [[1, P], [512, NH], [1, WIN]])
            sp.dma_start(up[:], win).then_inc(back, 16)
            sp.wait_ge(back, 16)

        @block.tensor
        def _(pe):
            pe.wait_ge(loaded, 64)
            nc.tensor.matmul(ps[0:NH, :], rb[:], hot[:], start=True, stop=True).then_inc(mm, 1)
            for c in range(2):
                nc.tensor.matmul(pr[:, c], hot[:, c * P:(c + 1) * P], rb[:], start=True, stop=True).then_inc(mm, 1)
            pe.wait_ge(back, 16)
            for n in range(NH // 2):
                if n >= 4:
                    pe.wait_ge(flipped, n - 3)
                nc.tensor.matmul(pf[:, n % 4], flip[:], up[:, 2 * n:2 * n + 2].rearrange("p h j -> p (h j)"),
                                 start=True, stop=True).then_inc(mm, 1)

        @block.vector
        def _(dve):
            dve.wait_ge(mm, 3)
            nc.vector.tensor_copy(byh[:], ps[0:NH, :]).then_inc(moved, 1)
            nc.vector.tensor_copy(rows[:], pr[:]).then_inc(moved, 1)
            dve.wait_ge(moved, 2)
            nc.vector.tensor_scalar(byh[:], byh[:], ps[0:NH, 0:1], None, ALU.subtract).then_inc(sub, 1)
            for n in range(NH // 2):
                dve.wait_ge(mm, 4 + n)
                nc.vector.tensor_copy(bias[:, 2 * n:2 * n + 2].rearrange("p h j -> p (h j)"), pf[:, n % 4]).then_inc(flipped, 1)


def attention_out(nc, d, h, att, A):
    with Phase(nc, "ao") as ph:
        w = ph.sb("w", [P, 2, KT, P])
        g = ph.sb("g", [P, NCH, NC])
        ps = [ph.ps(f"ps{q}", [P, NCH, 512]) for q in range(2)]
        w_in = [ph.sem(f"w_in{q}") for q in range(2)]
        mm, gated, merged = (ph.sem(n) for n in ("mm", "gated", "merged"))
        block = ph.block()

        @block.sync
        def _(sp):
            load_tiles(sp, w, w_in, mm, NCH, d["w_ao"], 2 * KT)

        @block.tensor
        def _(pe):
            with pe.Fori(0, KT) as i:
                for q, rhs in enumerate((h, att)):
                    pe.wait_ge(w_in[q], 16 * (i + 1))
                    pe.wait_ge((gated, merged)[q], NCH * i)
                    for c in range(NCH):
                        for k in range(KT):
                            m = nc.tensor.matmul(ps[q][:, c, 0:NC], w[:, q, k], rhs[:, k, c * NC:(c + 1) * NC],
                                                 start=k == 0, stop=k == KT - 1)
                        m.then_inc(mm, 1)

        @block.scalar
        def _(act):
            with act.Fori(0, KT) as i:
                act.wait_ge(merged, NCH * i)
                for c in range(NCH):
                    act.wait_ge(mm, 2 * NCH * i + c + 1)
                    nc.scalar.activation(g[:, c], ps[0][:, c, 0:NC], ACT.Sigmoid).then_inc(gated, 1)

        @block.vector
        def _(dve):
            with dve.Fori(0, KT) as i:
                for c in range(NCH):
                    dve.wait_ge(gated, NCH * i + c + 1)
                    dve.wait_ge(mm, 2 * NCH * i + NCH + c + 1)
                    nc.vector.tensor_tensor(A[:, i, c * NC:(c + 1) * NC], g[:, c], ps[1][:, c, 0:NC], ALU.mult).then_inc(merged, 1)


def ssd_gate(nc, d, h, A, S):
    with Phase(nc, "sg") as ph:
        w = ph.sb("w", [P, 2, KT, P])
        g = ph.sb("g", [P, 2, NCH, NC])
        ps = [ph.ps(f"ps{q}", [P, NCH, 512]) for q in range(2)]
        w_in = [ph.sem(f"w_in{q}") for q in range(2)]
        read = [ph.sem(f"read{q}") for q in range(2)]
        mm, mult, added = (ph.sem(n) for n in ("mm", "mult", "added"))
        block = ph.block()

        @block.sync
        def _(sp):
            load_tiles(sp, w, w_in, mm, NCH, d["w_gs"], KT)

        @block.tensor
        def _(pe):
            project_tiles(pe, nc, w, ps, h, w_in, mm, read, KT)

        @block.scalar
        def _(act):
            with act.Fori(0, KT // 2) as i:
                act.wait_ge(added, 2 * i)
                for q in range(2):
                    for c in range(NCH):
                        act.wait_ge(mm, NCH * (2 * i + q) + c + 1)
                        nc.scalar.activation(g[:, q, c], ps[q][:, c, 0:NC], ACT.Sigmoid).then_inc(read[q], 1)

        @block.vector
        def _(dve):
            with dve.Fori(0, KT // 2) as i:
                for q in range(2):
                    dve.wait_ge(read[q], NCH * (i + 1))
                    t = 2 * i + q
                    gv = g[:, q].rearrange("p c n -> p (c n)")
                    nc.vector.tensor_tensor(S[:, t], S[:, t], gv, ALU.mult).then_inc(mult, 1)
                    dve.wait_ge(mult, t + 1)
                    nc.vector.tensor_tensor(A[:, t], A[:, t], S[:, t], ALU.add).then_inc(added, 1)
            dve.wait_ge(added, KT)


def mix_out(nc, d, x_d, x, A, ada):
    with Phase(nc, "mo") as ph:
        w = ph.sb("w", [P, 2, KT, P])
        smp = ph.sb("smp", [P, 2, NB])
        ps = [ph.ps(f"ps{q}", [P, NCH, 512]) for q in range(2)]
        w_in = [ph.sem(f"w_in{q}") for q in range(2)]
        read = [ph.sem(f"read{q}") for q in range(2)]
        mm, x_in, smped = (ph.sem(n) for n in ("mm", "x_in", "smped"))
        block = ph.block()
        gate = 5 * KT

        @block.sync
        def _(sp):
            load_tiles(sp, w, w_in, mm, NCH, d["w_out"], KT)

        @block.scalar
        def _(act):
            act.dma_start(x[:], x_d).then_inc(x_in, 16)

        @block.tensor
        def _(pe):
            project_tiles(pe, nc, w, ps, A, w_in, mm, read, KT)

        @block.vector
        def _(dve):
            dve.wait_ge(x_in, 16)
            with dve.Fori(0, KT // 2) as i:
                for q in range(2):
                    t = 2 * i + q
                    dve.wait_ge(mm, NCH * (2 * i + q + 1))
                    nc.vector.tensor_tensor(smp[:, q], ps[q][:, 2, LASTP:NC], ada[:, gate + t, 1:NCOND],
                                            ALU.mult).then_inc(smped, 1)
                    for n in range(NCH):
                        c = NC if n < NCH - 1 else LASTP
                        v = nc.vector.scalar_tensor_tensor(
                            out=x[:, t, n * NC:n * NC + c], in0=ps[q][:, n, 0:c],
                            scalar=ada[:, bass.ds(gate + t, 1), 0:1].rearrange("p a b -> p (a b)"),
                            in1=x[:, t, n * NC:n * NC + c], op0=ALU.mult, op1=ALU.add)
                        if n < NCH - 1:
                            v.then_inc(read[q], 1)
                    dve.wait_ge(smped, 2 * i + q + 1)
                    nc.vector.tensor_tensor(x[:, t, SEQ:TOK], x[:, t, SEQ:TOK], smp[:, q], ALU.add).then_inc(read[q], 1)
            for q in range(2):
                dve.wait_ge(read[q], NCH * KT // 2)


def time_steps(nc, d, tok, dt, dtA, ea, te, etot, upper):
    with Phase(nc, "ts") as ph:
        rows = ph.sb("rows", [P, 2, SH])
        t = {n: ph.sb(n, [P, TB + 1, SH]) for n in ("v", "e", "u", "l", "r")}
        ps = ph.ps("ps", [P, 2, 512])
        r_in, negabs, exped, logged, ch_s, mm, ex, zero = (ph.sem(n) for n in ("r_in", "negabs", "exped", "logged", "ch", "mm", "ex", "zero"))
        ones = ph.sb("ones", [P, P])
        block = ph.block()
        v, e, u, l, r = (t[n] for n in ("v", "e", "u", "l", "r"))
        raw = tok[:, :, NKV * HD + NIH:VW]
        bc = lambda row: rows[:, row].unsqueeze(1).to_broadcast([P, TB, SH])

        @block.sync
        def _(sp):
            sp.dma_start(rows[:, 0], d["dt_bias"]).then_inc(r_in, 16)
            sp.dma_start(rows[:, 1], d["a_log"]).then_inc(r_in, 16)
            sp.dma_start(upper[:], d["upper"]).then_inc(r_in, 16)

        @block.scalar
        def _(act):
            act.wait_ge(r_in, 48)
            nc.scalar.activation(rows[:, 1], rows[:, 1], ACT.Exp).then_inc(exped, 1)
            act.wait_ge(negabs, 1)
            nc.scalar.activation(e[:], e[:], ACT.Exp).then_inc(exped, 1)
            act.wait_ge(negabs, 2)
            nc.scalar.activation(l[:], u[:], ACT.Ln).then_inc(logged, 1)
            act.wait_ge(ex, 1)
            f = lambda a: a[:].rearrange("p c h -> p (c h)")
            nc.scalar.activation(f(ea), ps[:, 0, 0:TB * SH], ACT.Exp).then_inc(exped, 1)
            nc.scalar.activation(f(etot), ps[:, 1, 0:TB * SH], ACT.Exp).then_inc(exped, 1)
            nc.scalar.activation(te[:], te[:], ACT.Exp).then_inc(exped, 1)
            act.wait_ge(exped, 5)

        @block.tensor
        def _(pe):
            pe.wait_ge(mm, 1)
            f = dtA[:, 0:TB].rearrange("p c h -> p (c h)")
            nc.tensor.matmul(ps[:, 0, 0:TB * SH], upper[:], f, start=True, stop=True)
            nc.tensor.matmul(ps[:, 1, 0:TB * SH], ones[:], f, start=True, stop=True).then_inc(mm, 1)

        @block.gpsimd
        def _(pool):
            nc.gpsimd.memset(ones[:], 1.0).then_inc(zero, 1)

        @block.vector
        def _(dve):
            ch = Chain(dve, ch_s)
            dve.wait_ge(r_in, 48)
            ch.link(nc.vector.memset(v[:, TB], 0.0))
            ch.link(nc.vector.tensor_tensor(v[:, 0:TB], raw[:, 0:TB], bc(0), ALU.add))
            ch.link(nc.vector.tensor_tensor(v[0:NB, TB], raw[0:NB, TB], rows[0:NB, 0], ALU.add))
            nc.vector.scalar_tensor_tensor(out=e[:], in0=v[:], scalar=-1.0, in1=v[:], op0=ALU.mult, op1=ALU.min).then_inc(negabs, 1)
            dve.wait_ge(exped, 2)
            ch.link(nc.vector.tensor_scalar(u[:], e[:], 1.0, None, ALU.add))
            dve.sem_inc(negabs, 1)
            ch.link(nc.vector.tensor_scalar(r[:], u[:], -1.0, None, ALU.add))
            dve.wait_ge(logged, 1)
            ch.link(nc.vector.tensor_scalar(u[:], r[:], 0.0, None, ALU.is_equal))
            ch.link(nc.vector.tensor_tensor(r[:], r[:], u[:], ALU.add))
            ch.link(nc.vector.reciprocal(r[:], r[:]))
            ch.link(nc.vector.tensor_tensor(l[:], l[:], r[:], ALU.mult))
            ch.link(nc.vector.tensor_tensor(l[:], l[:], u[:], ALU.add))
            ch.link(nc.vector.tensor_tensor(l[:], l[:], e[:], ALU.mult))
            ch.link(nc.vector.scalar_tensor_tensor(out=dt[:], in0=v[:], scalar=0.0, in1=l[:], op0=ALU.max, op1=ALU.add))
            ch.link(nc.vector.scalar_tensor_tensor(out=dtA[:, 0:TB], in0=dt[:, 0:TB], scalar=-1.0, in1=bc(1),
                                                   op0=ALU.mult, op1=ALU.mult))
            ch.link(nc.vector.scalar_tensor_tensor(out=dtA[:, TB], in0=dt[:, TB], scalar=-1.0, in1=rows[:, 1],
                                                   op0=ALU.mult, op1=ALU.mult))
            dve.wait_ge(zero, 1)
            dve.sem_inc(mm, 1)
            dve.wait_ge(mm, 2)
            f = lambda a: a[:].rearrange("p c h -> p (c h)")
            ch.link(nc.vector.tensor_copy(f(te), ps[:, 1, 0:TB * SH]))
            ch.link(nc.vector.tensor_tensor(f(te), f(te), ps[:, 0, 0:TB * SH], ALU.subtract))
            dve.sem_inc(ex, 1)


def ssd_project(nc, arena, banks, start, d, o, g, h, xb, xc, zs, cw, cb):
    with Phase(nc, "sp", arena, start, banks=banks) as ph:
        w = ph.sb("w", [P, 2, KT, P])
        cv = ph.sb("cv", [P, 2, SEQ])
        st = ph.sb("st", [P, XT, CW - 1, NB])
        sm = ph.sb("sm", [P, 2, XT, NB])
        ps = [ph.ps(f"ps{q}", [P, NCH, 512]) for q in range(2)]
        w_in = [ph.sem(f"w_in{q}") for q in range(2)]
        read = [ph.sem(f"read{q}") for q in range(2)]
        mm, st_in, pad, tap, conv, act_done, smp, saved = (
            ph.sem(n) for n in ("mm", "st_in", "pad", "tap", "conv", "act_done", "smp", "saved"))
        block = ph.block()
        PAD = CW - 1

        @block.sync
        def _(sp):
            load_tiles(sp, w, w_in, mm, NCH, d["w_ssd"][g], XT + 4)
            for q in range(2):
                sp.wait_ge(read[q], NCH * XT // 2)
            sp.dma_start(o["conv_p"][g], xb[:, :, SEQ:SEQ + PAD]).then_inc(saved, 16)
            sp.dma_start(o["conv_s"][g], xb[:, :, PAD + SEQ:PAD + TOK]).then_inc(saved, 16)
            sp.wait_ge(saved, 32)

        @block.gpsimd
        def _(pool):
            nc.gpsimd.memset(xb[:, :, 0:PAD], 0.0).then_inc(pad, 1)

        @block.tensor
        def _(pe):
            project_tiles(pe, nc, w, ps, h, w_in, mm, read, XT + 4)

        @block.scalar
        def _(act):
            act.dma_start(st[:], d["state_conv"][g]).then_inc(st_in, 16)
            copy_tiles(act, nc, xb[:, :, PAD:PAD + TOK], ps, mm, read, XT)
            copy_tiles(act, nc, zs, ps, mm, read, 4, before=XT, func=ACT.Silu)
            with act.Fori(0, XT // 2) as i:
                for q in range(2):
                    t = 2 * i + q
                    act.wait_ge(conv, t + 1)
                    nc.scalar.activation(xc[:, t, 0:SEQ], cv[:, q], ACT.Silu,
                                         bias=cb[:, bass.ds(g * XT + t, 1)]).then_inc(act_done, 1)
            act.wait_ge(smp, 2 * CW)
            nc.scalar.activation(xc[:, :, SEQ:TOK], sm[:, 0], ACT.Silu).then_inc(act_done, 1)
            act.wait_ge(act_done, XT + 1)

        @block.vector
        def _(dve):
            dve.wait_ge(pad, 1)
            with dve.Fori(0, XT // 2) as i:
                for q in range(2):
                    t = 2 * i + q
                    dve.wait_ge(read[q], NCH * (i + 1))
                    dve.wait_ge(act_done, 2 * i)
                    for k in range(CW):
                        src, wk = xb[:, t, k:k + SEQ], cw[:, bass.ds(g * XT + t, 1), k:k + 1].rearrange("p a b -> p (a b)")
                        if k == 0:
                            v = nc.vector.tensor_scalar(cv[:, q], src, wk, None, ALU.mult)
                        else:
                            v = nc.vector.scalar_tensor_tensor(out=cv[:, q], in0=src, scalar=wk, in1=cv[:, q],
                                                               op0=ALU.mult, op1=ALU.add)
                        if k < CW - 1:
                            v.then_inc(tap, 1)
                            dve.wait_ge(tap, (CW - 1) * t + k + 1)
                        else:
                            v.then_inc(conv, 1)
            dve.wait_ge(st_in, 16)
            n = 0
            for k in range(CW):
                src = st[:, :, k] if k < CW - 1 else xb[:, :, PAD + SEQ:PAD + TOK]
                wk = cw[:, bass.ds(g * XT, XT), k:k + 1].to_broadcast([P, XT, NB])
                nc.vector.tensor_tensor(sm[:, 0 if k == 0 else 1], src, wk, ALU.mult).then_inc(smp, 1)
                n += 1
                dve.wait_ge(smp, n)
                other = sm[:, 1] if k else cb[:, bass.ds(g * XT, XT)].unsqueeze(2).to_broadcast([P, XT, NB])
                nc.vector.tensor_tensor(sm[:, 0], sm[:, 0], other, ALU.add).then_inc(smp, 1)
                n += 1
                dve.wait_ge(smp, n)


def ssd_scan(nc, arena, banks, d, o, g, xc, y, dt, dtA, ea, te, etot, upper, below, ident, hT):
    R, PD = SH // SG, DI // SH
    GW = R * PD
    with Phase(nc, "sc", arena, banks=banks) as ph:
        st = ph.sb("st", [P, XT, P])
        lower = ph.sb("lower", [P, R, P])
        xdt = ph.sb("xdt", [P, GW])
        xw = ph.sb("xw", [P, GW])
        bt = ph.sb("bt", [P, P])
        cbm = ph.sb("cbm", [P, P])
        E = ph.sb("E", [P, R, P])
        yt = ph.sb("yt", [P, GW])
        pX, pB, pY, pO, pH, pT = (ph.ps(n, [P, 512]) for n in ("pX", "pB", "pY", "pO", "pH", "pT"))
        pS = ph.ps("pS", [P, R, P])
        names = ("staged", "segs", "turned", "seg", "x_dt", "x_w", "b_t", "cb_m", "decay", "M", "ydiag", "yoff", "hup",
                 "y1", "y2", "h0", "h1", "h2", "yturn", "ysaved", "saved")
        (staged, segs, turned, seg, x_dt, x_w, b_t, cb_m, decay, M, ydiag, yoff, hup, y1, y2, h0, h1, h2, yturn, ysaved,
         saved) = (ph.sem(n) for n in names)
        block = ph.block()
        heads = bass.ds(g * R, R)
        wide = lambda a, c: a[:, c, heads].unsqueeze(2).to_broadcast([P, R, PD])
        v3 = lambda a: a.rearrange("p (r d) -> p r d", r=R)

        @block.gpsimd
        def _(pool):
            with pool.Fori(0, TB) as c:
                pool.wait_ge(hup, c)
                pool.wait_ge(yoff, c)
                nc.gpsimd.tensor_copy(st[:], xc[:, :, bass.ds(c * P, P)]).then_inc(staged, 1)
                pool.wait_ge(seg, c)
                nc.gpsimd.tensor_tensor(lower[:], below[:].unsqueeze(1).to_broadcast([P, R, P]),
                                        dtA[:, c, heads].unsqueeze(2).to_broadcast([P, R, P]), ALU.mult).then_inc(segs, 1)
                pool.wait_ge(x_dt, c + 1)
                nc.gpsimd.tensor_tensor(v3(xw[:]), v3(xdt[:]), wide(te, c), ALU.mult).then_inc(x_w, 1)

        @block.tensor
        def _(pe):
            with pe.Fori(0, TB) as c:
                pe.wait_ge(staged, c + 1)
                pe.wait_ge(x_dt, c)
                pe.wait_ge(cb_m, c)
                for t in range(4):
                    nc.tensor.transpose(pX[:, t * P:(t + 1) * P], st[:, t], ident[:])
                nc.tensor.transpose(pB[:, 0:P], st[:, 4], ident[:])
                nc.tensor.matmul(pB[:, P:2 * P], st[:, 4], st[:, 5], start=True, stop=True).then_inc(turned, 1)
                pe.wait_ge(segs, c + 1)
                pe.wait_ge(decay, c)
                for r in range(R):
                    m = nc.tensor.matmul(pS[:, r], lower[:, r], upper[:], start=True, stop=True)
                m.then_inc(seg, 1)
                pe.wait_ge(h2, c + 1)
                pe.wait_ge(y1, c)
                nc.tensor.matmul(pO[:], st[:, 5], hT[:], start=True, stop=True).then_inc(yoff, 1)
                pe.wait_ge(b_t, c + 1)
                pe.wait_ge(x_w, c + 1)
                nc.tensor.matmul(pH[:], bt[:], xw[:], start=True, stop=True).then_inc(hup, 1)
                pe.wait_ge(M, c + 1)
                pe.wait_ge(y2, c)
                for r in range(R):
                    m = nc.tensor.matmul(pY[:, r * PD:(r + 1) * PD], E[:, r], xdt[:, r * PD:(r + 1) * PD], start=True, stop=True)
                m.then_inc(ydiag, 1)
                pe.wait_ge(y2, c + 1)
                pe.wait_ge(ysaved, c)
                for t in range(4):
                    m = nc.tensor.transpose(pT[:, t * P:(t + 1) * P], yt[:, t * P:(t + 1) * P], ident[:])
                m.then_inc(yturn, 1)

        @block.scalar
        def _(act):
            with act.Fori(0, TB) as c:
                act.wait_ge(seg, c + 1)
                act.wait_ge(ydiag, c)
                nc.scalar.activation(E[:].rearrange("p r l -> p (r l)"), pS[:].rearrange("p r l -> p (r l)"), ACT.Exp).then_inc(decay, 1)
                act.wait_ge(yturn, c + 1)
                nc.scalar.activation(y[:, 0:4, bass.ds(c * P, P)], pT[:].rearrange("p (t l) -> p t l", t=4), ACT.Copy).then_inc(ysaved, 1)
            act.wait_ge(ysaved, TB)

        @block.sync
        def _(sp):
            sp.wait_ge(h2, TB + 1)
            sp.dma_start(o["ssm_p"][g], hT[:]).then_inc(saved, 16)
            sp.wait_ge(saved, 16)

        @block.vector
        def _(dve):
            nc.vector.memset(hT[:], 0.0).then_inc(h2, 1)
            with dve.Fori(0, TB) as c:
                dve.wait_ge(turned, c + 1)
                dve.wait_ge(ydiag, c)
                dve.wait_ge(x_w, c)
                nc.vector.tensor_tensor(v3(xdt[:]), v3(pX[:]), wide(dt, c), ALU.mult).then_inc(x_dt, 1)
                dve.wait_ge(hup, c)
                nc.vector.tensor_copy(bt[:], pB[:, 0:P]).then_inc(b_t, 1)
                nc.vector.tensor_tensor(cbm[:], pB[:, P:2 * P], upper[:], ALU.mult).then_inc(cb_m, 1)
                dve.wait_ge(decay, c + 1)
                dve.wait_ge(cb_m, c + 1)
                nc.vector.tensor_tensor(E[:], E[:], cbm[:].unsqueeze(1).to_broadcast([P, R, P]), ALU.mult).then_inc(M, 1)
                dve.wait_ge(yoff, c + 1)
                dve.wait_ge(yturn, c)
                nc.vector.tensor_tensor(v3(yt[:]), v3(pO[:]), wide(ea, c), ALU.mult).then_inc(y1, 1)
                dve.wait_ge(h2, c + 1)
                nc.vector.tensor_tensor(v3(hT[:]), v3(hT[:]), wide(etot, c), ALU.mult).then_inc(h1, 1)
                dve.wait_ge(h1, c + 1)
                dve.wait_ge(hup, c + 1)
                nc.vector.tensor_tensor(hT[:], hT[:], pH[:], ALU.add).then_inc(h2, 1)
                dve.wait_ge(y1, c + 1)
                dve.wait_ge(ydiag, c + 1)
                nc.vector.tensor_tensor(yt[:], yt[:], pY[:], ALU.add).then_inc(y2, 1)


def ssd_sample(nc, arena, banks, d, o, g, xc, y, dt, dtA, ones, ident):
    R, PD = SH // SG, DI // SH
    HP = R // 2
    with Phase(nc, "ss", arena, banks=banks) as ph:
        H = ph.sb("H", [P, HP, NB, DS])
        T = ph.sb("T", [P, NB, DS])
        xs = ph.sb("xs", [NB, XT * P])
        dA = ph.sb("dA", [NB, R])
        dAx = ph.sb("dAx", [NB, R * PD])
        dAf = ph.sb("dAf", [P, HP, NB])
        eye = ph.sb("eye", [NB, 2, NB, DS])
        pX = ph.ps("pX", [NB, 2, 512])
        pA = ph.ps("pA", [P, HP, NB])
        pC = ph.ps("pC", [P, NB, DS])
        pU = ph.ps("pU", [P, NB, DS])
        H_in, turned, moved, exped, dAturn, ch_s, diag, mmc, mmu, upd, red, saved = (
            ph.sem(n) for n in ("H_in", "turned", "moved", "exped", "dAturn", "ch", "diag", "mmc", "mmu", "upd", "red", "saved"))
        block = ph.block()
        heads = bass.ds(g * R, R)
        chunks = lambda a: a.rearrange("p b n -> p (b n)")

        @block.sync
        def _(sp):
            sp.dma_start(H[:].rearrange("p q b n -> p (q b n)"), d["state_ssm"][g]).then_inc(H_in, 16)
            sp.wait_ge(upd, HP)
            sp.dma_start(o["ssm_s"][g], H[:].rearrange("p q b n -> p (q b n)")).then_inc(saved, 16)
            sp.wait_ge(saved, 16)

        @block.scalar
        def _(act):
            nc.scalar.activation(dA[:], dtA[0:NB, TB, heads], ACT.Exp).then_inc(exped, 1)

        @block.tensor
        def _(pe):
            for t in range(XT):
                m = nc.tensor.transpose(pX[:, t // 4, (t % 4) * P:(t % 4 + 1) * P], xc[:, t, SEQ:TOK], ident[:])
            m.then_inc(turned, 1)
            pe.wait_ge(moved, 2)
            for t in range(HP):
                m = nc.tensor.transpose(pA[:, t], dAx[:, t * P:(t + 1) * P], ident[0:NB, 0:NB])
            m.then_inc(dAturn, 1)
            pe.wait_ge(diag, 1)
            for c in range(2):
                m = nc.tensor.matmul(chunks(pC[:])[:, c * 512:(c + 1) * 512], ones[0:NB, :],
                                     chunks(eye[:, 1])[:, c * 512:(c + 1) * 512], start=True, stop=True)
            m.then_inc(mmc, 1)
            for t in range(HP):
                pe.wait_ge(upd, t) if t else None
                for c in range(2):
                    m = nc.tensor.matmul(chunks(pU[:])[:, c * 512:(c + 1) * 512], xs[:, t * P:(t + 1) * P],
                                         chunks(eye[:, 0])[:, c * 512:(c + 1) * 512], start=True, stop=True)
                m.then_inc(mmu, 1)

        @block.vector
        def _(dve):
            ch = Chain(dve, ch_s)
            dve.wait_ge(exped, 1)
            nc.vector.tensor_copy(dAx[:].rearrange("b (r p) -> b r p", r=R), dA[:].unsqueeze(2).to_broadcast([NB, R, PD])).then_inc(moved, 1)
            dve.wait_ge(turned, 1)
            nc.vector.tensor_copy(xs[:], pX[:].rearrange("b a n -> b (a n)")[:, 0:XT * P]).then_inc(moved, 1)
            dve.wait_ge(moved, 2)
            xv = xs[:, 0:R * PD].rearrange("b (r p) -> b r p", r=R)
            ch.link(nc.vector.tensor_tensor(xv, xv, dt[0:NB, TB, heads].unsqueeze(2).to_broadcast([NB, R, PD]), ALU.mult))
            for j in range(2):
                ch.link(nc.vector.tensor_tensor(eye[:, j], xs[:, (4 + j) * P:(5 + j) * P].unsqueeze(1).to_broadcast([NB, NB, DS]),
                                                ident[0:NB, 0:NB].unsqueeze(2).to_broadcast([NB, NB, DS]), ALU.mult))
            dve.sem_inc(diag, 1)
            dve.wait_ge(dAturn, 1)
            ch.link(nc.vector.tensor_copy(dAf[:], pA[:]))
            dve.wait_ge(H_in, 16)
            dve.wait_ge(mmc, 1)
            for t in range(HP):
                ch.link(nc.vector.tensor_tensor(H[:, t], H[:, t], dAf[:, t].unsqueeze(2).to_broadcast([P, NB, DS]), ALU.mult))
                dve.wait_ge(mmu, t + 1)
                nc.vector.tensor_tensor(H[:, t], H[:, t], pU[:], ALU.add).then_inc(upd, 1)
                dve.wait_ge(upd, t + 1)
                ch.link(nc.vector.tensor_tensor(T[:], H[:, t], pC[:], ALU.mult))
                ch.link(nc.vector.tensor_reduce(y[:, t, SEQ:TOK], T[:], AX, ALU.add))


def ssd_out(nc, arena, banks, d, g, xc, zs, y, ones, dskip, nssd, S):
    GT = 4
    with Phase(nc, "so", arena, banks=banks) as ph:
        w = ph.sb("w", [P, 2, GT, P])
        sq = ph.sb("sq", [P, 2, TOK])
        rstd = ph.sb("rstd", [P, TOK])
        eps = ph.sb("eps", [P, 1])
        ps = [ph.ps(f"ps{q}", [P, NCH, 512]) for q in range(2)]
        w_in = [ph.sem(f"w_in{q}") for q in range(2)]
        read = [ph.sem(f"read{q}") for q in range(2)]
        eps_set, skip, gated, squared, summed, root, inv, normed, scaled, mm = (
            ph.sem(n) for n in ("eps_set", "skip", "gated", "squared", "summed", "root", "inv", "normed", "scaled", "mm"))
        block = ph.block()

        @block.sync
        def _(sp):
            load_tiles(sp, w, w_in, mm, NCH, d["w_so"][g], KT)

        @block.scalar
        def _(act):
            for t in range(GT):
                act.wait_ge(gated, t + 1)
                if t >= 2:
                    act.wait_ge(summed, t - 1)
                nc.scalar.activation(sq[:, t % 2], y[:, t], ACT.Square).then_inc(squared, 1)
            act.wait_ge(summed, GT)
            act.wait_ge(eps_set, 1)
            nc.scalar.activation(rstd[:].rearrange("p (n c) -> p n c", n=NCH), ps[1][:, :, 0:NC], ACT.Sqrt,
                                 scale=1.0 / (GT * P), bias=eps[:]).then_inc(root, 1)

        @block.tensor
        def _(pe):
            for t in range(GT):
                pe.wait_ge(squared, t + 1)
                for n in range(NCH):
                    m = nc.tensor.matmul(ps[1][:, n, 0:NC], ones[:], sq[:, t % 2, n * NC:(n + 1) * NC],
                                         start=t == 0, stop=t == GT - 1)
                m.then_inc(summed, 1)
            pe.wait_ge(scaled, GT)
            project_tiles(pe, nc, w, ps, y, w_in, mm, read, KT, kt=GT)

        @block.vector
        def _(dve):
            nc.vector.memset(eps[:], EPS).then_inc(eps_set, 1)
            for t in range(GT):
                nc.vector.scalar_tensor_tensor(out=y[:, t], in0=xc[:, t], scalar=dskip[:, bass.ds(g * GT + t, 1)], in1=y[:, t],
                                               op0=ALU.mult, op1=ALU.add).then_inc(skip, 1)
                dve.wait_ge(skip, t + 1)
                nc.vector.tensor_tensor(y[:, t], y[:, t], zs[:, t], ALU.mult).then_inc(gated, 1)
            dve.wait_ge(root, 1)
            nc.vector.reciprocal(rstd[:], rstd[:]).then_inc(inv, 1)
            dve.wait_ge(inv, 1)
            dve.wait_ge(gated, GT)
            for t in range(GT):
                nc.vector.scalar_tensor_tensor(out=y[:, t], in0=y[:, t], scalar=nssd[:, bass.ds(g * GT + t, 1)], in1=rstd[:],
                                               op0=ALU.mult, op1=ALU.mult).then_inc(scaled, 1)
            with dve.Fori(0, KT // 2) as i:
                for q in range(2):
                    for c in range(NCH):
                        dve.wait_ge(mm, NCH * (2 * i + q) + c + 1)
                        part = S[:, 2 * i + q, c * NC:(c + 1) * NC]
                        nc.vector.tensor_tensor(part, part, ps[q][:, c, 0:NC], ALU.add).then_inc(read[q], 1)
            for q in range(2):
                dve.wait_ge(read[q], NCH * KT // 2)


def final_norm(nc, o, x, y, ones, gain_d):
    with Phase(nc, "fn") as ph:
        sq = ph.sb("sq", [P, 2, TOK])
        rstd = ph.sb("rstd", [P, TOK])
        eps = ph.sb("eps", [P, 1])
        gain = ph.sb("gain", [P, KT])
        ps = ph.ps("ps", [P, NCH, 512])
        gain_in, eps_set, squared, summed, root, inv, scaled, saved = (
            ph.sem(n) for n in ("gain_in", "eps_set", "squared", "summed", "root", "inv", "scaled", "saved"))
        block = ph.block()

        @block.sync
        def _(sp):
            sp.dma_start(gain[:], gain_d).then_inc(gain_in, 16)
            for k in range(KT):
                sp.wait_ge(scaled, k + 1)
                sp.dma_start(o["y"][:, k], y[:, k]).then_inc(saved, 16)
            sp.wait_ge(saved, 16 * KT)

        @block.scalar
        def _(act):
            for k in range(KT):
                if k >= 2:
                    act.wait_ge(summed, k - 1)
                nc.scalar.activation(sq[:, k % 2], x[:, k], ACT.Square).then_inc(squared, 1)
            act.wait_ge(summed, KT)
            act.wait_ge(eps_set, 1)
            nc.scalar.activation(rstd[:].rearrange("p (n c) -> p n c", n=NCH), ps[:, :, 0:NC], ACT.Sqrt,
                                 scale=1.0 / DM, bias=eps[:]).then_inc(root, 1)

        @block.tensor
        def _(pe):
            for k in range(KT):
                pe.wait_ge(squared, k + 1)
                for n in range(NCH):
                    m = nc.tensor.matmul(ps[:, n, 0:NC], ones[:], sq[:, k % 2, n * NC:(n + 1) * NC],
                                         start=k == 0, stop=k == KT - 1)
                m.then_inc(summed, 1)

        @block.vector
        def _(dve):
            nc.vector.memset(eps[:], EPS).then_inc(eps_set, 1)
            dve.wait_ge(root, 1)
            nc.vector.reciprocal(rstd[:], rstd[:]).then_inc(inv, 1)
            dve.wait_ge(inv, 1)
            dve.wait_ge(gain_in, 16)
            for k in range(KT):
                nc.vector.scalar_tensor_tensor(out=y[:, k], in0=x[:, k], scalar=gain[:, k:k + 1], in1=rstd[:],
                                               op0=ALU.mult, op1=ALU.mult).then_inc(scaled, 1)


def ssd_branch(nc, d, o, h, tok, ones, ident, S):
    with ExitStack() as c:
        sb = lambda n, s: c.enter_context(nc.sbuf_tensor(n, s, F32))
        dt, dtA = sb("dt", [P, TB + 1, SH]), sb("dtA", [P, TB + 1, SH])
        ea, te, etot = (sb(n, [P, TB, SH]) for n in ("ea", "te", "etot"))
        upper, below = sb("upper", [P, P]), sb("below", [P, P])
        cw, cb = sb("cw", [P, SG * XT, CW]), sb("cb", [P, SG * XT])
        dskip, nssd = sb("dskip", [P, DI // P]), sb("nssd", [P, DI // P])
        hT = sb("hT", [P, DI // SG])
        time_steps(nc, d, tok, dt, dtA, ea, te, etot, upper)
        with Phase(nc, "si") as ph:
            loaded, zeroed = ph.sem("loaded"), ph.sem("zeroed")
            block = ph.block()

            @block.sync
            def _(sp):
                for dst, src in ((below, "below"), (cw, "conv_w"), (cb, "conv_b"), (dskip, "d_skip"), (nssd, "norm_ssd")):
                    sp.dma_start(dst[:], d[src]).then_inc(loaded, 16)
                sp.dma_start(o["conv_old"], d["conv_old"]).then_inc(loaded, 16)
                sp.wait_ge(loaded, 96)

            @block.gpsimd
            def _(pool):
                nc.gpsimd.memset(S[:], 0.0).then_inc(zeroed, 1)
                pool.wait_ge(zeroed, 1)
        xc, zs, y = sb("xc", [P, XT, TOK]), sb("zs", [P, 4, TOK]), sb("y", [P, 4, TOK])
        arena = sb("arena", [P, 10560])
        banks = c.enter_context(nc.psum_tensor("banks", [P, 8 * 512], F32))
        start, xb = carve(arena, 0, [P, XT, CW - 1 + TOK])
        with nc.Fori(0, SG) as g:
            ssd_project(nc, arena, banks, start, d, o, g, h, xb, xc, zs, cw, cb)
            ssd_scan(nc, arena, banks, d, o, g, xc, y, dt, dtA, ea, te, etot, upper, below, ident, hT)
            ssd_sample(nc, arena, banks, d, o, g, xc, y, dt, dtA, ones, ident)
            ssd_out(nc, arena, banks, d, g, xc, zs, y, ones, dskip, nssd, S)


def by_page(a):
    return a.rearrange("(c b) (i s) -> (b i) c s", c=2, s=PAGE)


def sample_scores(nc, d, scr, pj, tok, ones, ident, snew):
    CH = 4
    with Phase(nc, "s1") as ph:
        kx = ph.sb("kx", [ID, 2, NPAGE, PAGE])
        qx = ph.sb("qx", [ID, NIH, NB])
        pt = ph.sb("pt", [1, NB * NPAGE], I32)
        hot = ph.sb("hot", [P, 2])
        prod = ph.sb("prod", [P, 4, NB])
        wid = ph.sb("wid", [NB, NB, NIH])
        wib = ph.sb("wib", [P, NB, NIH])
        t = ph.sb("t", [P, NPAGE, NIH])
        tn = ph.sb("tn", [NB, NIH])
        sc = ph.sb("sc", [P, NB, NPAGE])
        st = ph.sb("st", [P, 2, P])
        pW = ph.ps("pW", [P, NB * NIH])
        pN = ph.ps("pN", [NB, NIH])
        pS = [ph.ps(f"pS{q}", [P, NPAGE, NIH]) for q in range(2)]
        pT = ph.ps("pT", [P, 2, P])
        k_in = [ph.sem(f"k_in{q}") for q in range(2)]
        small, prodd, widd, mm, tmp, summed, ch_s, turned, moved, stored, newd, wread = (
            ph.sem(n) for n in ("small", "prodd", "widd", "mm", "tmp", "summed", "ch", "turned", "moved", "stored", "newd", "wread"))
        block = ph.block()
        SC = float((NIH * ID) ** -0.5)

        @block.sync
        def _(sp):
            sp.dma_start(pt[:], d["page_table"]).then_inc(small, 16)
            sp.dma_start(hot[:], d["half"]).then_inc(small, 16)
            for u in range(2):
                sp.dma_start(qx[:].rearrange("p (t u) b -> p u t b", u=2)[:, u],
                             pj[u * ID:(u + 1) * ID, QI0:QI0 + 4, SEQ:TOK]).then_inc(small, 16)
            sp.wait_ge(small, 64)
            for b in range(NB):
                if b >= 2:
                    sp.wait_ge(mm, b - 1)
                with sp.Fori(0, NPAGE) as i:
                    page = sp.value_load(pt[0:1, bass.ds(b * NPAGE + i, 1)], min_val=0, max_val=NPOOL - 1)
                    sp.dma_start(kx[:, b % 2, i], d["cache_kidx"][page]).then_inc(k_in[b % 2], 16)
            sp.wait_ge(moved, 1)
            sp.dma_start(by_page(scr["score"]), st[:]).then_inc(stored, 16)
            sp.wait_ge(stored, 16)

        @block.tensor
        def _(pe):
            pe.wait_ge(prodd, 1)
            for u in range(4):
                m = nc.tensor.matmul(pN[:, 2 * u:2 * u + 2], prod[:, u], hot[:], start=True, stop=True)
            pe.wait_ge(widd, 1)
            nc.tensor.matmul(pW[:], ones[0:NB, :], wid[:].rearrange("p b h -> p (b h)"), start=True, stop=True).then_inc(newd, 1)
            for b in range(NB):
                pe.wait_ge(k_in[b % 2], 16 * NPAGE * (b // 2 + 1))
                if b >= 2:
                    pe.wait_ge(tmp, b - 1)
                for i in range(NPAGE):
                    m = nc.tensor.matmul(pS[b % 2][:, i], kx[:, b % 2, i], qx[:, :, b], start=True, stop=True)
                m.then_inc(mm, 1)
            pe.wait_ge(summed, NB)
            for c in range(2):
                m = nc.tensor.transpose(pT[:, c], sc[:, 4 * c:4 * c + 4].rearrange("p b i -> p (b i)"), ident[:])
            m.then_inc(turned, 1)

        @block.vector
        def _(dve):
            ch = Chain(dve, ch_s)
            dve.wait_ge(small, 64)
            nc.vector.tensor_tensor(prod[:], pj[:, QI0:QI0 + 4, SEQ:TOK],
                                    pj[:, KI0, SEQ:TOK].unsqueeze(1).to_broadcast([P, 4, NB]), ALU.mult).then_inc(prodd, 1)
            wi = tok[0:NB, TB, NKV * HD:NKV * HD + NIH]
            nc.vector.scalar_tensor_tensor(out=wid[:], in0=wi.unsqueeze(1).to_broadcast([NB, NB, NIH]), scalar=SC,
                                           in1=ident[0:NB, 0:NB].unsqueeze(2).to_broadcast([NB, NB, NIH]),
                                           op0=ALU.mult, op1=ALU.mult).then_inc(widd, 1)
            dve.wait_ge(newd, 1)
            ch.link(nc.vector.tensor_copy(wib[:].rearrange("p b h -> p (b h)"), pW[:]))
            ch.link(nc.vector.scalar_tensor_tensor(out=tn[:], in0=pN[:], scalar=0.0, in1=wi, op0=ALU.max, op1=ALU.mult))
            ch.link(nc.vector.tensor_reduce(snew[:], tn[:], AX, ALU.add))
            ch.link(nc.vector.tensor_scalar(snew[:], snew[:], SC, None, ALU.mult))
            for b in range(NB):
                dve.wait_ge(mm, b + 1)
                if b:
                    dve.wait_ge(summed, b)
                nc.vector.scalar_tensor_tensor(out=t[:], in0=pS[b % 2][:], scalar=0.0,
                                               in1=wib[:, b].unsqueeze(1).to_broadcast([P, NPAGE, NIH]),
                                               op0=ALU.max, op1=ALU.mult).then_inc(tmp, 1)
                dve.wait_ge(tmp, b + 1)
                nc.vector.tensor_reduce(sc[:, b], t[:], AX, ALU.add).then_inc(summed, 1)
            dve.wait_ge(turned, 1)
            nc.vector.tensor_copy(st[:], pT[:]).then_inc(moved, 1)


def sample_topk(nc, scr, snew, cnt, seln):
    with Phase(nc, "s2") as ph:
        sc = ph.sb("sc", [NB, PAST + 1])
        sel = ph.sb("sel", [NB, PAST + 1])
        pos = ph.sb("pos", [NB, PAST])
        m8 = ph.sb("m8", [NB, 8])
        loaded, ch_s, tick, ready, stored = (ph.sem(n) for n in ("loaded", "ch", "tick", "ready", "stored"))
        block = ph.block()

        @block.sync
        def _(sp):
            sp.dma_start(sc[:, 0:PAST], scr["score"]).then_inc(loaded, 16)
            sp.wait_ge(ready, 1)
            sp.dma_start(scr["pos"], pos[:]).then_inc(stored, 16)
            sp.wait_ge(stored, 16)

        @block.vector
        def _(dve):
            ch = Chain(dve, ch_s, tick)
            ch.link(nc.vector.tensor_copy(sc[:, PAST:PAST + 1], snew[:]))
            dve.wait_ge(loaded, 16)
            ROUNDS, U = TOPK // 8, 4
            with dve.Fori(0, ROUNDS // U) as j:
                ch.loop(j, 2 * U)
                for _ in range(U):
                    ch.link(nc.vector.max(m8[:], sc[:]))
                    ch.link(nc.vector.match_replace(sc[:], m8[:], sc[:], TAKEN))
            ch.done(ROUNDS // U)
            ch.link(nc.vector.tensor_scalar(sel[:], sc[:], -3.2e38, None, ALU.is_lt))
            ch.link(nc.vector.tensor_tensor_scan(pos[:], sel[:, 0:PAST], sel[:, 0:PAST], 0.0, ALU.add, ALU.max))
            ch.link(nc.vector.tensor_copy(cnt[:], pos[:, PAST - 1:PAST]))
            ch.link(nc.vector.tensor_copy(seln[:], sel[:, PAST:PAST + 1]))
            ch.link(nc.vector.tensor_tensor(pos[:], pos[:], sel[:, 0:PAST], ALU.mult))
            ch.link(nc.vector.tensor_scalar(pos[:], pos[:], -1.0, None, ALU.add))
            dve.sem_inc(ready, 1)


def sample_gather(nc, d, scr, ident, gathered, kv, brows):
    RING = 4
    with Phase(nc, "s3") as ph:
        pt = ph.sb("pt", [P, 2, P])
        pos = ph.sb("pos", [P, NB * NPAGE])
        iota = ph.sb("iota", [P, TOPK], F16)
        vals = ph.sb("vals", [P, NB * NPAGE, 3], F16)
        tab = ph.sb("tab", [P, NB * NPAGE], I32)
        hots = ph.sb("hots", [P, RING, TOPK], F16)
        ent = ph.sb("ent", [P, NB, 2, 3])
        where = ph.sb("where", [P, 3, NB, 2])
        row = ph.sb("row", [P, NB, 2], U32)
        brow = ph.sb("brow", [P, NB, 2], U32)
        pT = ph.ps("pT", [P, 2, P])
        pE = [[ph.ps(f"pE{q}{f}", [P, 512]) for f in range(2)] for q in range(2)]
        loaded, turned, posd, valsd, hotd, used, mm, read, ch_s, ready = (
            ph.sem(n) for n in ("loaded", "turned", "posd", "valsd", "hotd", "used", "mm", "read", "ch", "ready"))
        block = ph.block()

        @block.sync
        def _(sp):
            sp.dma_start(pt[:], by_page(scr["pos"])).then_inc(loaded, 16)
            sp.dma_start(iota[:], d["iota"]).then_inc(loaded, 16)
            sp.dma_start(vals[:], d["slots"]).then_inc(loaded, 16)
            sp.dma_start(tab[:], d["page_table"].to_broadcast([P, NB * NPAGE])).then_inc(loaded, 16)
            sp.wait_ge(loaded, 64)

        @block.tensor
        def _(pe):
            pe.wait_ge(loaded, 64)
            for c in range(2):
                m = nc.tensor.transpose(pT[:, c], pt[:, c], ident[:])
            m.then_inc(turned, 1)
            pe.wait_ge(valsd, 1)
            with pe.Fori(0, NB // 2) as i:
                for q in range(2):
                    b = 2 * i + q
                    pe.wait_ge(read, 2 * i)
                    for p in range(NPAGE):
                        pe.wait_ge(hotd, NPAGE * b + p + 1)
                        for f in range(2):
                            m = nc.tensor.matmul(pE[q][f][:, 0:3], hots[:, p % RING, f * P:(f + 1) * P],
                                                 vals[:, b * NPAGE + p], start=p == 0, stop=p == NPAGE - 1)
                        m.then_inc(used, 1)

        @block.vector
        def _(dve):
            ch = Chain(dve, ch_s)
            dve.wait_ge(loaded, 64)
            nc.vector.tensor_copy(vals[:, :, 1], tab[:]).then_inc(valsd, 1)
            dve.wait_ge(turned, 1)
            ch.link(nc.vector.tensor_copy(pos[:], pT[:].rearrange("p c n -> p (c n)")))
            with dve.Fori(0, NB // 2) as i:
                for q in range(2):
                    b = 2 * i + q
                    for p in range(NPAGE):
                        if p >= RING:
                            dve.wait_ge(used, NPAGE * b + p - RING + 1)
                        else:
                            dve.wait_ge(used, NPAGE * b)
                        nc.vector.tensor_scalar(hots[:, p % RING], iota[:], pos[:, bass.ds(b * NPAGE + p, 1)], None,
                                                ALU.is_equal).then_inc(hotd, 1)
                    dve.wait_ge(used, NPAGE * (b + 1))
                    for f in range(2):
                        v = nc.vector.tensor_copy(ent[:, b, f], pE[q][f][:, 0:3])
                    v.then_inc(read, 1)
            dve.wait_ge(read, NB)
            off, page, log = (ent[:, :, :, n] for n in range(3))
            ch.link(nc.vector.scalar_tensor_tensor(out=where[:, 0], in0=page, scalar=float(PAGE), in1=off, op0=ALU.mult, op1=ALU.add))
            ch.link(nc.vector.scalar_tensor_tensor(out=where[:, 1], in0=log, scalar=float(PAGE), in1=off, op0=ALU.mult, op1=ALU.add))
            ch.link(nc.vector.tensor_scalar(where[:, 1], where[:, 1], float(WIN - 1 - PAST), 0.0, ALU.add, ALU.max))
            ch.link(nc.vector.tensor_copy(row[:], where[:, 0]))
            ch.link(nc.vector.tensor_copy(brow[:], where[:, 1]))
            dve.sem_inc(ready, 1)

        @block.gpsimd
        def _(pool):
            pool.wait_ge(ready, 1)
            n = 0
            for b in range(NB):
                for f in range(2):
                    at = bass.IndirectOffsetOnAxis(row[:, b, f:f + 1], 0)
                    for j, src in enumerate((d["cache_k"], d["cache_v"])):
                        pool.indirect_dma_start(kv[:, b, f, j], None, src, at).then_inc(gathered, 16)
                    pool.indirect_dma_start(brows[:, b, f], None, scr["brow"],
                                            bass.IndirectOffsetOnAxis(brow[:, b, f:f + 1], 0)).then_inc(gathered, 16)
                    n += 48
            pool.wait_ge(gathered, n)


def sample_attend(nc, d, scr, pj, tok, ones, ident, cnt, seln, kv, brows, att):
    NS = TOPK + 1
    F = 2 * HD
    with Phase(nc, "s4") as ph:
        hot = ph.sb("hot", [P, 2])
        qt = ph.sb("qt", [NB, DM])
        qm = ph.sb("qm", [NB, 2, DM])
        prod = ph.sb("prod", [P, DM])
        pn = ph.sb("pn", [P, KT, NB])
        Lg = ph.sb("Lg", [P, NB, 2, NH])
        Ln = ph.sb("Ln", [NB, NH])
        bn = ph.sb("bn", [NB, NH])
        lack = ph.sb("lack", [NB, 1])
        cd = ph.sb("cd", [NB, NB])
        cb = ph.sb("cb", [P, NB])
        slot = ph.sb("slot", [P, 2])
        mb = ph.sb("mb", [P, NB, 2])
        LL = ph.sb("LL", [NH, NB, NS])
        nm = ph.sb("nm", [NH, NB])
        den = ph.sb("den", [NH, NB])
        rd = ph.sb("rd", [NH, NB])
        PT = ph.sb("PT", [P, NB, 2, NH])
        wn = ph.sb("wn", [NB, NH])
        wd = ph.sb("wd", [NB, NB, NH])
        pq = ph.ps("pq", [P, 2, DM])
        pm = ph.ps("pm", [P, 512])
        pL = pq[0:NH].rearrange("h a (b j) -> h (a b) j", b=NB // 2)
        small, ch_s, qturn, qmd, qb, lread, pnd, nlog, cdd, cbd, lready, lturn, mx, ex, pready, pturn, wready, wturn, ptd, od = (
            ph.sem(n) for n in ("small", "ch", "qturn", "qmd", "qb", "lread", "pnd", "nlog", "cdd", "cbd", "lready", "lturn",
                                "mx", "ex", "pready", "pturn", "wready", "wturn", "ptd", "od"))
        block = ph.block()

        @block.sync
        def _(sp):
            sp.dma_start(hot[:], d["half"]).then_inc(small, 16)
            sp.dma_start(slot[:], d["slot"]).then_inc(small, 16)
            sp.dma_start(bn[:], scr["brow"][WIN - 1:WIN, :].to_broadcast([NB, NH])).then_inc(small, 16)
            sp.wait_ge(small, 48)

        @block.tensor
        def _(pe):
            for t in range(KT):
                m = nc.tensor.transpose(pq[0:NB, 1, t * P:(t + 1) * P], pj[:, QT0 + t, SEQ:TOK], ident[:])
            m.then_inc(qturn, 1)
            pe.wait_ge(small, 48)
            pe.wait_ge(pnd, 1)
            for t in range(KT):
                m = nc.tensor.matmul(pm[0:NB, 2 * t:2 * t + 2], pn[:, t], hot[:], start=True, stop=True)
            pe.wait_ge(cdd, 1)
            nc.tensor.matmul(pm[:, 16:16 + NB], ones[0:NB, :], cd[:], start=True, stop=True).then_inc(nlog, 1)
            for b in range(NB):
                pe.wait_ge(qmd, b + 1)
                if b >= 2:
                    pe.wait_ge(lread, b - 1)
                for c in range(2):
                    m = nc.tensor.matmul(pq[:, b % 2, c * 512:(c + 1) * 512], ones[0:NB, :], qm[:, b % 2, c * 512:(c + 1) * 512],
                                         start=True, stop=True)
                m.then_inc(qb, 1)
            pe.wait_ge(lready, 1)
            for b in range(NB):
                for f in range(2):
                    nc.tensor.transpose(pL[:, b, f * P:(f + 1) * P], Lg[:, b, f], ident[:])
            nc.tensor.transpose(pm[0:NH, 64:64 + NB], Ln[:], ident[0:NB, 0:NB]).then_inc(lturn, 1)
            pe.wait_ge(pready, 1)
            for b in range(NB):
                for f in range(2):
                    at = (2 * b + f) * NH
                    nc.tensor.transpose(pq[:, 0, at:at + NH], LL[:, b, f * P:(f + 1) * P], ident[0:NH, 0:NH])
            nc.tensor.transpose(pq[0:NB, 1, 0:NH], LL[:, :, TOPK], ident[0:NH, 0:NH]).then_inc(pturn, 1)
            pe.wait_ge(ptd, 1)
            for b in range(NB):
                for m in range(2):
                    out = pm[:, 128 + (2 * b + m) * NH:128 + (2 * b + m + 1) * NH]
                    for f in range(2):
                        nc.tensor.matmul(out, kv[:, b, f, 1, m * F:(m + 1) * F], PT[:, b, f], start=f == 0, stop=False)
                    x = nc.tensor.matmul(out, tok[0:NB, TB, m * F:(m + 1) * F], wd[:, b], start=False, stop=True)
            x.then_inc(od, 1)

        @block.scalar
        def _(act):
            act.wait_ge(mx, 1)
            for b in range(NB):
                nc.scalar.activation(LL[:, b], LL[:, b], ACT.Exp, bias=nm[:, b:b + 1], accum_out=den[:, b:b + 1]).then_inc(ex, 1)

        @block.vector
        def _(dve):
            ch = Chain(dve, ch_s)
            nc.vector.tensor_tensor(pn[:].rearrange("p (m g) b -> p m g b", m=2),
                                    pj[:, QT0:QT0 + KT, SEQ:TOK].rearrange("p (m g) b -> p m g b", m=2),
                                    pj[:, KT0:KT0 + 2, SEQ:TOK].unsqueeze(2).to_broadcast([P, 2, 4, NB]), ALU.mult).then_inc(pnd, 1)
            ch.link(nc.vector.tensor_tensor(cd[:], cnt[:].to_broadcast([NB, NB]), ident[0:NB, 0:NB], ALU.mult))
            dve.sem_inc(cdd, 1)
            dve.wait_ge(qturn, 1)
            ch.link(nc.vector.tensor_copy(qt[:], pq[0:NB, 1]))
            dve.wait_ge(nlog, 1)
            dve.wait_ge(small, 48)
            ch.link(nc.vector.scalar_tensor_tensor(out=Ln[:], in0=pm[0:NB, 0:NH], scalar=float(HD ** -0.5), in1=bn[:],
                                                   op0=ALU.mult, op1=ALU.add))
            ch.link(nc.vector.tensor_copy(cb[:], pm[:, 16:16 + NB]))
            ch.link(nc.vector.tensor_scalar(lack[:], seln[:], 1.0, BIG, ALU.subtract, ALU.mult))
            ch.link(nc.vector.tensor_scalar(Ln[:], Ln[:], lack[:], None, ALU.add))
            ch.link(nc.vector.tensor_tensor(mb[:], slot[:].unsqueeze(1).to_broadcast([P, NB, 2]),
                                            cb[:].unsqueeze(2).to_broadcast([P, NB, 2]), ALU.is_ge))
            ch.link(nc.vector.tensor_scalar(mb[:], mb[:], -BIG, None, ALU.mult))
            for b in range(NB):
                if b >= 2:
                    dve.wait_ge(qb, b - 1)
                nc.vector.tensor_scalar(qm[:, b % 2], qt[:], ident[0:NB, b:b + 1], None, ALU.mult).then_inc(qmd, 1)
                dve.wait_ge(qb, b + 1)
                for f in range(2):
                    k4 = kv[:, b, f, 0].rearrange("p (m c) -> p m c", m=2).unsqueeze(2).to_broadcast([P, 2, 4, F])
                    x = nc.vector.tensor_tensor(prod[:].rearrange("p (m g c) -> p m g c", m=2, g=4), k4,
                                                pq[:, b % 2].rearrange("p (m g c) -> p m g c", m=2, g=4), ALU.mult)
                    ch.link(x)
                    ch.link(nc.vector.tensor_reduce(Lg[:, b, f], prod[:].rearrange("p (h c) -> p h c", c=HD), AX, ALU.add))
                dve.sem_inc(lread, 1)
            fl = lambda a: a[:].rearrange("p b f h -> p (b f) h")
            ch.link(nc.vector.scalar_tensor_tensor(out=fl(Lg), in0=fl(Lg), scalar=float(HD ** -0.5), in1=fl(brows),
                                                   op0=ALU.mult, op1=ALU.add))
            ch.link(nc.vector.tensor_tensor(fl(Lg), fl(Lg), mb[:].rearrange("p b f -> p (b f)").unsqueeze(2).to_broadcast([P, 2 * NB, NH]),
                                            ALU.add))
            dve.sem_inc(lready, 1)
            dve.wait_ge(lturn, 1)
            ch.link(nc.vector.tensor_copy(LL[:, :, 0:TOPK], pL[:]))
            ch.link(nc.vector.tensor_copy(LL[:, :, TOPK], pm[0:NH, 64:64 + NB]))
            nc.vector.tensor_reduce(nm[:], LL[:], AX, ALU.max, negate=True).then_inc(mx, 1)
            dve.wait_ge(ex, NB)
            ch.link(nc.vector.reciprocal(rd[:], den[:]))
            ch.link(nc.vector.tensor_tensor(LL[:], LL[:], rd[:].unsqueeze(2).to_broadcast([NH, NB, NS]), ALU.mult))
            dve.sem_inc(pready, 1)
            dve.wait_ge(pturn, 1)
            ch.link(nc.vector.tensor_copy(PT[:].rearrange("p b f h -> p (b f h)"), pq[:, 0, 0:2 * NB * NH]))
            ch.link(nc.vector.tensor_copy(wn[:], pq[0:NB, 1, 0:NH]))
            ch.link(nc.vector.tensor_tensor(wd[:], wn[:].unsqueeze(1).to_broadcast([NB, NB, NH]),
                                            ident[0:NB, 0:NB].unsqueeze(2).to_broadcast([NB, NB, NH]), ALU.mult))
            dve.sem_inc(ptd, 1)
            dve.wait_ge(od, 1)
            ov = pm[:, 128:128 + 2 * NB * NH].rearrange("p (b m h) -> p m h b", b=NB, m=2)
            for m in range(2):
                for u in range(2):
                    r = slice(u * HD, (u + 1) * HD)
                    ch.link(nc.vector.tensor_copy(att[r, 4 * m:4 * m + 4, SEQ:TOK], ov[r, m, 8 * m + u:8 * m + 8:2]))


def move(nc, name, pairs):
    with Phase(nc, name) as ph:
        moved = ph.sem("moved")
        block = ph.block()

        @block.sync
        def _(sp):
            for dst, src in pairs:
                sp.dma_start(dst, src).then_inc(moved, 16)
            sp.wait_ge(moved, 16 * len(pairs))


def program(nc, d, o):
    dram = lambda n, s: nc.dram_tensor(f"scr_{n}", s, F32).ap()
    scr = {"byh": dram("byh", [NH, 512]), "brow": dram("brow", [WIN, NH]), "x": dram("x", [P, KT, TOK]),
           "A": dram("A", [P, KT, TOK]), "score": dram("score", [NB, PAST]), "pos": dram("pos", [NB, PAST])}
    with ExitStack() as ctx:
        def buf(c, n, s, t=F32):
            return c.enter_context(nc.sbuf_tensor(n, s, t))

        gathered = ctx.enter_context(nc.semaphore("gathered"))
        ada, sg = buf(ctx, "ada", [P, NA, NCOND]), buf(ctx, "sg", [P, 3, KT, NCOND])
        ones, ident = buf(ctx, "ones", [P, P]), buf(ctx, "ident", [P, P])
        h = buf(ctx, "h", [P, KT, TOK])
        adaln(nc, d, ada, sg)
        with ExitStack() as c1:
            x = buf(c1, "x", [P, KT, TOK])
            set_ones(nc, ones)
            norm_mod(nc, "n1", x, h, ones, ada, sg, 0, load=d["x"])
            ffn(nc, "f1", d["w_f1i"], d["w_f1o"], x, h, ada, 0)
            norm_mod(nc, "n2", x, h, ones, ada, sg, 1, store=scr["x"])
        with ExitStack() as c2:
            tok = buf(c2, "tok", [P, TB + 1, VW])
            with ExitStack() as c3:
                att = buf(c3, "att", [P, KT, TOK])
                with ExitStack() as c4:
                    pj = buf(c4, "pj", [P, AT, TOK])
                    project_attention(nc, d, o, h, pj, tok)
                    with ExitStack() as c5:
                        bias = buf(c5, "bias", [P, NH, WIN])
                        tables(nc, d, scr, ident, bias)
                        mask = buf(c5, "mask", [P, mask_at(TB)])
                        select_keys(nc, pj, tok, mask)
                        attend(nc, pj, tok, mask, bias, ident, att)
                    with ExitStack() as c5:
                        snew, cnt, seln = (buf(c5, n, [NB, 1]) for n in ("snew", "cnt", "seln"))
                        sample_scores(nc, d, scr, pj, tok, ones, ident, snew)
                        sample_topk(nc, scr, snew, cnt, seln)
                        kv = buf(c5, "kv", [P, NB, 2, 2, NKV * HD])
                        brows = buf(c5, "brows", [P, NB, 2, NH])
                        sample_gather(nc, d, scr, ident, gathered, kv, brows)
                        sample_attend(nc, d, scr, pj, tok, ones, ident, cnt, seln, kv, brows, att)
                A = buf(c3, "A", [P, KT, TOK])
                attention_out(nc, d, h, att, A)
                move(nc, "mA", [(scr["A"], A[:])])
            S = buf(c2, "S", [P, KT, TOK])
            ssd_branch(nc, d, o, h, tok, ones, ident, S)
            A2 = buf(c2, "A2", [P, KT, TOK])
            move(nc, "mB", [(A2[:], scr["A"])])
            ssd_gate(nc, d, h, A2, S)
            x = buf(c2, "x2", [P, KT, TOK])
            mix_out(nc, d, scr["x"], x, A2, ada)
            move(nc, "mC", [(scr["x"], x[:])])
        x = buf(ctx, "x3", [P, KT, TOK])
        norm_mod(nc, "n3", x, h, ones, ada, sg, 2, load=scr["x"])
        ffn(nc, "f2", d["w_f2i"], d["w_f2o"], x, h, ada, 2)
        final_norm(nc, o, x, h, ones, d["norm_final"])


def set_ones(nc, ones):
    with Phase(nc, "on") as ph:
        ready = ph.sem("ready")
        block = ph.block()

        @block.gpsimd
        def _(pool):
            nc.gpsimd.memset(ones[:], 1.0).then_inc(ready, 1)
            pool.wait_ge(ready, 1)


def tiled(w, cols):
    k, m = w.shape
    return np.ascontiguousarray(w.reshape(k // P, P, m // cols, cols).transpose(2, 1, 0, 3))


def fmajor(a):
    r, f = a.shape
    return np.ascontiguousarray(a.T.reshape(f // P, P, r).transpose(1, 0, 2))


def layout(i):
    a = {}
    a["x"] = fmajor(np.concatenate([i["x_prompt"][0], i["x_sample"][:, 0]], 0))
    a["c"] = fmajor(np.concatenate([i["c_prompt"], i["c_sample"]], 0))
    a["w_ada"] = tiled(i["w_ada"][0], P)
    a["b_ada"] = np.ascontiguousarray(i["b_ada"][0].reshape(NA, P).T)
    gains = np.stack([i["norm_ffn1"][0], i["norm_mix"][0], i["norm_ffn2"][0]])
    a["gains"] = np.ascontiguousarray(gains.reshape(3, KT, P).transpose(2, 0, 1))
    for n in (1, 2):
        wi = tiled(i[f"w_ffn{n}_in"][0], P)
        a[f"w_f{n}i"] = np.ascontiguousarray(np.stack([wi[:FT], wi[FT:]], 2)).reshape(FT, P, 2 * KT * P)
        wo = tiled(i[f"w_ffn{n}_out"][0], P)
        a[f"w_f{n}o"] = np.ascontiguousarray(wo.reshape(KT, P, 2, FT // 2, P).transpose(0, 2, 1, 3, 4)).reshape(2 * KT, P, FT // 2, P)
    cut = np.cumsum([0, NH * HD, NKV * HD, NKV * HD, NIH * ID, ID, NIH, DI, CONVD, SH, DM, DM])
    q, k, v, qi, ki, wi, z, xbc, dt, ga, gs = (i["w_in"][0][:, cut[n]:cut[n + 1]] for n in range(11))
    q = q[:, HEADCOLS]
    a["w_att"] = tiled(np.concatenate([q, k, qi, ki, ki], 1), P)
    wt = np.concatenate([v, wi, dt], 1)
    a["w_tok"] = np.ascontiguousarray(wt.reshape(KT, P, VW).transpose(1, 0, 2))
    a["w_ao"] = np.ascontiguousarray(np.stack([tiled(ga, P), tiled(i["w_attn_out"][0][HEADCOLS], P)], 1)).reshape(2 * KT, P, KT, P)
    a["w_gs"] = tiled(gs, P)
    a["w_out"] = tiled(i["w_out"][0], P)
    xt, zt = tiled(xbc, P)[ORDER].reshape(SG, XT, P, KT, P), tiled(z, P).reshape(SG, 4, P, KT, P)
    a["w_ssd"] = np.concatenate([xt, zt], 1)
    a["w_so"] = np.ascontiguousarray(i["w_ssd_out"][0].reshape(SG, 4, P, KT, P).transpose(0, 3, 2, 1, 4))
    ctile = lambda v: v.reshape(v.shape[:-1] + (CONVD // P, P))[..., ORDER, :]
    a["conv_w"] = np.ascontiguousarray(ctile(i["conv_w"][0]).transpose(2, 1, 0))
    a["conv_b"] = np.ascontiguousarray(ctile(i["conv_b"][0]).T)
    sc = i["state_conv"][0]
    a["state_conv"] = np.ascontiguousarray(ctile(sc).reshape(NB, CW - 1, SG, XT, P).transpose(2, 4, 3, 1, 0))
    a["conv_old"] = np.ascontiguousarray(sc[:, 1:])
    a["dt_bias"] = np.ascontiguousarray(np.broadcast_to(i["dt_bias"][0], (P, SH)))
    a["a_log"] = np.ascontiguousarray(np.broadcast_to(i["a_log"][0], (P, SH)))
    a["upper"] = np.triu(np.ones((P, P), np.float32))
    a["below"] = np.tril(np.ones((P, P), np.float32), -1)
    a["d_skip"] = np.ascontiguousarray(np.repeat(i["d_skip"][0], DI // SH).reshape(DI // P, P).T)
    a["norm_ssd"] = np.ascontiguousarray(i["norm_ssd"][0].reshape(DI // P, P).T)
    a["norm_final"] = np.ascontiguousarray(i["norm_final"].reshape(KT, P).T)
    ssm = i["state_ssm"][0].reshape(NB, SG, 4, P, DS)
    a["state_ssm"] = np.ascontiguousarray(ssm.transpose(1, 3, 2, 0, 4)).reshape(SG, P, 4 * NB * DS)
    a["cache_kidx"] = np.ascontiguousarray(i["cache_kidx"][0].transpose(0, 2, 1))
    a["cache_k"] = np.ascontiguousarray(i["cache_k"][0].reshape(NPOOL * PAGE, NKV * HD))
    a["cache_v"] = np.ascontiguousarray(i["cache_v"][0].reshape(NPOOL * PAGE, NKV * HD))
    a["page_table"] = np.ascontiguousarray(i["page_table"].reshape(1, NB * NPAGE))
    a["half"] = (np.arange(P)[:, None] // HD == np.arange(2)[None, :]).astype(np.float32)
    a["iota"] = np.ascontiguousarray(np.broadcast_to(np.arange(TOPK, dtype=np.float16), (P, TOPK)))
    slots = np.zeros((P, NB, NPAGE, 3), np.float16)
    slots[..., 0] = np.arange(P)[:, None, None]
    slots[..., 2] = np.arange(NPAGE)
    a["slots"] = slots.reshape(P, NB * NPAGE, 3)
    a["slot"] = (np.arange(P)[:, None] + P * np.arange(2)[None, :]).astype(np.float32)
    a["rel_bias"] = np.ascontiguousarray(i["rel_bias"][:, HEADS])
    a["flip"] = np.ascontiguousarray(np.eye(P, dtype=np.float32)[::-1])
    a["ident"] = np.eye(P, dtype=np.float32)
    dist = np.maximum(255 - np.arange(512), 0)
    far = NBUCKET // 2 + (np.log(np.maximum(dist, 1).astype(np.float32) / (NBUCKET // 2)) / np.log(MAXD / (NBUCKET // 2))
                          * (NBUCKET - NBUCKET // 2)).astype(np.int32)
    bucket = np.where(dist < NBUCKET // 2, dist, np.minimum(far, NBUCKET - 1))
    a["hot"] = (np.arange(NBUCKET)[:, None] == bucket[None, :]).astype(np.float32)
    return a


HEADS = np.array([4 * (2 * m + u) + g for m in range(2) for g in range(4) for u in range(2)])
HEADCOLS = (HEADS[:, None] * HD + np.arange(HD)).reshape(-1)

OUTS = {"k": [P, 2, TOK], "kidx": [ID, TOK], "v_p": [P, TB, NKV * HD], "v_s": [NB, NKV * HD], "y": [P, KT, TOK],
        "conv_p": [SG, P, XT, CW - 1], "conv_s": [SG, P, XT, NB], "conv_old": [NB, CW - 2, CONVD], "ssm_p": [SG, P, DI // SG],
        "ssm_s": [SG, P, 4 * NB * DS]}
ORDER = np.concatenate([np.concatenate([np.arange(4) + 4 * g, [16 + g], [20 + g]]) for g in range(SG)])


def unlay(r):
    y = r["y"].transpose(2, 1, 0).reshape(TOK, DM)
    k = r["k"].transpose(2, 1, 0).reshape(TOK, NKV, HD)
    kidx = r["kidx"].T
    v = r["v_p"].transpose(1, 0, 2).reshape(1, 1, SEQ, NKV, HD)
    back = np.argsort(ORDER)
    conv_p = r["conv_p"].transpose(3, 0, 2, 1).reshape(CW - 1, SG * XT, P)[:, back].reshape(1, 1, CW - 1, CONVD)
    new = r["conv_s"].transpose(3, 0, 2, 1).reshape(NB, SG * XT, P)[:, back].reshape(NB, 1, CONVD)
    conv_s = np.concatenate([r["conv_old"], new], 1)[None]
    R, PD = SH // SG, DI // SH
    ssm_p = r["ssm_p"].reshape(SG, DS, R, PD).transpose(0, 2, 3, 1).reshape(1, 1, SH, PD, DS)
    ssm_s = r["ssm_s"].reshape(SG, 2, PD, R // 2, NB, DS).transpose(4, 0, 3, 1, 2, 5).reshape(1, NB, SH, PD, DS)
    out = (y[:SEQ][None], y[SEQ:][:, None], k[:SEQ][None, None], v, kidx[:SEQ][None, None], ssm_p, conv_p,
           k[SEQ:].reshape(1, NB, 1, NKV, HD), r["v_s"].reshape(1, NB, 1, NKV, HD), kidx[SEQ:].reshape(1, NB, 1, ID),
           ssm_s, conv_s)
    return tuple(np.ascontiguousarray(a) for a in out)


def kernel(**inputs):
    import concourse.bacc as bacc
    from concourse.bass_utils import run_bass_kernel_spmd

    nc = bacc.Bacc("TRN2", target_bir_lowering=False, num_devices=1)
    arrays = layout({n: np.asarray(a) for n, a in inputs.items()})
    d = {n: nc.dram_tensor(f"in_{n}", a.shape, mybir.dt.from_np(a.dtype), kind="ExternalInput").ap() for n, a in arrays.items()}
    o = {n: nc.dram_tensor(f"out_{n}", s, F32, kind="ExternalOutput").ap() for n, s in OUTS.items()}
    program(nc, d, o)
    r = run_bass_kernel_spmd(nc, [{f"in_{n}": a for n, a in arrays.items()}], core_ids=[0])
    return unlay({n: r.results[0][f"out_{n}"] for n in OUTS})
```

```python
from contextlib import ExitStack

import numpy as np

import concourse.bass as bass
from concourse import mybir

P = 128
DM, SEQ, NB = 1024, 1024, 8
TOK = SEQ + NB
NCH = 3
NC = TOK // NCH
LASTP = NC - NB
KT = DM // P
TB = SEQ // P
DFF = 2816
FT = DFF // P
NH, HD, NKV = 16, 64, 4
NIH, ID = 8, 64
TOPK = 256
PAST, PAGE, NPAGE, NPOOL = 4096, 128, 32, 320
NBUCKET, MAXD = 32, 128
DI, SH, SG, DS, CW = 2048, 32, 4, 128, 4
CONVD = DI + 2 * SG * DS
XT = 6
EPS = 1e-6
AT = 15
QT0, KT0, QI0, KI0 = 0, 8, 10, 14
VW = NKV * HD + NIH + SH
BIG = 1.0e30
CAUSAL, TAKEN = -3.0e38, -3.3e38
WIN = 2 * P
NA = 9 * KT
NCOND = 1 + NB

F32 = mybir.dt.float32
F16 = mybir.dt.float16
I32 = mybir.dt.int32
U32 = mybir.dt.uint32
ALU = mybir.AluOpType
ACT = mybir.ActivationFunctionType
AX = mybir.AxisListType.X


class Chain:

    def __init__(self, eng, sem, tick=None):
        self.eng, self.sem, self.tick, self.n, self.off = eng, sem, tick, 0, 0

    def link(self, ins):
        self.n += 1
        ins.then_inc(self.sem, 1)
        self.eng.wait_ge(self.sem, self.off + self.n)
        if self.tick is not None:
            self.eng.sem_inc(self.tick, 1)

    def loop(self, i, per):
        self.off, self.start, self.per = i * per, self.n, per

    def done(self, times):
        assert self.n - self.start == self.per, (self.n - self.start, self.per)
        self.off, self.n = 0, self.start + self.per * times


def carve(arena, at, shape):
    n = int(np.prod(shape[1:]))
    a = arena[0:shape[0], at:at + n]
    assert at + n <= arena.shape[1], (at, n)
    names = "abcd"[:len(shape) - 1]
    if len(names) > 1:
        a = a.rearrange(f"p ({' '.join(names)}) -> p {' '.join(names)}", **dict(zip(names, shape[1:])))
    return at + n, a


class Phase:

    def __init__(self, nc, name, arena=None, start=0, banks=None):
        self.nc, self.name, self.ctx, self.arena, self.at = nc, name, ExitStack(), arena, start
        self.banks, self.bank, self.sems, self.blocks = banks, 0, [], ExitStack()

    def __enter__(self):
        return self

    def __exit__(self, *a):
        self.blocks.__exit__(*a)
        for s in self.sems:
            self.nc.gpsimd.sem_clear(s)
        self.nc.all_engine_barrier()
        return self.ctx.__exit__(*a)

    def sem(self, name):
        s = self.ctx.enter_context(self.nc.semaphore(f"{self.name}_{name}"))
        self.sems.append(s)
        return s

    def sb(self, name, shape, dt=F32):
        if self.arena is not None:
            self.at, a = carve(self.arena, self.at, shape)
            return a
        return self.ctx.enter_context(self.nc.sbuf_tensor(f"{self.name}_{name}", shape, dt))

    def ps(self, name, shape, dt=F32):
        if self.banks is not None:
            n, a = carve(self.banks, self.bank, shape)
            self.bank = -(-n // 512) * 512
            return a
        return self.ctx.enter_context(self.nc.psum_tensor(f"{self.name}_{name}", shape, dt))

    def block(self):
        return self.blocks.enter_context(self.nc.Block())


ADA_STEP = 4
ADA_LATE = FT // 2 * ADA_STEP
ADA_EARLY = NA - ADA_LATE
assert ADA_EARLY >= 3 * KT and ADA_EARLY % ADA_STEP == 0


def finish_ada(dve, nc, sem, ada, sg, gains, s, n):
    scale = ada[:, (3 * s + 1) * KT:(3 * s + 2) * KT]
    gate = ada[:, (3 * s + 2) * KT:(3 * s + 3) * KT]
    if s != 1:
        nc.vector.tensor_scalar(gate, gate, 0.5, None, ALU.mult).then_inc(sem, 1)
        n += 1
    nc.vector.tensor_scalar(sg[:, s], scale, 1.0, None, ALU.add).then_inc(sem, 1)
    n += 1
    dve.wait_ge(sem, n)
    nc.vector.tensor_tensor(sg[:, s], sg[:, s], gains[:, s].unsqueeze(2).to_broadcast([P, KT, NCOND]), ALU.mult).then_inc(sem, 1)
    n += 1
    dve.wait_ge(sem, n)
    return n


def first_norm(nc, d, x, h, ones, ident, c, b_ada, gains, ada, sg):
    ROUNDS = ADA_EARLY // ADA_STEP
    with Phase(nc, "n1") as ph:
        w = ph.sb("w", [P, 2, ADA_STEP, KT, P])
        sq = ph.sb("sq", [P, 2, TOK])
        rstd = ph.sb("rstd", [P, TOK])
        smp = ph.sb("smp", [P, KT, NB])
        eps = ph.sb("eps", [P, 1])
        ps = ph.ps("ps", [P, NCH, 512])
        pa = [ph.ps(f"pa{q}", [P, ADA_STEP, NCOND]) for q in range(2)]
        w_in = [ph.sem(f"w_in{q}") for q in range(2)]
        x_in = [ph.sem(f"x_in{k}") for k in range(KT)]
        c_in, c_act, mm, evac, fix, ones_set, squared, summed, root, inv, scaled, modded, smp_mod, eps_set = (
            ph.sem(n) for n in ("c_in", "c_act", "mm", "evac", "fix", "ones_set", "squared", "summed", "root", "inv", "scaled",
                                "modded", "smp_mod", "eps_set"))
        block = ph.block()

        def load(sp, r):
            src = d["w_ada"][r * ADA_STEP:(r + 1) * ADA_STEP].rearrange("t p k m -> p t k m")
            sp.dma_start(w[:, r % 2].rearrange("p t k m -> p t (k m)"), src.rearrange("p t k m -> p t (k m)")).then_inc(w_in[r % 2], 16)

        @block.sync
        def _(sp):
            for k in range(KT):
                sp.dma_start(x[:, k], d["x"][:, k]).then_inc(x_in[k], 16)
            for r in range(ROUNDS):
                if r >= 2:
                    sp.wait_ge(mm, r - 1)
                load(sp, r)

        @block.gpsimd
        def _(pool):
            nc.gpsimd.memset(ones[:], 1.0).then_inc(ones_set, 1)

        @block.scalar
        def _(act):
            act.dma_start(c[:], d["c"]).then_inc(c_in, 16)
            act.dma_start(b_ada[:], d["b_ada"]).then_inc(c_in, 16)
            act.dma_start(gains[:], d["gains"]).then_inc(c_in, 16)
            act.dma_start(ident[:], d["ident"]).then_inc(c_in, 16)
            act.wait_ge(c_in, 64)
            nc.scalar.activation(c[:], c[:], ACT.Silu).then_inc(c_act, 1)
            for k in range(KT):
                act.wait_ge(x_in[k], 16)
                if k >= 2:
                    act.wait_ge(summed, k - 1)
                nc.scalar.activation(sq[:, k % 2], x[:, k], ACT.Square).then_inc(squared, 1)
            act.wait_ge(summed, KT)
            act.wait_ge(eps_set, 1)
            nc.scalar.activation(rstd[:].rearrange("p (n c) -> p n c", n=NCH), ps[:, :, 0:NC], ACT.Sqrt,
                                 scale=1.0 / DM, bias=eps[:]).then_inc(root, 1)
            act.wait_ge(fix, 4)
            for k in range(KT):
                act.wait_ge(scaled, k + 1)
                nc.scalar.activation(h[:, k, 0:SEQ], h[:, k, 0:SEQ], ACT.Identity,
                                     scale=sg[:, 0, k, 0:1], bias=ada[:, k, 0:1]).then_inc(modded, 1)
            act.wait_ge(modded, KT)

        @block.tensor
        def _(pe):
            pe.wait_ge(ones_set, 1)
            for k in range(KT):
                pe.wait_ge(squared, k + 1)
                for n in range(NCH):
                    m = nc.tensor.matmul(ps[:, n, 0:NC], ones[:], sq[:, k % 2, n * NC:(n + 1) * NC],
                                         start=k == 0, stop=k == KT - 1)
                m.then_inc(summed, 1)
            pe.wait_ge(c_act, 1)
            for r in range(ROUNDS):
                pe.wait_ge(w_in[r % 2], 16 * (r // 2 + 1))
                if r >= 2:
                    pe.wait_ge(evac, r - 1)
                for t in range(ADA_STEP):
                    for k in range(KT):
                        m = nc.tensor.matmul(pa[r % 2][:, t], w[:, r % 2, t, k], c[:, k], start=k == 0, stop=k == KT - 1)
                m.then_inc(mm, 1)

        @block.vector
        def _(dve):
            nc.vector.memset(eps[:], EPS).then_inc(eps_set, 1)
            dve.wait_ge(root, 1)
            nc.vector.reciprocal(rstd[:], rstd[:]).then_inc(inv, 1)
            dve.wait_ge(inv, 1)
            for k in range(KT):
                nc.vector.tensor_tensor(h[:, k], x[:, k], rstd[:], ALU.mult).then_inc(scaled, 1)
            dve.wait_ge(c_in, 64)
            for r in range(ROUNDS):
                dve.wait_ge(mm, r + 1)
                at = slice(r * ADA_STEP, (r + 1) * ADA_STEP)
                nc.vector.tensor_tensor(ada[:, at], pa[r % 2][:], b_ada[:, at].unsqueeze(2).to_broadcast([P, ADA_STEP, NCOND]),
                                        ALU.add).then_inc(evac, 1)
            dve.wait_ge(evac, ROUNDS)
            n = finish_ada(dve, nc, fix, ada, sg, gains, 0, 0)
            dve.sem_inc(fix, 1)
            dve.wait_ge(scaled, KT)
            nc.vector.tensor_tensor(smp[:], h[:, :, SEQ:TOK], sg[:, 0, :, 1:NCOND], ALU.mult).then_inc(smp_mod, 1)
            dve.wait_ge(smp_mod, 1)
            nc.vector.tensor_tensor(h[:, :, SEQ:TOK], smp[:], ada[:, 0:KT, 1:NCOND], ALU.add).then_inc(smp_mod, 1)
            dve.wait_ge(smp_mod, 2)


def norm_mod(nc, name, x, h, ones, ada, sg, s, load=None, store=None):
    with Phase(nc, name) as ph:
        sq = ph.sb("sq", [P, 2, TOK])
        rstd = ph.sb("rstd", [P, TOK])
        smp = ph.sb("smp", [P, KT, NB])
        eps = ph.sb("eps", [P, 1])
        ps = ph.ps("ps", [P, NCH, 512])
        x_in = [ph.sem(f"x_in{k}") for k in range(KT)] if load is not None else None
        squared, summed, root, inv, scaled, modded, smp_mod, eps_set, saved = (
            ph.sem(n) for n in ("squared", "summed", "root", "inv", "scaled", "modded", "smp_mod", "eps_set", "saved"))
        block = ph.block()

        @block.sync
        def _(sp):
            if load is not None:
                for k in range(KT):
                    sp.dma_start(x[:, k], load[:, k]).then_inc(x_in[k], 16)
            if store is not None:
                sp.dma_start(store, x[:]).then_inc(saved, 16)
                sp.wait_ge(saved, 16)

        @block.scalar
        def _(act):
            for k in range(KT):
                if load is not None:
                    act.wait_ge(x_in[k], 16)
                if k >= 2:
                    act.wait_ge(summed, k - 1)
                nc.scalar.activation(sq[:, k % 2], x[:, k], ACT.Square).then_inc(squared, 1)
            act.wait_ge(summed, KT)
            act.wait_ge(eps_set, 1)
            nc.scalar.activation(rstd[:].rearrange("p (n c) -> p n c", n=NCH), ps[:, :, 0:NC], ACT.Sqrt,
                                 scale=1.0 / DM, bias=eps[:]).then_inc(root, 1)
            for k in range(KT):
                act.wait_ge(scaled, k + 1)
                nc.scalar.activation(h[:, k, 0:SEQ], h[:, k, 0:SEQ], ACT.Identity,
                                     scale=sg[:, s, k, 0:1], bias=ada[:, 3 * s * KT + k, 0:1]).then_inc(modded, 1)
            act.wait_ge(modded, KT)

        @block.tensor
        def _(pe):
            for k in range(KT):
                pe.wait_ge(squared, k + 1)
                for n in range(NCH):
                    m = nc.tensor.matmul(ps[:, n, 0:NC], ones[:], sq[:, k % 2, n * NC:(n + 1) * NC],
                                         start=k == 0, stop=k == KT - 1)
                m.then_inc(summed, 1)

        @block.vector
        def _(dve):
            nc.vector.memset(eps[:], EPS).then_inc(eps_set, 1)
            dve.wait_ge(root, 1)
            nc.vector.reciprocal(rstd[:], rstd[:]).then_inc(inv, 1)
            dve.wait_ge(inv, 1)
            for k in range(KT):
                nc.vector.tensor_tensor(h[:, k], x[:, k], rstd[:], ALU.mult).then_inc(scaled, 1)
            dve.wait_ge(scaled, KT)
            nc.vector.tensor_tensor(smp[:], h[:, :, SEQ:TOK], sg[:, s, :, 1:NCOND], ALU.mult).then_inc(smp_mod, 1)
            dve.wait_ge(smp_mod, 1)
            nc.vector.tensor_tensor(h[:, :, SEQ:TOK], smp[:], ada[:, 3 * s * KT:(3 * s + 1) * KT, 1:NCOND],
                                    ALU.add).then_inc(smp_mod, 1)
            dve.wait_ge(smp_mod, 2)


def ffn(nc, name, w_in_d, w_out_d, x, h, ada, s, late=None):
    with Phase(nc, name) as ph:
        a = ph.sb("a", [P, FT, TOK])
        w = ph.sb("w", [P, 2, 2 * KT * P])
        wo = ph.sb("wo", [P, 2, FT // 2, P])
        g = ph.sb("g", [P, NCH, NC])
        smp = ph.sb("smp", [P, 2, NB])
        ps = [ph.ps(f"ps{n}", [P, 2, 512]) for n in range(NCH)]
        w_in = [ph.sem(f"w_in{q}") for q in range(2)]
        wo_in = [ph.sem(f"wo_in{q}") for q in range(2)]
        mm, silued, acted, wo_used, mo, added, smped, smpadd = (
            ph.sem(n) for n in ("mm", "silued", "acted", "wo_used", "mo", "added", "smped", "smpadd"))
        wv = w[:].rearrange("p q (u k m) -> p q u k m", u=2, k=KT)
        if late is not None:
            wa = ph.sb("wa", [P, ADA_STEP, KT, P])
            pa = ph.ps("pa", [P, ADA_STEP, NCOND])
            wa_in, ma, evac, fix = (ph.sem(n) for n in ("wa_in", "ma", "evac", "fix"))
        block = ph.block()
        HK = FT // 2
        if late is not None:
            d, c, b_ada, gains, sg = late

        def load_ada(sp, i):
            at = bass.ds(ADA_EARLY + ADA_STEP * i, ADA_STEP)
            sp.dma_start(wa[:].rearrange("p t k m -> p t (k m)"), d["w_ada"][at].rearrange("t p k m -> p t (k m)")).then_inc(wa_in, 16)

        @block.sync
        def _(sp):
            if late is not None:
                load_ada(sp, 0)
            for q in range(2):
                sp.dma_start(w[:, q], w_in_d[q]).then_inc(w_in[q], 16)
            for q in range(2):
                sp.dma_start(wo[:, q], w_out_d[q]).then_inc(wo_in[q], 16)
            with sp.Fori(1, FT // 2) as i:
                for q in range(2):
                    sp.wait_ge(mm, NCH * (2 * (i - 1) + q + 1))
                    sp.dma_start(w[:, q], w_in_d[2 * i + q]).then_inc(w_in[q], 16)
                if late is not None:
                    sp.wait_ge(ma, i)
                    load_ada(sp, i)
            with sp.Fori(1, KT) as i:
                for q in range(2):
                    sp.wait_ge(wo_used, 2 * (i - 1) + q + 1)
                    sp.dma_start(wo[:, q], w_out_d[2 * i + q]).then_inc(wo_in[q], 16)

        @block.tensor
        def _(pe):
            with pe.Fori(0, FT // 2) as i:
                for q in range(2):
                    pe.wait_ge(w_in[q], 16 * (i + 1))
                    for n in range(NCH):
                        pe.wait_ge(acted, 2 * NCH * i + (n + 1 if q else 0))
                        for u in range(2):
                            for k in range(KT):
                                m = nc.tensor.matmul(ps[n][:, u, 0:NC], wv[:, q, u, k], h[:, k, n * NC:(n + 1) * NC],
                                                     start=k == 0, stop=k == KT - 1)
                        m.then_inc(mm, 1)
                if late is not None:
                    pe.wait_ge(wa_in, 16 * (i + 1))
                    pe.wait_ge(evac, i)
                    for t in range(ADA_STEP):
                        for k in range(KT):
                            m = nc.tensor.matmul(pa[:, t], wa[:, t, k], c[:, k], start=k == 0, stop=k == KT - 1)
                    m.then_inc(ma, 1)
            pe.wait_ge(acted, FT * NCH)
            with pe.Fori(0, KT // 2) as i:
                for q in range(2):
                    pe.wait_ge(added, 2 * i)
                    for hf in range(2):
                        pe.wait_ge(wo_in[hf], 32 * i + 16 * (q + 1))
                        for n in range(NCH):
                            for k in range(HK):
                                m = nc.tensor.matmul(ps[n][:, q, 0:NC], wo[:, hf, k], a[:, hf * HK + k, n * NC:(n + 1) * NC],
                                                     start=hf == 0 and k == 0, stop=hf == 1 and k == HK - 1)
                        m.then_inc(wo_used, 1)

        @block.scalar
        def _(act):
            with act.Fori(0, FT) as i:
                for n in range(NCH):
                    act.wait_ge(mm, NCH * i + n + 1)
                    act.wait_ge(acted, NCH * i)
                    nc.scalar.activation(g[:, n], ps[n][:, 0, 0:NC], ACT.Silu).then_inc(silued, 1)

        @block.vector
        def _(dve):
            with dve.Fori(0, FT // 2) as i:
                for q in range(2):
                    for n in range(NCH):
                        dve.wait_ge(silued, NCH * (2 * i + q) + n + 1)
                        nc.vector.tensor_tensor(a[:, 2 * i + q, n * NC:(n + 1) * NC], g[:, n], ps[n][:, 1, 0:NC],
                                                ALU.mult).then_inc(acted, 1)
                if late is not None:
                    dve.wait_ge(ma, i + 1)
                    at = bass.ds(ADA_EARLY + ADA_STEP * i, ADA_STEP)
                    nc.vector.tensor_tensor(ada[:, at], pa[:], b_ada[:, at].unsqueeze(2).to_broadcast([P, ADA_STEP, NCOND]),
                                            ALU.add).then_inc(evac, 1)
            if late is not None:
                dve.wait_ge(evac, FT // 2)
                n = finish_ada(dve, nc, fix, ada, sg, gains, 1, 0)
                finish_ada(dve, nc, fix, ada, sg, gains, 2, n)
            gate = (3 * s + 2) * KT
            with dve.Fori(0, KT // 2) as i:
                for q in range(2):
                    t = 2 * i + q
                    dve.wait_ge(wo_used, 4 * i + 2 * q + 2)
                    nc.vector.tensor_tensor(smp[:, q], ps[2][:, q, LASTP:NC], ada[:, gate + t, 1:NCOND],
                                            ALU.mult).then_inc(smped, 1)
                    for n in range(NCH):
                        c = NC if n < NCH - 1 else LASTP
                        v = nc.vector.scalar_tensor_tensor(
                            out=x[:, t, n * NC:n * NC + c], in0=ps[n][:, q, 0:c], scalar=ada[:, bass.ds(gate + t, 1), 0:1].rearrange("p a b -> p (a b)"),
                            in1=x[:, t, n * NC:n * NC + c], op0=ALU.mult, op1=ALU.add)
                    dve.wait_ge(smped, 2 * i + q + 1)
                    nc.vector.tensor_tensor(x[:, t, SEQ:TOK], x[:, t, SEQ:TOK], smp[:, q], ALU.add).then_inc(added, 1)
            dve.wait_ge(added, KT)


def load_tiles(eng, slots, w_in, used, per, src, n):
    for q in range(2):
        eng.dma_start(slots[:, q], src[q]).then_inc(w_in[q], 16)
    with eng.Fori(1, n // 2) as i:
        for q in range(2):
            eng.wait_ge(used, per * (2 * (i - 1) + q + 1))
            eng.dma_start(slots[:, q], src[2 * i + q]).then_inc(w_in[q], 16)
    if n % 2:
        eng.wait_ge(used, per * (n - 2))
        eng.dma_start(slots[:, 0], src[n - 1]).then_inc(w_in[0], 16)


def project_tiles(pe, nc, slots, ps, rhs, w_in, mm, read, n, kt=KT):
    def tile(i, q):
        pe.wait_ge(w_in[q], 16 * (i + 1))
        for c in range(NCH):
            if c == 0:
                pe.wait_ge(read[q], NCH * i)
            for k in range(kt):
                m = nc.tensor.matmul(ps[q][:, c, 0:NC], slots[:, q, k], rhs[:, k, c * NC:(c + 1) * NC],
                                     start=k == 0, stop=k == kt - 1)
            m.then_inc(mm, 1)

    with pe.Fori(0, n // 2) as i:
        for q in range(2):
            tile(i, q)
    if n % 2:
        tile(n // 2, 0)


def copy_tiles(act, nc, dst, ps, mm, read, n, before=0, func=ACT.Copy):
    def tile(i, q):
        for c in range(NCH):
            act.wait_ge(mm, NCH * (2 * i + q + before) + c + 1)
            nc.scalar.activation(dst[:, 2 * i + q, c * NC:(c + 1) * NC], ps[q][:, c, 0:NC], func).then_inc(read[q], 1)

    with act.Fori(0, n // 2) as i:
        for q in range(2):
            tile(i, q)
    if n % 2:
        tile(n // 2, 0)


def project_attention(nc, d, o, scr, paged, h, pj, tok):
    with Phase(nc, "pja") as ph:
        w = ph.sb("w", [P, 2, KT, P])
        wt = ph.sb("wt", [P, KT, VW])
        ps = [ph.ps(f"ps{q}", [P, NCH, 512]) for q in range(2)]
        pt = ph.ps("pt", [P, 2, 512])
        tab = ph.sb("tab", [P, 2], I32)
        tabf = ph.sb("tabf", [P, 2])
        rows = ph.sb("rows", [P, 2, 2], U32)
        pages = ph.sb("pages", [P, 2, ID * PAGE // 2])
        tab_in, tabbed = ph.sem("tab_in"), ph.sem("tabbed")
        w_in = [ph.sem(f"w_in{q}") for q in range(2)]
        read = [ph.sem(f"read{q}") for q in range(2)]
        mm, wt_in, tmm, tread, saved, qk_saved = (ph.sem(n) for n in ("mm", "wt_in", "tmm", "tread", "saved", "qk_saved"))
        block = ph.block()

        @block.sync
        def _(sp):
            with nc.allow_non_contiguous_dma(reason="256 page numbers"):
                sp.dma_start(tab[:], d["page_table"].rearrange("o (c p) -> p (o c)", c=2)).then_inc(tab_in, 16)
            sp.dma_start(wt[:], d["w_tok"]).then_inc(wt_in, 16)
            load_tiles(sp, w, w_in, mm, NCH, d["w_att"], AT)
            sp.wait_ge(read[0], NCH * (AT - AT // 2))
            sp.wait_ge(read[1], NCH * (AT // 2))
            sp.wait_ge(tread, TB + 1)
            sp.dma_start(o["k"], pj[:, KT0:KT0 + 2]).then_inc(saved, 16)
            sp.dma_start(o["kidx"], pj[0:ID, KI0]).then_inc(saved, 16)
            sp.dma_start(o["v_p"], tok[:, 0:TB, 0:NKV * HD]).then_inc(saved, 16)
            sp.dma_start(o["v_s"], tok[0:NB, TB, 0:NKV * HD]).then_inc(saved, 16)
            sp.wait_ge(saved, 64)

        @block.gpsimd
        def _(pool):
            pool.wait_ge(tabbed, 5)
            n = 0
            for f in range(2):
                for c in range(2):
                    if n >= 2:
                        pool.wait_ge(paged, 16 * (2 * n - 2))
                    pool.indirect_dma_start(pages[:, c], None, d["cache_kidx"], bass.IndirectOffsetOnAxis(rows[:, f, c:c + 1], 0)).then_inc(paged, 16)
                    n += 1
                    pool.wait_ge(paged, 16 * (2 * n - 1))
                    pool.dma_start(scr["kidx"][c * P:(c + 1) * P, f], pages[:, c]).then_inc(paged, 16)
            pool.wait_ge(paged, 16 * 2 * n)

        @block.tensor
        def _(pe):
            project_tiles(pe, nc, w, ps, h, w_in, mm, read, AT)
            pe.wait_ge(wt_in, 16)
            for t in range(TB + 1):
                rows = P if t < TB else NB
                if t >= 2:
                    pe.wait_ge(tread, t - 1)
                for k in range(KT):
                    m = nc.tensor.matmul(pt[0:rows, t % 2, 0:VW], h[:, k, t * P:t * P + rows], wt[:, k],
                                         start=k == 0, stop=k == KT - 1)
                m.then_inc(tmm, 1)

        @block.scalar
        def _(act):
            copy_tiles(act, nc, pj, ps, mm, read, AT)
            act.wait_ge(read[0], NCH * (AT - AT // 2))
            act.wait_ge(read[1], NCH * (AT // 2))
            act.dma_start(scr["qk"], pj[:, 0:QI0]).then_inc(qk_saved, 16)
            act.wait_ge(qk_saved, 16)

        @block.vector
        def _(dve):
            dve.wait_ge(tab_in, 16)
            nc.vector.tensor_copy(tabf[:], tab[:]).then_inc(tabbed, 1)
            for f in range(2):
                dve.wait_ge(tabbed, 1 + 2 * f)
                nc.vector.tensor_scalar(tabf[:], tabf[:], 2.0 if f == 0 else 1.0, 0.0 if f == 0 else 1.0, ALU.mult, ALU.add).then_inc(tabbed, 1)
                dve.wait_ge(tabbed, 2 + 2 * f)
                nc.vector.tensor_copy(rows[:, f], tabf[:]).then_inc(tabbed, 1)
            for t in range(TB + 1):
                rows_t = P if t < TB else NB
                dve.wait_ge(tmm, t + 1)
                nc.vector.tensor_copy(tok[0:rows_t, t], pt[0:rows_t, t % 2, 0:VW]).then_inc(tread, 1)


def mask_at(b):
    return P * (b * (b + 1) // 2)


FIRST = TOPK // P
CHOSEN = range(FIRST, TB)


def index_scores(nc, d, scr, pj, tok, ones, ident, mask):
    with Phase(nc, "sel") as ph:
        r = ph.sb("r", [P, 2, SEQ])
        wis = ph.sb("wis", [P, TB, NIH])
        ps = ph.ps("ps", [P, 2, SEQ])
        mm, relu, acc, zeroed, causal, scored, masked, free = (
            ph.sem(n) for n in ("mm", "relu", "acc", "zeroed", "causal", "scored", "masked", "free"))
        kx = ph.sb("kx", [ID, 2, NPAGE, PAGE])
        qx = ph.sb("qx", [ID, NIH, NB])
        hot = ph.sb("hot", [P, 2])
        prod = ph.sb("prod", [P, 4, NB])
        wid = ph.sb("wid", [NB, NB, NIH])
        wib = ph.sb("wib", [P, NB, NIH])
        t = ph.sb("t", [P, NPAGE, NIH])
        tn = ph.sb("tn", [NB, NIH])
        snew = ph.sb("snew", [NB, 1])
        sc = ph.sb("sc", [P, NB, NPAGE])
        st = ph.sb("st", [P, 2, P])
        pW = ph.ps("pW", [P, 512])
        pS = [ph.ps(f"pS{q}", [P, 512]) for q in range(2)]
        k_in = [ph.sem(f"k_in{q}") for q in range(2)]
        small, prodd, widd, smm, tmp, summed, ch_s, turned, moved, stored, newd = (
            ph.sem(n) for n in ("small", "prodd", "widd", "smm", "tmp", "summed", "ch", "turned", "moved", "stored", "newd"))
        block = ph.block()
        SC = float((NIH * ID) ** -0.5)
        pN = pW[0:NB, NB * NIH:NB * NIH + NIH]
        pT = pW[:, 0:2 * P].rearrange("p (c s) -> p c s", c=2)
        pSv = [p[:, 0:NPAGE * NIH].rearrange("p (i h) -> p i h", i=NPAGE) for p in pS]

        @block.sync
        def _(sp):
            sp.dma_start(hot[:], d["half"]).then_inc(small, 16)
            for u in range(2):
                sp.dma_start(qx[:].rearrange("p (t u) b -> p u t b", u=2)[:, u],
                             pj[u * ID:(u + 1) * ID, QI0:QI0 + 4, SEQ:TOK]).then_inc(small, 16)
            sp.wait_ge(small, 48)
            for b in range(NB):
                if b >= 2:
                    sp.wait_ge(smm, b - 1)
                src = scr["kidx"][b * NPAGE:(b + 1) * NPAGE].rearrange("i f (d s) -> (f d) i s", s=PAGE)
                sp.dma_start(kx[:, b % 2], src).then_inc(k_in[b % 2], 16)
            sp.wait_ge(moved, 1)
            sp.dma_start(by_page(scr["score"]), st[:]).then_inc(stored, 16)
            sp.dma_start(scr["snew"], snew[:]).then_inc(stored, 16)
            sp.wait_ge(stored, 32)

        @block.tensor
        def _(pe):
            pe.wait_ge(small, 48)
            pe.wait_ge(prodd, 1)
            for u in range(4):
                m = nc.tensor.matmul(pN[:, 2 * u:2 * u + 2], prod[:, u], hot[:], start=True, stop=True)
            pe.wait_ge(widd, 1)
            nc.tensor.matmul(pW[:, 0:NB * NIH], ones[0:NB, :], wid[:].rearrange("p b h -> p (b h)"),
                             start=True, stop=True).then_inc(newd, 1)

            def sample(b):
                pe.wait_ge(k_in[b % 2], 16 * (b // 2 + 1))
                if b >= 2:
                    pe.wait_ge(tmp, b - 1)
                for i in range(NPAGE):
                    m = nc.tensor.matmul(pSv[b % 2][:, i], kx[:, b % 2, i], qx[:, :, b], start=True, stop=True)
                m.then_inc(smm, 1)

            n = 0
            for i, b in enumerate(CHOSEN):
                for hd in range(NIH):
                    lo = 64 * (hd % 2)
                    if n >= 2:
                        pe.wait_ge(relu, n - 1)
                    for c in range(0, (b + 1) * P, 512):
                        e = min(c + 512, (b + 1) * P)
                        m = nc.tensor.matmul(ps[:, n % 2, c:e], pj[lo:lo + ID, QI0 + hd // 2, b * P:(b + 1) * P],
                                             pj[lo:lo + ID, KI0, c:e], start=True, stop=True)
                    m.then_inc(mm, 1)
                    n += 1
                sample(i)
            for b in range(len(CHOSEN), NB):
                sample(b)
            pe.wait_ge(summed, NB)
            for c in range(2):
                m = nc.tensor.transpose(pT[:, c], sc[:, 4 * c:4 * c + 4].rearrange("p b i -> p (b i)"), ident[:])
            m.then_inc(turned, 1)

        @block.scalar
        def _(act):
            n = 0
            for b in CHOSEN:
                for hd in range(NIH):
                    act.wait_ge(mm, n + 1)
                    if n >= 2:
                        act.wait_ge(acc, n - 1)
                    nc.scalar.activation(r[:, n % 2, 0:(b + 1) * P], ps[:, n % 2, 0:(b + 1) * P], ACT.Relu).then_inc(relu, 1)
                    n += 1

        @block.gpsimd
        def _(pool):
            nc.gpsimd.memset(mask[:, 0:mask_at(FIRST)], 0.0).then_inc(zeroed, 1)
            pool.wait_ge(zeroed, 1)
            for b in range(FIRST):
                part = mask[:, mask_at(b) + b * P:mask_at(b + 1)]
                nc.gpsimd.affine_select(out=part, in_=part, compare_op=ALU.is_ge, fill=-BIG, base=0,
                                        pattern=[[-1, P]], channel_multiplier=1).then_inc(masked, 1)
            for i, b in enumerate(CHOSEN):
                pool.wait_ge(scored, i + 1)
                part = mask[:, mask_at(b) + b * P:mask_at(b + 1)]
                nc.gpsimd.affine_select(out=part, in_=part, compare_op=ALU.is_ge, fill=CAUSAL, base=0,
                                        pattern=[[-1, P]], channel_multiplier=1).then_inc(causal, 1)

        @block.vector
        def _(dve):
            ch = Chain(dve, ch_s)
            nc.vector.tensor_scalar(wis[:], tok[:, 0:TB, NKV * HD:NKV * HD + NIH], SC, None, ALU.mult).then_inc(free, 1)
            nc.vector.tensor_tensor(prod[:], pj[:, QI0:QI0 + 4, SEQ:TOK],
                                    pj[:, KI0, SEQ:TOK].unsqueeze(1).to_broadcast([P, 4, NB]), ALU.mult).then_inc(prodd, 1)
            wi = tok[0:NB, TB, NKV * HD:NKV * HD + NIH]
            nc.vector.scalar_tensor_tensor(out=wid[:], in0=wi.unsqueeze(1).to_broadcast([NB, NB, NIH]), scalar=SC,
                                           in1=ident[0:NB, 0:NB].unsqueeze(2).to_broadcast([NB, NB, NIH]),
                                           op0=ALU.mult, op1=ALU.mult).then_inc(widd, 1)
            dve.wait_ge(small, 48)
            dve.wait_ge(newd, 1)
            ch.link(nc.vector.tensor_copy(wib[:].rearrange("p b h -> p (b h)"), pW[:, 0:NB * NIH]))
            ch.link(nc.vector.scalar_tensor_tensor(out=tn[:], in0=pN, scalar=0.0, in1=wi, op0=ALU.max, op1=ALU.mult))
            ch.link(nc.vector.tensor_reduce(snew[:], tn[:], AX, ALU.add))
            ch.link(nc.vector.tensor_scalar(snew[:], snew[:], SC, None, ALU.mult))
            dve.wait_ge(free, 1)

            def sample(b):
                dve.wait_ge(smm, b + 1)
                if b:
                    dve.wait_ge(summed, b)
                nc.vector.scalar_tensor_tensor(out=t[:], in0=pSv[b % 2], scalar=0.0,
                                               in1=wib[:, b].unsqueeze(1).to_broadcast([P, NPAGE, NIH]),
                                               op0=ALU.max, op1=ALU.mult).then_inc(tmp, 1)
                dve.wait_ge(tmp, b + 1)
                nc.vector.tensor_reduce(sc[:, b], t[:], AX, ALU.add).then_inc(summed, 1)

            n = 0
            for i, b in enumerate(CHOSEN):
                s = mask[:, mask_at(b):mask_at(b + 1)]
                for hd in range(NIH):
                    dve.wait_ge(relu, n + 1)
                    if hd == 0:
                        v = nc.vector.tensor_scalar(s, r[:, n % 2, 0:(b + 1) * P], wis[:, b, 0:1], None, ALU.mult)
                    else:
                        dve.wait_ge(acc, n)
                        v = nc.vector.scalar_tensor_tensor(out=s, in0=r[:, n % 2, 0:(b + 1) * P], scalar=wis[:, b, hd:hd + 1],
                                                           in1=s, op0=ALU.mult, op1=ALU.add)
                    v.then_inc(acc, 1)
                    n += 1
                dve.wait_ge(acc, n)
                dve.sem_inc(scored, 1)
                sample(i)
            for b in range(len(CHOSEN), NB):
                sample(b)
            dve.wait_ge(turned, 1)
            nc.vector.tensor_copy(st[:], pT[:]).then_inc(moved, 1)


ROUNDS = TOPK // 8
SHARE = ROUNDS // SG
PROMPT_ROUNDS = SHARE - KT // 2


def top_round(dve, nc, rows, m8, found, tick, before):
    dve.wait_ge(found, before)
    dve.sem_inc(tick, 1)
    for i, s in enumerate(rows):
        nc.vector.max(m8[0:s.shape[0], i], s).then_inc(found, 1)
    dve.wait_ge(found, before + len(rows))
    dve.sem_inc(tick, 1)
    for i, s in enumerate(rows):
        nc.vector.match_replace(s, m8[0:s.shape[0], i], s, TAKEN).then_inc(found, 1)


def top_rounds(dve, nc, rows, m8, found, tick, before, rounds):
    with dve.Fori(0, rounds) as j:
        top_round(dve, nc, rows, m8, found, tick, before + 2 * len(rows) * j)
    return before + 2 * len(rows) * rounds


def chosen_rows(mask):
    return [mask[:, mask_at(b):mask_at(b + 1)] for b in CHOSEN]


def attend(nc, scr, pj, tok, mask, bias, ident, att):
    with Phase(nc, "att") as ph:
        q = ph.sb("q", [P, 2, P])
        L = ph.sb("L", [P, 2, 2, SEQ])
        ET = ph.sb("ET", [P, 2, SEQ])
        nm = ph.sb("nm", [P, 2, 2])
        den = ph.sb("den", [P, 2, 2])
        rd = ph.sb("rd", [P, 2])
        pair = ph.sb("pair", [P, P])
        pS = ph.ps("pS", [P, 2, SEQ])
        pT = ph.ps("pT", [P, 2, 512])
        pO = ph.ps("pO", [P, 2, 512])
        staged, mm, logit, rmax, exped, trans, copied, pv, scaled, recip, turned, done = (
            ph.sem(n) for n in ("staged", "mm", "logit", "rmax", "exped", "trans", "copied", "pv", "scaled", "recip",
                                "turned", "done"))
        k_in = ph.sem("k_in")
        q_in = [ph.sem(f"q_in{b}") for b in range(TB)]
        block = ph.block()
        PAIRS = NH // 2
        G = NH // NKV

        @block.sync
        def _(sp):
            sp.dma_start(pj[:, KT0:KT0 + 2], scr["qk"][:, KT0:KT0 + 2]).then_inc(k_in, 16)
            for b in range(TB):
                e = (b + 1) * P if b < TB - 1 else TOK
                sp.dma_start(pj[:, QT0:QT0 + 8, b * P:e], scr["qk"][:, QT0:QT0 + 8, b * P:e]).then_inc(q_in[b], 16)

        PC = 4

        def pieces(b):
            return [(u, c, min(c + PC, b + 1)) for u in range(2) for c in range(0, b + 1, PC)]

        def before(b):
            return sum(PAIRS * len(pieces(a)) for a in range(b))

        def loops(eng, body):
            for b in range(TB):
                with eng.Fori(0, G - 1) as g:
                    for m in range(2):
                        body(b * PAIRS + 2 * g + m, b, m, g, (b, g + 1))
                for m in range(2):
                    body(b * PAIRS + 2 * (G - 1) + m, b, m, G - 1, (b + 1, 0) if b + 1 < TB else None)

        @block.gpsimd
        def _(pool):
            def stage(b, m, g):
                pool.wait_ge(q_in[b], 16)
                nc.gpsimd.tensor_copy(q[:, m], pj[:, QT0 + m * G + g, b * P:(b + 1) * P]).then_inc(staged, 1)

            def body(t, b, m, g, nxt):
                if nxt is not None:
                    pool.wait_ge(mm, 2 * t + 2)
                    stage(nxt[0], m, nxt[1])

            stage(0, 0, 0)
            stage(0, 1, 0)
            loops(pool, body)

        @block.tensor
        def _(pe):
            def logits(t, b, m):
                W = (b + 1) * P
                pe.wait_ge(staged, t + 1)
                for u in range(2):
                    if isinstance(t, int) and t == 0:
                        pass
                    else:
                        pe.wait_ge(logit, 4 * (t - 1) + 2 * u + 1)
                    for c in range(0, W, 512):
                        e = min(c + 512, W)
                        x = nc.tensor.matmul(pS[:, u, c:e], q[64 * u:64 * u + 64, m],
                                             pj[64 * u:64 * u + 64, KT0 + m, c:e], start=True, stop=True)
                    x.then_inc(mm, 1)

            def body(t, b, m, g, nxt):
                ps = pieces(b)
                first = before(b) + len(ps) * (2 * g + m)

                def turn(i):
                    u, c0, c1 = ps[i]
                    pe.wait_ge(exped, 2 * t + u + 1)
                    pe.wait_ge(copied, first + i)
                    for c in range(c0, c1):
                        x = nc.tensor.transpose(pT[:, i % 2, (c - c0) * P:(c - c0 + 1) * P], L[:, m, u, c * P:(c + 1) * P], ident[:])
                    x.then_inc(trans, 1)

                turn(0)
                turn(1)
                for i, (u, c0, c1) in enumerate(ps):
                    pe.wait_ge(copied, first + i + 2)
                    if i == 0:
                        pe.wait_ge(scaled, t)
                    for c in range(c0, c1):
                        x = nc.tensor.matmul(pO[:, 0, u * HD:(u + 1) * HD], ET[:, u, c * P:(c + 1) * P],
                                             tok[:, c, (2 * m + u) * HD:(2 * m + u + 1) * HD], start=c == 0, stop=c == b)
                    x.then_inc(pv, 1)
                    if i + 2 < len(ps):
                        turn(i + 2)
                if nxt is not None:
                    logits(t + 2, nxt[0], m)
                pe.wait_ge(scaled, t + 1)
                pe.wait_ge(done, t)
                nc.tensor.transpose(pO[:, 1, 0:P], pair[:], ident[:]).then_inc(turned, 1)

            pe.wait_ge(k_in, 16)
            logits(0, 0, 0)
            logits(1, 0, 1)
            loops(pe, body)

        @block.scalar
        def _(act):
            def exps(t, b, m):
                W = (b + 1) * P
                for u in range(2):
                    act.wait_ge(rmax, 2 * t + u + 1)
                    nc.scalar.activation(L[:, m, u, 0:W], L[:, m, u, 0:W], ACT.Exp, bias=nm[:, m, u:u + 1],
                                         accum_out=den[:, m, u:u + 1]).then_inc(exped, 1)

            def body(t, b, m, g, nxt):
                ps = pieces(b)
                first = before(b) + len(ps) * (2 * g + m)
                act.wait_ge(pv, first)
                for i, (u, c0, c1) in enumerate(ps):
                    act.wait_ge(trans, first + i + 1)
                    nc.scalar.activation(ET[:, u, c0 * P:c1 * P], pT[:, i % 2, 0:(c1 - c0) * P], ACT.Copy).then_inc(copied, 1)
                if m == 0:
                    exps(t + 1, b, 1)
                elif nxt is not None:
                    exps(t + 1, nxt[0], 0)
                act.wait_ge(turned, t + 1)
                nc.scalar.activation(att[:, m * G + g, b * P:(b + 1) * P], pO[:, 1, 0:P], ACT.Copy).then_inc(done, 1)

            act.sem_inc(copied, 1)
            exps(0, 0, 0)
            loops(act, body)

        @block.vector
        def _(dve):
            def logits(t, b, m, g):
                W = (b + 1) * P
                lo = max(W - WIN, 0)
                if isinstance(t, int):
                    r = t - b * PAIRS
                    if t >= 2:
                        dve.wait_ge(trans, before(b) + len(pieces(b)) * (r - 1) if r else before(b) - len(pieces(b - 1)))
                else:
                    dve.wait_ge(trans, before(b) + len(pieces(b)) * (2 * g + m - 1))
                for u in range(2):
                    dve.wait_ge(mm, 2 * t + u + 1)
                    l = L[:, m, u]
                    nc.vector.scalar_tensor_tensor(out=l[:, 0:W], in0=pS[:, u, 0:W], scalar=float(HD ** -0.5),
                                                   in1=mask[:, mask_at(b):mask_at(b + 1)], op0=ALU.mult,
                                                   op1=ALU.add).then_inc(logit, 1)
                    dve.wait_ge(logit, 4 * t + 2 * u + 1)
                    nc.vector.tensor_tensor(l[:, lo:W], l[:, lo:W], bias[:, 2 * (m * G + g) + u, WIN - (W - lo):WIN],
                                            ALU.add).then_inc(logit, 1)
                    dve.wait_ge(logit, 4 * t + 2 * u + 2)
                    nc.vector.tensor_reduce(nm[:, m, u:u + 1], l[:, 0:W], AX, ALU.max, negate=True).then_inc(rmax, 1)

            def body(t, b, m, g, nxt):
                if m == 0:
                    logits(t + 1, b, 1, g)
                elif nxt is not None:
                    logits(t + 1, nxt[0], 0, nxt[1])
                dve.wait_ge(turned, t)
                dve.wait_ge(exped, 2 * t + 2)
                nc.vector.reciprocal(rd[:], den[:, m]).then_inc(recip, 1)
                dve.wait_ge(recip, t + 1)
                dve.wait_ge(pv, before(b) + len(pieces(b)) * (2 * g + m + 1))
                nc.vector.tensor_tensor(pair[:].rearrange("p (u d) -> p u d", u=2),
                                        pO[:, 0, 0:2 * HD].rearrange("p (u d) -> p u d", u=2),
                                        rd[:].unsqueeze(2).to_broadcast([P, 2, HD]), ALU.mult).then_inc(scaled, 1)

            logits(0, 0, 0, 0)
            loops(dve, body)


def tables(nc, d, s, bias):
    with Phase(nc, "tab") as ph:
        hot = ph.sb("hot", [NBUCKET, 512])
        rb = ph.sb("rb", [NBUCKET, NH])
        byh = ph.sb("byh", [NH, 512])
        rows = ph.sb("rows", [P, 2, NH])
        flip = ph.sb("flip", [P, P])
        up = ph.sb("up", [P, NH, WIN])
        pf = ph.ps("pf", [P, 4, 2 * WIN])
        ps = ph.ps("ps", [P, 512])
        pr = ph.ps("pr", [P, 2, NH])
        flipped, loaded, mm, moved, sub, stored, back = (
            ph.sem(n) for n in ("flipped", "loaded", "mm", "moved", "sub", "stored", "back"))
        block = ph.block()

        @block.sync
        def _(sp):
            sp.dma_start(hot[:], d["hot"]).then_inc(loaded, 16)
            sp.dma_start(rb[:], d["rel_bias"]).then_inc(loaded, 16)
            sp.dma_start(flip[:], d["flip"]).then_inc(loaded, 16)
            sp.wait_ge(sub, 1)
            sp.dma_start(s["byh"], byh[:]).then_inc(stored, 16)
            sp.wait_ge(moved, 2)
            sp.dma_start(s["brow"].rearrange("(c p) h -> p c h", c=2), rows[:]).then_inc(stored, 16)
            sp.wait_ge(stored, 32)
            win = bass.AP(s["byh"].tensor, 0, [[1, P], [512, NH], [1, WIN]])
            sp.dma_start(up[:], win).then_inc(back, 16)
            sp.wait_ge(back, 16)

        @block.tensor
        def _(pe):
            pe.wait_ge(loaded, 48)
            nc.tensor.matmul(ps[0:NH, :], rb[:], hot[:], start=True, stop=True).then_inc(mm, 1)
            for c in range(2):
                nc.tensor.matmul(pr[:, c], hot[:, c * P:(c + 1) * P], rb[:], start=True, stop=True).then_inc(mm, 1)
            pe.wait_ge(back, 16)
            for n in range(NH // 2):
                if n >= 4:
                    pe.wait_ge(flipped, n - 3)
                nc.tensor.matmul(pf[:, n % 4], flip[:], up[:, 2 * n:2 * n + 2].rearrange("p h j -> p (h j)"),
                                 start=True, stop=True).then_inc(mm, 1)

        @block.vector
        def _(dve):
            dve.wait_ge(mm, 3)
            nc.vector.tensor_copy(byh[:], ps[0:NH, :]).then_inc(moved, 1)
            nc.vector.tensor_copy(rows[:], pr[:]).then_inc(moved, 1)
            dve.wait_ge(moved, 2)
            nc.vector.tensor_scalar(byh[:], byh[:], ps[0:NH, 0:1], None, ALU.subtract).then_inc(sub, 1)
            for n in range(NH // 2):
                dve.wait_ge(mm, 4 + n)
                nc.vector.tensor_copy(bias[:, 2 * n:2 * n + 2].rearrange("p h j -> p (h j)"), pf[:, n % 4]).then_inc(flipped, 1)


def attention_out(nc, d, scr, att, A):
    with Phase(nc, "ao") as ph:
        w = ph.sb("w", [P, 2, KT, P])
        g = ph.sb("g", [P, 2, NCH, NC])
        s = ph.sb("s", [P, 2, TOK])
        ps = [ph.ps(f"ps{q}", [P, NCH, 512]) for q in range(2)]
        w_in = [ph.sem(f"w_in{q}") for q in range(2)]
        read = [ph.sem(f"read{q}") for q in range(2)]
        g_in = [ph.sem(f"g_in{q}") for q in range(2)]
        mm, added = ph.sem("mm"), ph.sem("added")
        block = ph.block()

        @block.sync
        def _(sp):
            load_tiles(sp, w, w_in, mm, NCH, d["w_ao"], KT)

        @block.scalar
        def _(act):
            for t in range(KT):
                q = t % 2
                if t >= 2:
                    act.wait_ge(added, t - 1)
                act.dma_start(g[:, q].rearrange("p c n -> p (c n)"), scr["ga"][:, t]).then_inc(g_in[q], 16)
                act.dma_start(s[:, q], scr["S"][:, t]).then_inc(g_in[q], 16)

        @block.tensor
        def _(pe):
            project_tiles(pe, nc, w, ps, att, w_in, mm, read, KT)

        @block.vector
        def _(dve):
            for t in range(KT):
                q = t % 2
                dve.wait_ge(g_in[q], 32 * (t // 2 + 1))
                for c in range(NCH):
                    dve.wait_ge(mm, NCH * t + c + 1)
                    nc.vector.tensor_tensor(A[:, t, c * NC:(c + 1) * NC], g[:, q, c], ps[q][:, c, 0:NC], ALU.mult).then_inc(read[q], 1)
                dve.wait_ge(read[q], NCH * (t // 2 + 1))
                nc.vector.tensor_tensor(A[:, t], A[:, t], s[:, q], ALU.add).then_inc(added, 1)
            dve.wait_ge(added, KT)


def ssd_gate(nc, d, scr, h, S, mask, cnt, seln):
    with Phase(nc, "sg") as ph:
        w = ph.sb("w", [P, 2, KT, P])
        g = ph.sb("g", [P, 2, NCH, NC])
        sc = ph.sb("sc", [NB, PAST + 1])
        sel = ph.sb("sel", [NB, PAST + 1])
        pos = ph.sb("pos", [NB, PAST])
        ps = [ph.ps(f"ps{q}", [P, NCH, 512]) for q in range(2)]
        w_in = [ph.sem(f"w_in{q}") for q in range(2)]
        read = [ph.sem(f"read{q}") for q in range(2)]
        mm, mult, loaded, ch_s, ready, stored, saved, masked = (
            ph.sem(n) for n in ("mm", "mult", "loaded", "ch", "ready", "stored", "saved", "masked"))
        block = ph.block()

        @block.sync
        def _(sp):
            sp.dma_start(sc[:, 0:PAST], scr["score"]).then_inc(loaded, 16)
            sp.dma_start(sc[:, PAST:PAST + 1], scr["snew"]).then_inc(loaded, 16)
            load_tiles(sp, w, w_in, mm, NCH, d["w_gs"], KT)
            sp.wait_ge(ready, 1)
            sp.dma_start(scr["pos"], pos[:]).then_inc(stored, 16)
            sp.wait_ge(mult, KT)
            sp.dma_start(scr["S"], S[:]).then_inc(stored, 16)
            sp.wait_ge(stored, 32)

        @block.tensor
        def _(pe):
            project_tiles(pe, nc, w, ps, h, w_in, mm, read, KT)

        @block.scalar
        def _(act):
            with act.Fori(0, KT // 2) as i:
                act.wait_ge(mult, 2 * i)
                for q in range(2):
                    for c in range(NCH):
                        act.wait_ge(mm, NCH * (2 * i + q) + c + 1)
                        nc.scalar.activation(g[:, q, c], ps[q][:, c, 0:NC], ACT.Sigmoid).then_inc(read[q], 1)

        @block.vector
        def _(dve):
            ch = Chain(dve, ch_s)

            def gate(t):
                dve.wait_ge(read[t % 2], NCH * (t // 2 + 1))
                nc.vector.tensor_tensor(S[:, t], S[:, t], g[:, t % 2].rearrange("p c n -> p (c n)"), ALU.mult).then_inc(mult, 1)

            dve.wait_ge(loaded, 32)
            ch.link(nc.vector.tensor_scalar(sel[:], sc[:], -3.2e38, None, ALU.is_lt))
            gate(0)
            ch.link(nc.vector.tensor_tensor_scan(pos[:], sel[:, 0:PAST], sel[:, 0:PAST], 0.0, ALU.add, ALU.max))
            ch.link(nc.vector.tensor_copy(cnt[:], pos[:, PAST - 1:PAST]))
            ch.link(nc.vector.tensor_copy(seln[:], sel[:, PAST:PAST + 1]))
            gate(1)
            ch.link(nc.vector.tensor_tensor(pos[:], pos[:], sel[:, 0:PAST], ALU.mult))
            gate(2)
            ch.link(nc.vector.tensor_scalar(pos[:], pos[:], -1.0, None, ALU.add))
            dve.sem_inc(ready, 1)
            gate(3)
            part = mask[:, mask_at(FIRST):mask_at(TB)]
            nc.vector.tensor_scalar(part, part, -3.2e38, -BIG, ALU.is_gt, ALU.mult).then_inc(masked, 1)
            for t in range(4, KT):
                gate(t)


def mix_out(nc, d, x_d, x, A, ada):
    with Phase(nc, "mo") as ph:
        w = ph.sb("w", [P, 2, KT, P])
        smp = ph.sb("smp", [P, 2, NB])
        ps = [ph.ps(f"ps{q}", [P, NCH, 512]) for q in range(2)]
        w_in = [ph.sem(f"w_in{q}") for q in range(2)]
        read = [ph.sem(f"read{q}") for q in range(2)]
        mm, x_in, smped = (ph.sem(n) for n in ("mm", "x_in", "smped"))
        block = ph.block()
        gate = 5 * KT

        @block.sync
        def _(sp):
            load_tiles(sp, w, w_in, mm, NCH, d["w_out"], KT)

        @block.scalar
        def _(act):
            act.dma_start(x[:], x_d).then_inc(x_in, 16)

        @block.tensor
        def _(pe):
            project_tiles(pe, nc, w, ps, A, w_in, mm, read, KT)

        @block.vector
        def _(dve):
            dve.wait_ge(x_in, 16)
            with dve.Fori(0, KT // 2) as i:
                for q in range(2):
                    t = 2 * i + q
                    dve.wait_ge(mm, NCH * (2 * i + q + 1))
                    nc.vector.tensor_tensor(smp[:, q], ps[q][:, 2, LASTP:NC], ada[:, gate + t, 1:NCOND],
                                            ALU.mult).then_inc(smped, 1)
                    for n in range(NCH):
                        c = NC if n < NCH - 1 else LASTP
                        v = nc.vector.scalar_tensor_tensor(
                            out=x[:, t, n * NC:n * NC + c], in0=ps[q][:, n, 0:c],
                            scalar=ada[:, bass.ds(gate + t, 1), 0:1].rearrange("p a b -> p (a b)"),
                            in1=x[:, t, n * NC:n * NC + c], op0=ALU.mult, op1=ALU.add)
                        if n < NCH - 1:
                            v.then_inc(read[q], 1)
                    dve.wait_ge(smped, 2 * i + q + 1)
                    nc.vector.tensor_tensor(x[:, t, SEQ:TOK], x[:, t, SEQ:TOK], smp[:, q], ALU.add).then_inc(read[q], 1)
            for q in range(2):
                dve.wait_ge(read[q], NCH * KT // 2)


def time_steps(nc, d, tok, dt, dtA, ea, te, etot, upper):
    with Phase(nc, "ts") as ph:
        rows = ph.sb("rows", [P, 2, SH])
        t = {n: ph.sb(n, [P, TB + 1, SH]) for n in ("v", "e", "u", "l", "r")}
        ps = ph.ps("ps", [P, 2, 512])
        r_in, negabs, exped, logged, ch_s, mm, ex, zero = (ph.sem(n) for n in ("r_in", "negabs", "exped", "logged", "ch", "mm", "ex", "zero"))
        ones = ph.sb("ones", [P, P])
        block = ph.block()
        v, e, u, l, r = (t[n] for n in ("v", "e", "u", "l", "r"))
        raw = tok[:, :, NKV * HD + NIH:VW]
        bc = lambda row: rows[:, row].unsqueeze(1).to_broadcast([P, TB, SH])

        @block.sync
        def _(sp):
            sp.dma_start(rows[:, 0], d["dt_bias"]).then_inc(r_in, 16)
            sp.dma_start(rows[:, 1], d["a_log"]).then_inc(r_in, 16)
            sp.dma_start(upper[:], d["upper"]).then_inc(r_in, 16)

        @block.scalar
        def _(act):
            act.wait_ge(r_in, 48)
            nc.scalar.activation(rows[:, 1], rows[:, 1], ACT.Exp).then_inc(exped, 1)
            act.wait_ge(negabs, 1)
            nc.scalar.activation(e[:], e[:], ACT.Exp).then_inc(exped, 1)
            act.wait_ge(negabs, 2)
            nc.scalar.activation(l[:], u[:], ACT.Ln).then_inc(logged, 1)
            act.wait_ge(ex, 1)
            f = lambda a: a[:].rearrange("p c h -> p (c h)")
            nc.scalar.activation(f(ea), ps[:, 0, 0:TB * SH], ACT.Exp).then_inc(exped, 1)
            nc.scalar.activation(f(etot), ps[:, 1, 0:TB * SH], ACT.Exp).then_inc(exped, 1)
            nc.scalar.activation(te[:], te[:], ACT.Exp).then_inc(exped, 1)
            act.wait_ge(exped, 5)

        @block.tensor
        def _(pe):
            pe.wait_ge(mm, 1)
            f = dtA[:, 0:TB].rearrange("p c h -> p (c h)")
            nc.tensor.matmul(ps[:, 0, 0:TB * SH], upper[:], f, start=True, stop=True)
            nc.tensor.matmul(ps[:, 1, 0:TB * SH], ones[:], f, start=True, stop=True).then_inc(mm, 1)

        @block.gpsimd
        def _(pool):
            nc.gpsimd.memset(ones[:], 1.0).then_inc(zero, 1)

        @block.vector
        def _(dve):
            ch = Chain(dve, ch_s)
            dve.wait_ge(r_in, 48)
            ch.link(nc.vector.memset(v[:, TB], 0.0))
            ch.link(nc.vector.tensor_tensor(v[:, 0:TB], raw[:, 0:TB], bc(0), ALU.add))
            ch.link(nc.vector.tensor_tensor(v[0:NB, TB], raw[0:NB, TB], rows[0:NB, 0], ALU.add))
            nc.vector.scalar_tensor_tensor(out=e[:], in0=v[:], scalar=-1.0, in1=v[:], op0=ALU.mult, op1=ALU.min).then_inc(negabs, 1)
            dve.wait_ge(exped, 2)
            ch.link(nc.vector.tensor_scalar(u[:], e[:], 1.0, None, ALU.add))
            dve.sem_inc(negabs, 1)
            ch.link(nc.vector.tensor_scalar(r[:], u[:], -1.0, None, ALU.add))
            dve.wait_ge(logged, 1)
            ch.link(nc.vector.tensor_scalar(u[:], r[:], 0.0, None, ALU.is_equal))
            ch.link(nc.vector.tensor_tensor(r[:], r[:], u[:], ALU.add))
            ch.link(nc.vector.reciprocal(r[:], r[:]))
            ch.link(nc.vector.tensor_tensor(l[:], l[:], r[:], ALU.mult))
            ch.link(nc.vector.tensor_tensor(l[:], l[:], u[:], ALU.add))
            ch.link(nc.vector.tensor_tensor(l[:], l[:], e[:], ALU.mult))
            ch.link(nc.vector.scalar_tensor_tensor(out=dt[:], in0=v[:], scalar=0.0, in1=l[:], op0=ALU.max, op1=ALU.add))
            ch.link(nc.vector.scalar_tensor_tensor(out=dtA[:, 0:TB], in0=dt[:, 0:TB], scalar=-1.0, in1=bc(1),
                                                   op0=ALU.mult, op1=ALU.mult))
            ch.link(nc.vector.scalar_tensor_tensor(out=dtA[:, TB], in0=dt[:, TB], scalar=-1.0, in1=rows[:, 1],
                                                   op0=ALU.mult, op1=ALU.mult))
            dve.wait_ge(zero, 1)
            dve.sem_inc(mm, 1)
            dve.wait_ge(mm, 2)
            f = lambda a: a[:].rearrange("p c h -> p (c h)")
            ch.link(nc.vector.tensor_copy(f(te), ps[:, 1, 0:TB * SH]))
            ch.link(nc.vector.tensor_tensor(f(te), f(te), ps[:, 0, 0:TB * SH], ALU.subtract))
            dve.sem_inc(ex, 1)


def ssd_project(nc, arena, banks, start, d, o, scr, g, h, xb, xc, zs, cw, cb, y, mask):
    with Phase(nc, "sp", arena, start, banks=banks) as ph:
        w = ph.sb("w", [P, 2, KT, P])
        cv = ph.sb("cv", [P, 2, SEQ])
        st = ph.sb("st", [P, XT, CW - 1, NB])
        sm = ph.sb("sm", [P, 2, XT, NB])
        m8 = ph.sb("m8", [P, len(CHOSEN) + 1, 8])
        top = y[0:NB].rearrange("p a b -> p (a b)")[:, 0:PAST + 1]
        top_in, found, tick = ph.sem("top_in"), ph.sem("found"), ph.sem("tick")
        ps = [ph.ps(f"ps{q}", [P, NCH, 512]) for q in range(2)]
        w_in = [ph.sem(f"w_in{q}") for q in range(2)]
        read = [ph.sem(f"read{q}") for q in range(2)]
        mm, st_in, pad, tap, conv, act_done, smp, saved = (
            ph.sem(n) for n in ("mm", "st_in", "pad", "tap", "conv", "act_done", "smp", "saved"))
        block = ph.block()
        PAD = CW - 1

        @block.sync
        def _(sp):
            sp.dma_start(top[:, 0:PAST], scr["score"]).then_inc(top_in, 16)
            sp.dma_start(top[:, PAST:PAST + 1], scr["snew"]).then_inc(top_in, 16)
            load_tiles(sp, w, w_in, mm, NCH, d["w_ssd"][g], XT + 4)
            for q in range(2):
                sp.wait_ge(read[q], NCH * XT // 2)
            sp.dma_start(o["conv_p"][g], xb[:, :, SEQ:SEQ + PAD]).then_inc(saved, 16)
            sp.dma_start(o["conv_s"][g], xb[:, :, PAD + SEQ:PAD + TOK]).then_inc(saved, 16)
            sp.wait_ge(found, 2 * (len(CHOSEN) * PROMPT_ROUNDS + SHARE))
            sp.dma_start(scr["score"], top[:, 0:PAST]).then_inc(saved, 16)
            sp.dma_start(scr["snew"], top[:, PAST:PAST + 1]).then_inc(saved, 16)
            sp.wait_ge(saved, 64)

        @block.gpsimd
        def _(pool):
            nc.gpsimd.memset(xb[:, :, 0:PAD], 0.0).then_inc(pad, 1)

        @block.tensor
        def _(pe):
            project_tiles(pe, nc, w, ps, h, w_in, mm, read, XT + 4)

        @block.scalar
        def _(act):
            act.dma_start(st[:], d["state_conv"][g]).then_inc(st_in, 16)

            def copy(dst, i, before=0, func=ACT.Copy):
                for q in range(2):
                    for c in range(NCH):
                        act.wait_ge(mm, NCH * (before + 2 * i + q) + c + 1)
                        nc.scalar.activation(dst[:, 2 * i + q, c * NC:(c + 1) * NC], ps[q][:, c, 0:NC], func).then_inc(read[q], 1)

            def silu(i):
                for q in range(2):
                    t = 2 * i + q
                    act.wait_ge(conv, t + 1)
                    nc.scalar.activation(xc[:, t, 0:SEQ], cv[:, q], ACT.Silu,
                                         bias=cb[:, bass.ds(g * XT + t, 1)]).then_inc(act_done, 1)

            raw = xb[:, :, PAD:PAD + TOK]
            copy(raw, 0)
            copy(raw, 1)
            silu(0)
            copy(raw, 2)
            silu(1)
            copy(zs, 0, XT, ACT.Silu)
            silu(2)
            copy(zs, 1, XT, ACT.Silu)
            act.wait_ge(smp, 2 * CW)
            nc.scalar.activation(xc[:, :, SEQ:TOK], sm[:, 0], ACT.Silu).then_inc(act_done, 1)
            act.wait_ge(act_done, XT + 1)

        @block.vector
        def _(dve):

            def convolve(i):
                for q in range(2):
                    t = 2 * i + q
                    dve.wait_ge(read[q], NCH * (i + 1))
                    dve.wait_ge(act_done, 2 * i)
                    for k in range(CW):
                        src, wk = xb[:, t, k:k + SEQ], cw[:, bass.ds(g * XT + t, 1), k:k + 1].rearrange("p a b -> p (a b)")
                        if k == 0:
                            v = nc.vector.tensor_scalar(cv[:, q], src, wk, None, ALU.mult)
                        else:
                            v = nc.vector.scalar_tensor_tensor(out=cv[:, q], in0=src, scalar=wk, in1=cv[:, q],
                                                               op0=ALU.mult, op1=ALU.add)
                        if k < CW - 1:
                            v.then_inc(tap, 1)
                            dve.wait_ge(tap, (CW - 1) * t + k + 1)
                        else:
                            v.then_inc(conv, 1)

            n = top_rounds(dve, nc, chosen_rows(mask), m8, found, tick, 0, PROMPT_ROUNDS)
            dve.wait_ge(pad, 1)
            convolve(0)
            dve.wait_ge(top_in, 32)
            n = top_rounds(dve, nc, [top], m8, found, tick, n, SHARE // 4)
            convolve(1)
            n = top_rounds(dve, nc, [top], m8, found, tick, n, SHARE // 4)
            convolve(2)
            dve.wait_ge(st_in, 16)
            for k in range(CW):
                src = st[:, :, k] if k < CW - 1 else xb[:, :, PAD + SEQ:PAD + TOK]
                wk = cw[:, bass.ds(g * XT, XT), k:k + 1].to_broadcast([P, XT, NB])
                nc.vector.tensor_tensor(sm[:, 0 if k == 0 else 1], src, wk, ALU.mult).then_inc(smp, 1)
                dve.wait_ge(smp, 2 * k + 1)
                other = sm[:, 1] if k else cb[:, bass.ds(g * XT, XT)].unsqueeze(2).to_broadcast([P, XT, NB])
                nc.vector.tensor_tensor(sm[:, 0], sm[:, 0], other, ALU.add).then_inc(smp, 1)
                dve.wait_ge(smp, 2 * k + 2)
            top_rounds(dve, nc, [top], m8, found, tick, n, SHARE - SHARE // 4 * 2)


def ssd_scan(nc, arena, banks, d, o, g, xc, y, dt, dtA, ea, te, etot, upper, below, ident, hT):
    R, PD = SH // SG, DI // SH
    GW = R * PD
    with Phase(nc, "sc", arena, banks=banks) as ph:
        st = ph.sb("st", [P, XT, P])
        lower = ph.sb("lower", [P, R, P])
        xdt = ph.sb("xdt", [P, GW])
        xw = ph.sb("xw", [P, GW])
        bt = ph.sb("bt", [P, P])
        cbm = ph.sb("cbm", [P, P])
        E = ph.sb("E", [P, R, P])
        yt = ph.sb("yt", [P, GW])
        pX, pB, pY, pO, pH, pT = (ph.ps(n, [P, 512]) for n in ("pX", "pB", "pY", "pO", "pH", "pT"))
        pS = ph.ps("pS", [P, R, P])
        names = ("staged", "segs", "turned", "seg", "x_dt", "x_w", "b_t", "cb_m", "decay", "M", "ydiag", "yoff", "hup",
                 "y1", "y2", "h0", "h1", "h2", "yturn", "ysaved", "saved")
        (staged, segs, turned, seg, x_dt, x_w, b_t, cb_m, decay, M, ydiag, yoff, hup, y1, y2, h0, h1, h2, yturn, ysaved,
         saved) = (ph.sem(n) for n in names)
        block = ph.block()
        heads = bass.ds(g * R, R)
        wide = lambda a, c: a[:, c, heads].unsqueeze(2).to_broadcast([P, R, PD])
        v3 = lambda a: a.rearrange("p (r d) -> p r d", r=R)

        @block.gpsimd
        def _(pool):
            with pool.Fori(0, TB) as c:
                pool.wait_ge(hup, c)
                pool.wait_ge(yoff, c)
                nc.gpsimd.tensor_copy(st[:], xc[:, :, bass.ds(c * P, P)]).then_inc(staged, 1)
                pool.wait_ge(seg, c)
                nc.gpsimd.tensor_tensor(lower[:], below[:].unsqueeze(1).to_broadcast([P, R, P]),
                                        dtA[:, c, heads].unsqueeze(2).to_broadcast([P, R, P]), ALU.mult).then_inc(segs, 1)
                pool.wait_ge(x_dt, c + 1)
                nc.gpsimd.tensor_tensor(v3(xw[:]), v3(xdt[:]), wide(te, c), ALU.mult).then_inc(x_w, 1)

        @block.tensor
        def _(pe):
            with pe.Fori(0, TB) as c:
                pe.wait_ge(staged, c + 1)
                pe.wait_ge(x_dt, c)
                pe.wait_ge(cb_m, c)
                for t in range(4):
                    nc.tensor.transpose(pX[:, t * P:(t + 1) * P], st[:, t], ident[:])
                nc.tensor.transpose(pB[:, 0:P], st[:, 4], ident[:])
                nc.tensor.matmul(pB[:, P:2 * P], st[:, 4], st[:, 5], start=True, stop=True).then_inc(turned, 1)
                pe.wait_ge(segs, c + 1)
                pe.wait_ge(decay, c)
                for r in range(R):
                    m = nc.tensor.matmul(pS[:, r], lower[:, r], upper[:], start=True, stop=True)
                m.then_inc(seg, 1)
                pe.wait_ge(h2, c + 1)
                pe.wait_ge(y1, c)
                nc.tensor.matmul(pO[:], st[:, 5], hT[:], start=True, stop=True).then_inc(yoff, 1)
                pe.wait_ge(b_t, c + 1)
                pe.wait_ge(x_w, c + 1)
                nc.tensor.matmul(pH[:], bt[:], xw[:], start=True, stop=True).then_inc(hup, 1)
                pe.wait_ge(M, c + 1)
                pe.wait_ge(y2, c)
                for r in range(R):
                    m = nc.tensor.matmul(pY[:, r * PD:(r + 1) * PD], E[:, r], xdt[:, r * PD:(r + 1) * PD], start=True, stop=True)
                m.then_inc(ydiag, 1)
                pe.wait_ge(y2, c + 1)
                pe.wait_ge(ysaved, c)
                for t in range(4):
                    m = nc.tensor.transpose(pT[:, t * P:(t + 1) * P], yt[:, t * P:(t + 1) * P], ident[:])
                m.then_inc(yturn, 1)

        @block.scalar
        def _(act):
            with act.Fori(0, TB) as c:
                act.wait_ge(seg, c + 1)
                act.wait_ge(ydiag, c)
                nc.scalar.activation(E[:].rearrange("p r l -> p (r l)"), pS[:].rearrange("p r l -> p (r l)"), ACT.Exp).then_inc(decay, 1)
                act.wait_ge(yturn, c + 1)
                nc.scalar.activation(y[:, 0:4, bass.ds(c * P, P)], pT[:].rearrange("p (t l) -> p t l", t=4), ACT.Copy).then_inc(ysaved, 1)
            act.wait_ge(ysaved, TB)

        @block.sync
        def _(sp):
            sp.wait_ge(h2, TB + 1)
            sp.dma_start(o["ssm_p"][g], hT[:]).then_inc(saved, 16)
            sp.wait_ge(saved, 16)

        @block.vector
        def _(dve):
            nc.vector.memset(hT[:], 0.0).then_inc(h2, 1)
            with dve.Fori(0, TB) as c:
                dve.wait_ge(turned, c + 1)
                dve.wait_ge(ydiag, c)
                dve.wait_ge(x_w, c)
                nc.vector.tensor_tensor(v3(xdt[:]), v3(pX[:]), wide(dt, c), ALU.mult).then_inc(x_dt, 1)
                dve.wait_ge(hup, c)
                nc.vector.tensor_copy(bt[:], pB[:, 0:P]).then_inc(b_t, 1)
                nc.vector.tensor_tensor(cbm[:], pB[:, P:2 * P], upper[:], ALU.mult).then_inc(cb_m, 1)
                dve.wait_ge(decay, c + 1)
                dve.wait_ge(cb_m, c + 1)
                nc.vector.tensor_tensor(E[:], E[:], cbm[:].unsqueeze(1).to_broadcast([P, R, P]), ALU.mult).then_inc(M, 1)
                dve.wait_ge(yoff, c + 1)
                dve.wait_ge(yturn, c)
                nc.vector.tensor_tensor(v3(yt[:]), v3(pO[:]), wide(ea, c), ALU.mult).then_inc(y1, 1)
                dve.wait_ge(h2, c + 1)
                nc.vector.tensor_tensor(v3(hT[:]), v3(hT[:]), wide(etot, c), ALU.mult).then_inc(h1, 1)
                dve.wait_ge(h1, c + 1)
                dve.wait_ge(hup, c + 1)
                nc.vector.tensor_tensor(hT[:], hT[:], pH[:], ALU.add).then_inc(h2, 1)
                dve.wait_ge(y1, c + 1)
                dve.wait_ge(ydiag, c + 1)
                nc.vector.tensor_tensor(yt[:], yt[:], pY[:], ALU.add).then_inc(y2, 1)


def ssd_sample(nc, arena, banks, d, o, g, xc, y, dt, dtA, ones, ident):
    R, PD = SH // SG, DI // SH
    HP = R // 2
    with Phase(nc, "ss", arena, banks=banks) as ph:
        H = ph.sb("H", [P, HP, NB, DS])
        T = ph.sb("T", [P, NB, DS])
        xs = ph.sb("xs", [NB, XT * P])
        dA = ph.sb("dA", [NB, R])
        dAx = ph.sb("dAx", [NB, R * PD])
        dAf = ph.sb("dAf", [P, HP, NB])
        eye = ph.sb("eye", [NB, 2, NB, DS])
        pX = ph.ps("pX", [NB, 2, 512])
        pA = ph.ps("pA", [P, HP, NB])
        pC = ph.ps("pC", [P, NB, DS])
        pU = ph.ps("pU", [P, NB, DS])
        H_in, turned, moved, exped, dAturn, ch_s, diag, mmc, mmu, upd, red, saved = (
            ph.sem(n) for n in ("H_in", "turned", "moved", "exped", "dAturn", "ch", "diag", "mmc", "mmu", "upd", "red", "saved"))
        block = ph.block()
        heads = bass.ds(g * R, R)
        chunks = lambda a: a.rearrange("p b n -> p (b n)")

        @block.sync
        def _(sp):
            sp.dma_start(H[:].rearrange("p q b n -> p (q b n)"), d["state_ssm"][g]).then_inc(H_in, 16)
            sp.wait_ge(upd, HP)
            sp.dma_start(o["ssm_s"][g], H[:].rearrange("p q b n -> p (q b n)")).then_inc(saved, 16)
            sp.wait_ge(saved, 16)

        @block.scalar
        def _(act):
            nc.scalar.activation(dA[:], dtA[0:NB, TB, heads], ACT.Exp).then_inc(exped, 1)

        @block.tensor
        def _(pe):
            for t in range(XT):
                m = nc.tensor.transpose(pX[:, t // 4, (t % 4) * P:(t % 4 + 1) * P], xc[:, t, SEQ:TOK], ident[:])
            m.then_inc(turned, 1)
            pe.wait_ge(moved, 2)
            for t in range(HP):
                m = nc.tensor.transpose(pA[:, t], dAx[:, t * P:(t + 1) * P], ident[0:NB, 0:NB])
            m.then_inc(dAturn, 1)
            pe.wait_ge(diag, 1)
            for c in range(2):
                m = nc.tensor.matmul(chunks(pC[:])[:, c * 512:(c + 1) * 512], ones[0:NB, :],
                                     chunks(eye[:, 1])[:, c * 512:(c + 1) * 512], start=True, stop=True)
            m.then_inc(mmc, 1)
            for t in range(HP):
                pe.wait_ge(upd, t) if t else None
                for c in range(2):
                    m = nc.tensor.matmul(chunks(pU[:])[:, c * 512:(c + 1) * 512], xs[:, t * P:(t + 1) * P],
                                         chunks(eye[:, 0])[:, c * 512:(c + 1) * 512], start=True, stop=True)
                m.then_inc(mmu, 1)

        @block.vector
        def _(dve):
            ch = Chain(dve, ch_s)
            dve.wait_ge(exped, 1)
            nc.vector.tensor_copy(dAx[:].rearrange("b (r p) -> b r p", r=R), dA[:].unsqueeze(2).to_broadcast([NB, R, PD])).then_inc(moved, 1)
            dve.wait_ge(turned, 1)
            nc.vector.tensor_copy(xs[:], pX[:].rearrange("b a n -> b (a n)")[:, 0:XT * P]).then_inc(moved, 1)
            dve.wait_ge(moved, 2)
            xv = xs[:, 0:R * PD].rearrange("b (r p) -> b r p", r=R)
            ch.link(nc.vector.tensor_tensor(xv, xv, dt[0:NB, TB, heads].unsqueeze(2).to_broadcast([NB, R, PD]), ALU.mult))
            for j in range(2):
                ch.link(nc.vector.tensor_tensor(eye[:, j], xs[:, (4 + j) * P:(5 + j) * P].unsqueeze(1).to_broadcast([NB, NB, DS]),
                                                ident[0:NB, 0:NB].unsqueeze(2).to_broadcast([NB, NB, DS]), ALU.mult))
            dve.sem_inc(diag, 1)
            dve.wait_ge(dAturn, 1)
            ch.link(nc.vector.tensor_copy(dAf[:], pA[:]))
            dve.wait_ge(H_in, 16)
            dve.wait_ge(mmc, 1)
            for t in range(HP):
                ch.link(nc.vector.tensor_tensor(H[:, t], H[:, t], dAf[:, t].unsqueeze(2).to_broadcast([P, NB, DS]), ALU.mult))
                dve.wait_ge(mmu, t + 1)
                nc.vector.tensor_tensor(H[:, t], H[:, t], pU[:], ALU.add).then_inc(upd, 1)
                dve.wait_ge(upd, t + 1)
                ch.link(nc.vector.tensor_tensor(T[:], H[:, t], pC[:], ALU.mult))
                ch.link(nc.vector.tensor_reduce(y[:, t, SEQ:TOK], T[:], AX, ALU.add))


def ssd_out(nc, arena, banks, d, g, xc, zs, y, ones, dskip, nssd, S, mask):
    GT = 4
    with Phase(nc, "so", arena, banks=banks) as ph:
        w = ph.sb("w", [P, 2, GT, P])
        sq = ph.sb("sq", [P, 2, TOK])
        rstd = ph.sb("rstd", [P, TOK])
        eps = ph.sb("eps", [P, 1])
        m8 = ph.sb("m8", [P, len(CHOSEN), 8])
        found, tick = ph.sem("found"), ph.sem("tick")
        ps = [ph.ps(f"ps{q}", [P, NCH, 512]) for q in range(2)]
        w_in = [ph.sem(f"w_in{q}") for q in range(2)]
        read = [ph.sem(f"read{q}") for q in range(2)]
        eps_set, skip, gated, squared, summed, root, inv, normed, scaled, mm = (
            ph.sem(n) for n in ("eps_set", "skip", "gated", "squared", "summed", "root", "inv", "normed", "scaled", "mm"))
        block = ph.block()

        @block.sync
        def _(sp):
            load_tiles(sp, w, w_in, mm, NCH, d["w_so"][g], KT)

        @block.scalar
        def _(act):
            for t in range(GT):
                act.wait_ge(gated, t + 1)
                if t >= 2:
                    act.wait_ge(summed, t - 1)
                nc.scalar.activation(sq[:, t % 2], y[:, t], ACT.Square).then_inc(squared, 1)
            act.wait_ge(summed, GT)
            act.wait_ge(eps_set, 1)
            nc.scalar.activation(rstd[:].rearrange("p (n c) -> p n c", n=NCH), ps[1][:, :, 0:NC], ACT.Sqrt,
                                 scale=1.0 / (GT * P), bias=eps[:]).then_inc(root, 1)

        @block.tensor
        def _(pe):
            for t in range(GT):
                pe.wait_ge(squared, t + 1)
                for n in range(NCH):
                    m = nc.tensor.matmul(ps[1][:, n, 0:NC], ones[:], sq[:, t % 2, n * NC:(n + 1) * NC],
                                         start=t == 0, stop=t == GT - 1)
                m.then_inc(summed, 1)
            pe.wait_ge(scaled, GT)
            project_tiles(pe, nc, w, ps, y, w_in, mm, read, KT, kt=GT)

        @block.vector
        def _(dve):
            nc.vector.memset(eps[:], EPS).then_inc(eps_set, 1)
            for t in range(GT):
                nc.vector.scalar_tensor_tensor(out=y[:, t], in0=xc[:, t], scalar=dskip[:, bass.ds(g * GT + t, 1)], in1=y[:, t],
                                               op0=ALU.mult, op1=ALU.add).then_inc(skip, 1)
                dve.wait_ge(skip, t + 1)
                nc.vector.tensor_tensor(y[:, t], y[:, t], zs[:, t], ALU.mult).then_inc(gated, 1)
            dve.wait_ge(root, 1)
            nc.vector.reciprocal(rstd[:], rstd[:]).then_inc(inv, 1)
            dve.wait_ge(inv, 1)
            dve.wait_ge(gated, GT)
            for t in range(GT):
                nc.vector.scalar_tensor_tensor(out=y[:, t], in0=y[:, t], scalar=nssd[:, bass.ds(g * GT + t, 1)], in1=rstd[:],
                                               op0=ALU.mult, op1=ALU.mult).then_inc(scaled, 1)
            with dve.Fori(0, KT // 2) as i:
                top_round(dve, nc, chosen_rows(mask), m8, found, tick, 2 * len(CHOSEN) * i)
                for q in range(2):
                    for c in range(NCH):
                        dve.wait_ge(mm, NCH * (2 * i + q) + c + 1)
                        part = S[:, 2 * i + q, c * NC:(c + 1) * NC]
                        nc.vector.tensor_tensor(part, part, ps[q][:, c, 0:NC], ALU.add).then_inc(read[q], 1)
            for q in range(2):
                dve.wait_ge(read[q], NCH * KT // 2)


def final_norm(nc, o, x, y, ones, gain_d):
    with Phase(nc, "fn") as ph:
        sq = ph.sb("sq", [P, 2, TOK])
        rstd = ph.sb("rstd", [P, TOK])
        eps = ph.sb("eps", [P, 1])
        gain = ph.sb("gain", [P, KT])
        ps = ph.ps("ps", [P, NCH, 512])
        gain_in, eps_set, squared, summed, root, inv, scaled, saved = (
            ph.sem(n) for n in ("gain_in", "eps_set", "squared", "summed", "root", "inv", "scaled", "saved"))
        block = ph.block()

        @block.sync
        def _(sp):
            sp.dma_start(gain[:], gain_d).then_inc(gain_in, 16)
            for k in range(KT):
                sp.wait_ge(scaled, k + 1)
                sp.dma_start(o["y"][:, k], y[:, k]).then_inc(saved, 16)
            sp.wait_ge(saved, 16 * KT)

        @block.scalar
        def _(act):
            for k in range(KT):
                if k >= 2:
                    act.wait_ge(summed, k - 1)
                nc.scalar.activation(sq[:, k % 2], x[:, k], ACT.Square).then_inc(squared, 1)
            act.wait_ge(summed, KT)
            act.wait_ge(eps_set, 1)
            nc.scalar.activation(rstd[:].rearrange("p (n c) -> p n c", n=NCH), ps[:, :, 0:NC], ACT.Sqrt,
                                 scale=1.0 / DM, bias=eps[:]).then_inc(root, 1)

        @block.tensor
        def _(pe):
            for k in range(KT):
                pe.wait_ge(squared, k + 1)
                for n in range(NCH):
                    m = nc.tensor.matmul(ps[:, n, 0:NC], ones[:], sq[:, k % 2, n * NC:(n + 1) * NC],
                                         start=k == 0, stop=k == KT - 1)
                m.then_inc(summed, 1)

        @block.vector
        def _(dve):
            nc.vector.memset(eps[:], EPS).then_inc(eps_set, 1)
            dve.wait_ge(root, 1)
            nc.vector.reciprocal(rstd[:], rstd[:]).then_inc(inv, 1)
            dve.wait_ge(inv, 1)
            dve.wait_ge(gain_in, 16)
            for k in range(KT):
                nc.vector.scalar_tensor_tensor(out=y[:, k], in0=x[:, k], scalar=gain[:, k:k + 1], in1=rstd[:],
                                               op0=ALU.mult, op1=ALU.mult).then_inc(scaled, 1)


def ssd_branch(nc, d, o, scr, h, tok, ones, ident, S, mask):
    with ExitStack() as c:
        sb = lambda n, s: c.enter_context(nc.sbuf_tensor(n, s, F32))
        dt, dtA = sb("dt", [P, TB + 1, SH]), sb("dtA", [P, TB + 1, SH])
        ea, te, etot = (sb(n, [P, TB, SH]) for n in ("ea", "te", "etot"))
        upper, below = sb("upper", [P, P]), sb("below", [P, P])
        cw, cb = sb("cw", [P, SG * XT, CW]), sb("cb", [P, SG * XT])
        dskip, nssd = sb("dskip", [P, DI // P]), sb("nssd", [P, DI // P])
        hT = sb("hT", [P, DI // SG])
        time_steps(nc, d, tok, dt, dtA, ea, te, etot, upper)
        with Phase(nc, "si") as ph:
            loaded, zeroed = ph.sem("loaded"), ph.sem("zeroed")
            block = ph.block()

            @block.sync
            def _(sp):
                for dst, src in ((below, "below"), (cw, "conv_w"), (cb, "conv_b"), (dskip, "d_skip"), (nssd, "norm_ssd")):
                    sp.dma_start(dst[:], d[src]).then_inc(loaded, 16)
                sp.dma_start(o["conv_old"], d["conv_old"]).then_inc(loaded, 16)
                sp.wait_ge(loaded, 96)

            @block.gpsimd
            def _(pool):
                nc.gpsimd.memset(S[:], 0.0).then_inc(zeroed, 1)
                pool.wait_ge(zeroed, 1)
        xc, zs, y = sb("xc", [P, XT, TOK]), sb("zs", [P, 4, TOK]), sb("y", [P, 4, TOK])
        arena = sb("arena", [P, 10602])
        banks = c.enter_context(nc.psum_tensor("banks", [P, 8 * 512], F32))
        start, xb = carve(arena, 0, [P, XT, CW - 1 + TOK])
        with nc.Fori(0, SG) as g:
            ssd_project(nc, arena, banks, start, d, o, scr, g, h, xb, xc, zs, cw, cb, y, mask)
            ssd_scan(nc, arena, banks, d, o, g, xc, y, dt, dtA, ea, te, etot, upper, below, ident, hT)
            ssd_sample(nc, arena, banks, d, o, g, xc, y, dt, dtA, ones, ident)
            ssd_out(nc, arena, banks, d, g, xc, zs, y, ones, dskip, nssd, S, mask)


def by_page(a):
    return a.rearrange("(c b) (i s) -> (b i) c s", c=2, s=PAGE)


def sample_gather(nc, d, scr, h, ident, gathered, kv, brows):
    RING = 2 * NPAGE
    with Phase(nc, "s3") as ph:
        pt = ph.sb("pt", [P, 2, P])
        pos = ph.sb("pos", [P, NB * NPAGE])
        iota = ph.sb("iota", [P, TOPK], F16)
        vals = ph.sb("vals", [P, NB * NPAGE, 3], F16)
        tab = ph.sb("tab", [P, NB * NPAGE], I32)
        hots = ph.sb("hots", [P, RING, TOPK], F16)
        ent = ph.sb("ent", [P, NB, 2, 3])
        where = ph.sb("where", [P, 3, NB, 2])
        row = ph.sb("row", [P, NB, 2], U32)
        brow = ph.sb("brow", [P, NB, 2], U32)
        w = ph.sb("w", [P, 2, KT, P])
        g = ph.sb("g", [P, 2, NCH, NC])
        ps = ph.ps("ps", [P, NCH, 512])
        w_in = [ph.sem(f"w_in{q}") for q in range(2)]
        saved = [ph.sem(f"saved{q}") for q in range(2)]
        gmm, gread = ph.sem("gmm"), ph.sem("gread")
        pT = ph.ps("pT", [P, 2, P])
        pE = [[ph.ps(f"pE{q}{f}", [P, 512]) for f in range(2)] for q in range(2)]
        loaded, turned, posd, valsd, hotd, used, mm, read, ch_s, ready = (
            ph.sem(n) for n in ("loaded", "turned", "posd", "valsd", "hotd", "used", "mm", "read", "ch", "ready"))
        block = ph.block()

        @block.sync
        def _(sp):
            sp.dma_start(pt[:], by_page(scr["pos"])).then_inc(loaded, 16)
            sp.dma_start(iota[:], d["iota"]).then_inc(loaded, 16)
            sp.dma_start(vals[:], d["slots"]).then_inc(loaded, 16)
            sp.dma_start(tab[:], d["page_table"].to_broadcast([P, NB * NPAGE])).then_inc(loaded, 16)
            load_tiles(sp, w, w_in, gmm, NCH, d["w_ga"], KT)
            sp.wait_ge(loaded, 64)

        @block.scalar
        def _(act):
            act.sem_inc(gread, NCH)
            with act.Fori(0, KT // 2) as i:
                for q in range(2):
                    t = 2 * i + q
                    act.wait_ge(saved[q], 16 * i)
                    for c in range(NCH):
                        act.wait_ge(gmm, NCH * t + c + 1)
                        nc.scalar.activation(g[:, q, c], ps[:, c, 0:NC], ACT.Sigmoid).then_inc(gread, 1)
                    act.wait_ge(gread, NCH * (t + 2))
                    act.dma_start(scr["ga"][:, t], g[:, q].rearrange("p c n -> p (c n)")).then_inc(saved[q], 16)
            for q in range(2):
                act.wait_ge(saved[q], 16 * KT // 2)

        @block.tensor
        def _(pe):
            pe.wait_ge(loaded, 64)
            for c in range(2):
                m = nc.tensor.transpose(pT[:, c], pt[:, c], ident[:])
            m.then_inc(turned, 1)
            pe.wait_ge(valsd, 1)

            def gate(i, q):
                pe.wait_ge(w_in[q], 16 * (i + 1))
                for c in range(NCH):
                    pe.wait_ge(gread, NCH * (2 * i + q) + c + 1)
                    for k in range(KT):
                        m = nc.tensor.matmul(ps[:, c, 0:NC], w[:, q, k], h[:, k, c * NC:(c + 1) * NC],
                                             start=k == 0, stop=k == KT - 1)
                    m.then_inc(gmm, 1)

            with pe.Fori(0, NB // 4) as i:
                for q in range(2):
                    gate(i, q)
                    for r in range(2):
                        b = 4 * i + 2 * q + r
                        pe.wait_ge(read, 4 * i + 2 * q)
                        pe.wait_ge(hotd, NPAGE * (b + 1))
                        for p in range(NPAGE):
                            for f in range(2):
                                m = nc.tensor.matmul(pE[r][f][:, 0:3], hots[:, r * NPAGE + p, f * P:(f + 1) * P],
                                                     vals[:, b * NPAGE + p], start=p == 0, stop=p == NPAGE - 1)
                        m.then_inc(used, 1)
            with pe.Fori(NB // 4, KT // 2) as i:
                for q in range(2):
                    gate(i, q)

        @block.vector
        def _(dve):
            ch = Chain(dve, ch_s)
            dve.wait_ge(loaded, 64)
            nc.vector.tensor_copy(vals[:, :, 1], tab[:]).then_inc(valsd, 1)
            dve.wait_ge(turned, 1)
            ch.link(nc.vector.tensor_copy(pos[:], pT[:].rearrange("p c n -> p (c n)")))
            with dve.Fori(0, NB // 2) as i:
                for r in range(2):
                    dve.wait_ge(used, 2 * i)
                    for p in range(NPAGE):
                        nc.vector.tensor_scalar(hots[:, r * NPAGE + p], iota[:], pos[:, bass.ds((2 * i + r) * NPAGE + p, 1)], None,
                                                ALU.is_equal).then_inc(hotd, 1)
                for r in range(2):
                    dve.wait_ge(used, 2 * i + r + 1)
                    for f in range(2):
                        v = nc.vector.tensor_copy(ent[:, 2 * i + r, f], pE[r][f][:, 0:3])
                    v.then_inc(read, 1)
            dve.wait_ge(read, NB)
            off, page, log = (ent[:, :, :, n] for n in range(3))
            ch.link(nc.vector.scalar_tensor_tensor(out=where[:, 0], in0=page, scalar=float(PAGE), in1=off, op0=ALU.mult, op1=ALU.add))
            ch.link(nc.vector.scalar_tensor_tensor(out=where[:, 1], in0=log, scalar=float(PAGE), in1=off, op0=ALU.mult, op1=ALU.add))
            ch.link(nc.vector.tensor_scalar(where[:, 1], where[:, 1], float(WIN - 1 - PAST), 0.0, ALU.add, ALU.max))
            ch.link(nc.vector.tensor_copy(row[:], where[:, 0]))
            ch.link(nc.vector.tensor_copy(brow[:], where[:, 1]))
            dve.sem_inc(ready, 1)

        @block.gpsimd
        def _(pool):
            pool.wait_ge(ready, 1)
            n = 0
            for b in range(NB):
                for f in range(2):
                    at = bass.IndirectOffsetOnAxis(row[:, b, f:f + 1], 0)
                    for j, src in enumerate((d["cache_k"], d["cache_v"])):
                        pool.indirect_dma_start(kv[:, b, f, j], None, src, at).then_inc(gathered, 16)
                    pool.indirect_dma_start(brows[:, b, f], None, scr["brow"],
                                            bass.IndirectOffsetOnAxis(brow[:, b, f:f + 1], 0)).then_inc(gathered, 16)
                    n += 48
            pool.wait_ge(gathered, n)


def sample_attend(nc, d, scr, pj, tok, ones, ident, cnt, seln, kv, brows, att):
    NS = TOPK + 1
    F = 2 * HD
    with Phase(nc, "s4") as ph:
        hot = ph.sb("hot", [P, 2])
        qt = ph.sb("qt", [NB, DM])
        qm = ph.sb("qm", [NB, 2, DM])
        prod = ph.sb("prod", [P, DM])
        pn = ph.sb("pn", [P, KT, NB])
        Lg = ph.sb("Lg", [P, NB, 2, NH])
        Ln = ph.sb("Ln", [NB, NH])
        bn = ph.sb("bn", [NB, NH])
        lack = ph.sb("lack", [NB, 1])
        cd = ph.sb("cd", [NB, NB])
        cb = ph.sb("cb", [P, NB])
        slot = ph.sb("slot", [P, 2])
        mb = ph.sb("mb", [P, NB, 2])
        LL = ph.sb("LL", [NH, NB, NS])
        nm = ph.sb("nm", [NH, NB])
        den = ph.sb("den", [NH, NB])
        rd = ph.sb("rd", [NH, NB])
        PT = ph.sb("PT", [P, NB, 2, NH])
        wn = ph.sb("wn", [NB, NH])
        wd = ph.sb("wd", [NB, NB, NH])
        pq = ph.ps("pq", [P, 2, DM])
        pm = ph.ps("pm", [P, 512])
        pL = pq[0:NH].rearrange("h a (b j) -> h (a b) j", b=NB // 2)
        small, ch_s, qturn, qmd, qb, lread, pnd, nlog, cdd, cbd, lready, lturn, mx, ex, pready, pturn, wready, wturn, ptd, od = (
            ph.sem(n) for n in ("small", "ch", "qturn", "qmd", "qb", "lread", "pnd", "nlog", "cdd", "cbd", "lready", "lturn",
                                "mx", "ex", "pready", "pturn", "wready", "wturn", "ptd", "od"))
        block = ph.block()

        @block.sync
        def _(sp):
            sp.dma_start(hot[:], d["half"]).then_inc(small, 16)
            sp.dma_start(slot[:], d["slot"]).then_inc(small, 16)
            sp.dma_start(bn[:], scr["brow"][WIN - 1:WIN, :].to_broadcast([NB, NH])).then_inc(small, 16)
            sp.wait_ge(small, 48)

        @block.tensor
        def _(pe):
            for t in range(KT):
                m = nc.tensor.transpose(pq[0:NB, 1, t * P:(t + 1) * P], pj[:, QT0 + t, SEQ:TOK], ident[:])
            m.then_inc(qturn, 1)
            pe.wait_ge(small, 48)
            pe.wait_ge(pnd, 1)
            for t in range(KT):
                m = nc.tensor.matmul(pm[0:NB, 2 * t:2 * t + 2], pn[:, t], hot[:], start=True, stop=True)
            pe.wait_ge(cdd, 1)
            nc.tensor.matmul(pm[:, 16:16 + NB], ones[0:NB, :], cd[:], start=True, stop=True).then_inc(nlog, 1)
            for b in range(NB):
                pe.wait_ge(qmd, b + 1)
                if b >= 2:
                    pe.wait_ge(lread, b - 1)
                for c in range(2):
                    m = nc.tensor.matmul(pq[:, b % 2, c * 512:(c + 1) * 512], ones[0:NB, :], qm[:, b % 2, c * 512:(c + 1) * 512],
                                         start=True, stop=True)
                m.then_inc(qb, 1)
            pe.wait_ge(lready, 1)
            for b in range(NB):
                for f in range(2):
                    nc.tensor.transpose(pL[:, b, f * P:(f + 1) * P], Lg[:, b, f], ident[:])
            nc.tensor.transpose(pm[0:NH, 64:64 + NB], Ln[:], ident[0:NB, 0:NB]).then_inc(lturn, 1)
            pe.wait_ge(pready, 1)
            for b in range(NB):
                for f in range(2):
                    at = (2 * b + f) * NH
                    nc.tensor.transpose(pq[:, 0, at:at + NH], LL[:, b, f * P:(f + 1) * P], ident[0:NH, 0:NH])
            nc.tensor.transpose(pq[0:NB, 1, 0:NH], LL[:, :, TOPK], ident[0:NH, 0:NH]).then_inc(pturn, 1)
            pe.wait_ge(ptd, 1)
            for b in range(NB):
                for m in range(2):
                    out = pm[:, 128 + (2 * b + m) * NH:128 + (2 * b + m + 1) * NH]
                    for f in range(2):
                        nc.tensor.matmul(out, kv[:, b, f, 1, m * F:(m + 1) * F], PT[:, b, f], start=f == 0, stop=False)
                    x = nc.tensor.matmul(out, tok[0:NB, TB, m * F:(m + 1) * F], wd[:, b], start=False, stop=True)
            x.then_inc(od, 1)

        @block.scalar
        def _(act):
            act.wait_ge(mx, 1)
            for b in range(NB):
                nc.scalar.activation(LL[:, b], LL[:, b], ACT.Exp, bias=nm[:, b:b + 1], accum_out=den[:, b:b + 1]).then_inc(ex, 1)

        @block.vector
        def _(dve):
            ch = Chain(dve, ch_s)
            nc.vector.tensor_tensor(pn[:].rearrange("p (m g) b -> p m g b", m=2),
                                    pj[:, QT0:QT0 + KT, SEQ:TOK].rearrange("p (m g) b -> p m g b", m=2),
                                    pj[:, KT0:KT0 + 2, SEQ:TOK].unsqueeze(2).to_broadcast([P, 2, 4, NB]), ALU.mult).then_inc(pnd, 1)
            ch.link(nc.vector.tensor_tensor(cd[:], cnt[:].to_broadcast([NB, NB]), ident[0:NB, 0:NB], ALU.mult))
            dve.sem_inc(cdd, 1)
            dve.wait_ge(qturn, 1)
            ch.link(nc.vector.tensor_copy(qt[:], pq[0:NB, 1]))
            dve.wait_ge(nlog, 1)
            dve.wait_ge(small, 48)
            ch.link(nc.vector.scalar_tensor_tensor(out=Ln[:], in0=pm[0:NB, 0:NH], scalar=float(HD ** -0.5), in1=bn[:],
                                                   op0=ALU.mult, op1=ALU.add))
            ch.link(nc.vector.tensor_copy(cb[:], pm[:, 16:16 + NB]))
            ch.link(nc.vector.tensor_scalar(lack[:], seln[:], 1.0, BIG, ALU.subtract, ALU.mult))
            ch.link(nc.vector.tensor_scalar(Ln[:], Ln[:], lack[:], None, ALU.add))
            ch.link(nc.vector.tensor_tensor(mb[:], slot[:].unsqueeze(1).to_broadcast([P, NB, 2]),
                                            cb[:].unsqueeze(2).to_broadcast([P, NB, 2]), ALU.is_ge))
            ch.link(nc.vector.tensor_scalar(mb[:], mb[:], -BIG, None, ALU.mult))
            for b in range(NB):
                if b >= 2:
                    dve.wait_ge(qb, b - 1)
                nc.vector.tensor_scalar(qm[:, b % 2], qt[:], ident[0:NB, b:b + 1], None, ALU.mult).then_inc(qmd, 1)
                dve.wait_ge(qb, b + 1)
                for f in range(2):
                    k4 = kv[:, b, f, 0].rearrange("p (m c) -> p m c", m=2).unsqueeze(2).to_broadcast([P, 2, 4, F])
                    x = nc.vector.tensor_tensor(prod[:].rearrange("p (m g c) -> p m g c", m=2, g=4), k4,
                                                pq[:, b % 2].rearrange("p (m g c) -> p m g c", m=2, g=4), ALU.mult)
                    ch.link(x)
                    ch.link(nc.vector.tensor_reduce(Lg[:, b, f], prod[:].rearrange("p (h c) -> p h c", c=HD), AX, ALU.add))
                dve.sem_inc(lread, 1)
            fl = lambda a: a[:].rearrange("p b f h -> p (b f) h")
            ch.link(nc.vector.scalar_tensor_tensor(out=fl(Lg), in0=fl(Lg), scalar=float(HD ** -0.5), in1=fl(brows),
                                                   op0=ALU.mult, op1=ALU.add))
            ch.link(nc.vector.tensor_tensor(fl(Lg), fl(Lg), mb[:].rearrange("p b f -> p (b f)").unsqueeze(2).to_broadcast([P, 2 * NB, NH]),
                                            ALU.add))
            dve.sem_inc(lready, 1)
            dve.wait_ge(lturn, 1)
            ch.link(nc.vector.tensor_copy(LL[:, :, 0:TOPK], pL[:]))
            ch.link(nc.vector.tensor_copy(LL[:, :, TOPK], pm[0:NH, 64:64 + NB]))
            nc.vector.tensor_reduce(nm[:], LL[:], AX, ALU.max, negate=True).then_inc(mx, 1)
            dve.wait_ge(ex, NB)
            ch.link(nc.vector.reciprocal(rd[:], den[:]))
            ch.link(nc.vector.tensor_tensor(LL[:], LL[:], rd[:].unsqueeze(2).to_broadcast([NH, NB, NS]), ALU.mult))
            dve.sem_inc(pready, 1)
            dve.wait_ge(pturn, 1)
            ch.link(nc.vector.tensor_copy(PT[:].rearrange("p b f h -> p (b f h)"), pq[:, 0, 0:2 * NB * NH]))
            ch.link(nc.vector.tensor_copy(wn[:], pq[0:NB, 1, 0:NH]))
            ch.link(nc.vector.tensor_tensor(wd[:], wn[:].unsqueeze(1).to_broadcast([NB, NB, NH]),
                                            ident[0:NB, 0:NB].unsqueeze(2).to_broadcast([NB, NB, NH]), ALU.mult))
            dve.sem_inc(ptd, 1)
            dve.wait_ge(od, 1)
            ov = pm[:, 128:128 + 2 * NB * NH].rearrange("p (b m h) -> p m h b", b=NB, m=2)
            for m in range(2):
                for u in range(2):
                    r = slice(u * HD, (u + 1) * HD)
                    ch.link(nc.vector.tensor_copy(att[r, 4 * m:4 * m + 4, SEQ:TOK], ov[r, m, 8 * m + u:8 * m + 8:2]))


def program(nc, d, o):
    dram = lambda n, s: nc.dram_tensor(f"scr_{n}", s, F32).ap()
    scr = {"byh": dram("byh", [NH, 512]), "brow": dram("brow", [WIN, NH]), "x": dram("x", [P, KT, TOK]),
           "S": dram("S", [P, KT, TOK]), "ga": dram("ga", [P, KT, TOK]),
           "qk": dram("qk", [P, QI0, TOK]), "snew": dram("snew", [NB, 1]), "score": dram("score", [NB, PAST]), "pos": dram("pos", [NB, PAST]), "kidx": dram("kidx", [NB * NPAGE, 2, ID * PAGE // 2])}
    with ExitStack() as ctx:
        def buf(c, n, s, t=F32):
            return c.enter_context(nc.sbuf_tensor(n, s, t))

        gathered, paged = ctx.enter_context(nc.semaphore("gathered")), ctx.enter_context(nc.semaphore("paged"))
        ada, sg = buf(ctx, "ada", [P, NA, NCOND]), buf(ctx, "sg", [P, 3, KT, NCOND])
        ones, ident = buf(ctx, "ones", [P, P]), buf(ctx, "ident", [P, P])
        h = buf(ctx, "h", [P, KT, TOK])
        with ExitStack() as c1:
            x = buf(c1, "x", [P, KT, TOK])
            c, b_ada, gains = buf(c1, "c", [P, KT, NCOND]), buf(c1, "b_ada", [P, NA]), buf(c1, "gains", [P, 3, KT])
            first_norm(nc, d, x, h, ones, ident, c, b_ada, gains, ada, sg)
            ffn(nc, "f1", d["w_f1i"], d["w_f1o"], x, h, ada, 0, late=(d, c, b_ada, gains, sg))
            norm_mod(nc, "n2", x, h, ones, ada, sg, 1, store=scr["x"])
        with ExitStack() as c2:
            tok = buf(c2, "tok", [P, TB + 1, VW])
            mask = buf(c2, "mask", [P, mask_at(TB)])
            cnt, seln = (buf(c2, n, [NB, 1]) for n in ("cnt", "seln"))
            att = h
            with ExitStack() as c3:
                pj = buf(c3, "pj", [P, AT, TOK])
                project_attention(nc, d, o, scr, paged, h, pj, tok)
                index_scores(nc, d, scr, pj, tok, ones, ident, mask)
            with ExitStack() as c3:
                S = buf(c3, "S", [P, KT, TOK])
                ssd_branch(nc, d, o, scr, h, tok, ones, ident, S, mask)
                ssd_gate(nc, d, scr, h, S, mask, cnt, seln)
            kv = buf(c2, "kv", [P, NB, 2, 2, NKV * HD])
            brows = buf(c2, "brows", [P, NB, 2, NH])
            with ExitStack() as c3:
                bias = buf(c3, "bias", [P, NH, WIN])
                tables(nc, d, scr, bias)
                sample_gather(nc, d, scr, h, ident, gathered, kv, brows)
                pj = buf(c3, "qk", [P, QI0, TOK])
                attend(nc, scr, pj, tok, mask, bias, ident, att)
                sample_attend(nc, d, scr, pj, tok, ones, ident, cnt, seln, kv, brows, att)
        x = buf(ctx, "x3", [P, KT, TOK])
        with ExitStack() as c2:
            A = buf(c2, "A", [P, KT, TOK])
            attention_out(nc, d, scr, att, A)
            mix_out(nc, d, scr["x"], x, A, ada)
        norm_mod(nc, "n3", x, h, ones, ada, sg, 2)
        ffn(nc, "f2", d["w_f2i"], d["w_f2o"], x, h, ada, 2)
        final_norm(nc, o, x, h, ones, d["norm_final"])


def tiled(w, cols):
    k, m = w.shape
    return np.ascontiguousarray(w.reshape(k // P, P, m // cols, cols).transpose(2, 1, 0, 3))


def fmajor(a):
    r, f = a.shape
    return np.ascontiguousarray(a.T.reshape(f // P, P, r).transpose(1, 0, 2))


def layout(i):
    a = {}
    a["x"] = fmajor(np.concatenate([i["x_prompt"][0], i["x_sample"][:, 0]], 0))
    a["c"] = fmajor(np.concatenate([i["c_prompt"], i["c_sample"]], 0))
    a["w_ada"] = tiled(i["w_ada"][0], P)
    a["b_ada"] = np.ascontiguousarray(i["b_ada"][0].reshape(NA, P).T)
    gains = np.stack([i["norm_ffn1"][0], i["norm_mix"][0], i["norm_ffn2"][0]])
    a["gains"] = np.ascontiguousarray(gains.reshape(3, KT, P).transpose(2, 0, 1))
    for n in (1, 2):
        wi = tiled(i[f"w_ffn{n}_in"][0], P)
        a[f"w_f{n}i"] = np.ascontiguousarray(np.stack([wi[:FT], wi[FT:]], 2)).reshape(FT, P, 2 * KT * P)
        wo = tiled(i[f"w_ffn{n}_out"][0], P)
        a[f"w_f{n}o"] = np.ascontiguousarray(wo.reshape(KT, P, 2, FT // 2, P).transpose(0, 2, 1, 3, 4)).reshape(2 * KT, P, FT // 2, P)
    cut = np.cumsum([0, NH * HD, NKV * HD, NKV * HD, NIH * ID, ID, NIH, DI, CONVD, SH, DM, DM])
    q, k, v, qi, ki, wi, z, xbc, dt, ga, gs = (i["w_in"][0][:, cut[n]:cut[n + 1]] for n in range(11))
    q = q[:, HEADCOLS]
    a["w_att"] = tiled(np.concatenate([q, k, qi, ki, ki], 1), P)
    wt = np.concatenate([v, wi, dt], 1)
    a["w_tok"] = np.ascontiguousarray(wt.reshape(KT, P, VW).transpose(1, 0, 2))
    a["w_ao"] = tiled(i["w_attn_out"][0][HEADCOLS], P)
    a["w_ga"] = tiled(ga, P)
    a["w_gs"] = tiled(gs, P)
    a["w_out"] = tiled(i["w_out"][0], P)
    xt, zt = tiled(xbc, P)[ORDER].reshape(SG, XT, P, KT, P), tiled(z, P).reshape(SG, 4, P, KT, P)
    a["w_ssd"] = np.concatenate([xt, zt], 1)
    a["w_so"] = np.ascontiguousarray(i["w_ssd_out"][0].reshape(SG, 4, P, KT, P).transpose(0, 3, 2, 1, 4))
    ctile = lambda v: v.reshape(v.shape[:-1] + (CONVD // P, P))[..., ORDER, :]
    a["conv_w"] = np.ascontiguousarray(ctile(i["conv_w"][0]).transpose(2, 1, 0))
    a["conv_b"] = np.ascontiguousarray(ctile(i["conv_b"][0]).T)
    sc = i["state_conv"][0]
    a["state_conv"] = np.ascontiguousarray(ctile(sc).reshape(NB, CW - 1, SG, XT, P).transpose(2, 4, 3, 1, 0))
    a["conv_old"] = np.ascontiguousarray(sc[:, 1:])
    a["dt_bias"] = np.ascontiguousarray(np.broadcast_to(i["dt_bias"][0], (P, SH)))
    a["a_log"] = np.ascontiguousarray(np.broadcast_to(i["a_log"][0], (P, SH)))
    a["upper"] = np.triu(np.ones((P, P), np.float32))
    a["below"] = np.tril(np.ones((P, P), np.float32), -1)
    a["d_skip"] = np.ascontiguousarray(np.repeat(i["d_skip"][0], DI // SH).reshape(DI // P, P).T)
    a["norm_ssd"] = np.ascontiguousarray(i["norm_ssd"][0].reshape(DI // P, P).T)
    a["norm_final"] = np.ascontiguousarray(i["norm_final"].reshape(KT, P).T)
    ssm = i["state_ssm"][0].reshape(NB, SG, 4, P, DS)
    a["state_ssm"] = np.ascontiguousarray(ssm.transpose(1, 3, 2, 0, 4)).reshape(SG, P, 4 * NB * DS)
    a["cache_kidx"] = np.ascontiguousarray(i["cache_kidx"][0].transpose(0, 2, 1)).reshape(2 * NPOOL, ID * PAGE // 2)
    a["cache_k"] = np.ascontiguousarray(i["cache_k"][0].reshape(NPOOL * PAGE, NKV * HD))
    a["cache_v"] = np.ascontiguousarray(i["cache_v"][0].reshape(NPOOL * PAGE, NKV * HD))
    a["page_table"] = np.ascontiguousarray(i["page_table"].reshape(1, NB * NPAGE))
    a["half"] = (np.arange(P)[:, None] // HD == np.arange(2)[None, :]).astype(np.float32)
    a["iota"] = np.ascontiguousarray(np.broadcast_to(np.arange(TOPK, dtype=np.float16), (P, TOPK)))
    slots = np.zeros((P, NB, NPAGE, 3), np.float16)
    slots[..., 0] = np.arange(P)[:, None, None]
    slots[..., 2] = np.arange(NPAGE)
    a["slots"] = slots.reshape(P, NB * NPAGE, 3)
    a["slot"] = (np.arange(P)[:, None] + P * np.arange(2)[None, :]).astype(np.float32)
    a["rel_bias"] = np.ascontiguousarray(i["rel_bias"][:, HEADS])
    a["flip"] = np.ascontiguousarray(np.eye(P, dtype=np.float32)[::-1])
    a["ident"] = np.eye(P, dtype=np.float32)
    dist = np.maximum(255 - np.arange(512), 0)
    far = NBUCKET // 2 + (np.log(np.maximum(dist, 1).astype(np.float32) / (NBUCKET // 2)) / np.log(MAXD / (NBUCKET // 2))
                          * (NBUCKET - NBUCKET // 2)).astype(np.int32)
    bucket = np.where(dist < NBUCKET // 2, dist, np.minimum(far, NBUCKET - 1))
    a["hot"] = (np.arange(NBUCKET)[:, None] == bucket[None, :]).astype(np.float32)
    return a


HEADS = np.array([4 * (2 * m + u) + g for m in range(2) for g in range(4) for u in range(2)])
HEADCOLS = (HEADS[:, None] * HD + np.arange(HD)).reshape(-1)

OUTS = {"k": [P, 2, TOK], "kidx": [ID, TOK], "v_p": [P, TB, NKV * HD], "v_s": [NB, NKV * HD], "y": [P, KT, TOK],
        "conv_p": [SG, P, XT, CW - 1], "conv_s": [SG, P, XT, NB], "conv_old": [NB, CW - 2, CONVD], "ssm_p": [SG, P, DI // SG],
        "ssm_s": [SG, P, 4 * NB * DS]}
ORDER = np.concatenate([np.concatenate([np.arange(4) + 4 * g, [16 + g], [20 + g]]) for g in range(SG)])


def unlay(r):
    y = r["y"].transpose(2, 1, 0).reshape(TOK, DM)
    k = r["k"].transpose(2, 1, 0).reshape(TOK, NKV, HD)
    kidx = r["kidx"].T
    v = r["v_p"].transpose(1, 0, 2).reshape(1, 1, SEQ, NKV, HD)
    back = np.argsort(ORDER)
    conv_p = r["conv_p"].transpose(3, 0, 2, 1).reshape(CW - 1, SG * XT, P)[:, back].reshape(1, 1, CW - 1, CONVD)
    new = r["conv_s"].transpose(3, 0, 2, 1).reshape(NB, SG * XT, P)[:, back].reshape(NB, 1, CONVD)
    conv_s = np.concatenate([r["conv_old"], new], 1)[None]
    R, PD = SH // SG, DI // SH
    ssm_p = r["ssm_p"].reshape(SG, DS, R, PD).transpose(0, 2, 3, 1).reshape(1, 1, SH, PD, DS)
    ssm_s = r["ssm_s"].reshape(SG, 2, PD, R // 2, NB, DS).transpose(4, 0, 3, 1, 2, 5).reshape(1, NB, SH, PD, DS)
    out = (y[:SEQ][None], y[SEQ:][:, None], k[:SEQ][None, None], v, kidx[:SEQ][None, None], ssm_p, conv_p,
           k[SEQ:].reshape(1, NB, 1, NKV, HD), r["v_s"].reshape(1, NB, 1, NKV, HD), kidx[SEQ:].reshape(1, NB, 1, ID),
           ssm_s, conv_s)
    return tuple(np.ascontiguousarray(a) for a in out)


def kernel(**inputs):
    import concourse.bacc as bacc
    from concourse.bass_utils import run_bass_kernel_spmd

    nc = bacc.Bacc("TRN2", target_bir_lowering=False, num_devices=1)
    arrays = layout({n: np.asarray(a) for n, a in inputs.items()})
    d = {n: nc.dram_tensor(f"in_{n}", a.shape, mybir.dt.from_np(a.dtype), kind="ExternalInput").ap() for n, a in arrays.items()}
    o = {n: nc.dram_tensor(f"out_{n}", s, F32, kind="ExternalOutput").ap() for n, s in OUTS.items()}
    program(nc, d, o)
    r = run_bass_kernel_spmd(nc, [{f"in_{n}": a for n, a in arrays.items()}], core_ids=[0])
    return unlay({n: r.results[0][f"out_{n}"] for n in OUTS})
```

```python
from contextlib import ExitStack

import numpy as np

import concourse.bass as bass
from concourse import mybir

P = 128
DM, SEQ, NB = 1024, 1024, 8
TOK = SEQ + NB
NCH = 3
NC = TOK // NCH
LASTP = NC - NB
KT = DM // P
TB = SEQ // P
DFF = 2816
FT = DFF // P
NH, HD, NKV = 16, 64, 4
NIH, ID = 8, 64
TOPK = 256
PAST, PAGE, NPAGE, NPOOL = 4096, 128, 32, 320
NBUCKET, MAXD = 32, 128
DI, SH, SG, DS, CW = 2048, 32, 4, 128, 4
CONVD = DI + 2 * SG * DS
XT = 6
EPS = 1e-6
AT = 15
QT0, KT0, QI0, KI0 = 0, 8, 10, 14
VW = NKV * HD + NIH + SH
BIG = 1.0e30
CAUSAL, TAKEN = -3.0e38, -3.3e38
WIN = 2 * P
NA = 9 * KT
NCOND = 1 + NB

F32 = mybir.dt.float32
F16 = mybir.dt.float16
I32 = mybir.dt.int32
U32 = mybir.dt.uint32
ALU = mybir.AluOpType
ACT = mybir.ActivationFunctionType
AX = mybir.AxisListType.X


class Chain:

    def __init__(self, eng, sem, tick=None):
        self.eng, self.sem, self.tick, self.n, self.off = eng, sem, tick, 0, 0

    def link(self, ins):
        self.n += 1
        ins.then_inc(self.sem, 1)
        self.eng.wait_ge(self.sem, UP + self.off + self.n)
        if self.tick is not None:
            self.eng.sem_inc(self.tick, 1)

    def loop(self, i, per):
        self.off, self.start, self.per = i * per, self.n, per

    def done(self, times):
        assert self.n - self.start == self.per, (self.n - self.start, self.per)
        self.off, self.n = 0, self.start + self.per * times


def carve(arena, at, shape):
    n = int(np.prod(shape[1:]))
    a = arena[0:shape[0], at:at + n]
    assert at + n <= arena.shape[1], (at, n)
    names = "abcd"[:len(shape) - 1]
    if len(names) > 1:
        a = a.rearrange(f"p ({' '.join(names)}) -> p {' '.join(names)}", **dict(zip(names, shape[1:])))
    return at + n, a


UP = 1


class Phase:
    shared = []

    @classmethod
    def share(cls, nc, ctx, n):
        cls.shared = [ctx.enter_context(nc.semaphore(f"stage{i}")) for i in range(n)]
        for s in cls.shared:
            nc.gpsimd.sem_inc(s, UP)
        nc.all_engine_barrier()

    def __init__(self, nc, name, arena=None, start=0, banks=None):
        self.nc, self.name, self.ctx, self.arena, self.at = nc, name, ExitStack(), arena, start
        self.banks, self.bank, self.used, self.blocks = banks, 0, {}, ExitStack()

    def __enter__(self):
        return self

    def __exit__(self, *a):
        self.blocks.__exit__(*a)
        for s in self.used.values():
            self.nc.gpsimd.sem_clear(s)
            self.nc.gpsimd.sem_inc(s, UP)
        self.nc.all_engine_barrier()
        return self.ctx.__exit__(*a)

    def sem(self, name):
        assert name not in self.used
        self.used[name] = self.shared[len(self.used)]
        return self.used[name]

    def sb(self, name, shape, dt=F32):
        if self.arena is not None:
            self.at, a = carve(self.arena, self.at, shape)
            return a
        return self.ctx.enter_context(self.nc.sbuf_tensor(f"{self.name}_{name}", shape, dt))

    def ps(self, name, shape, dt=F32):
        if self.banks is not None:
            n, a = carve(self.banks, self.bank, shape)
            self.bank = -(-n // 512) * 512
            return a
        return self.ctx.enter_context(self.nc.psum_tensor(f"{self.name}_{name}", shape, dt))

    def block(self):
        return self.blocks.enter_context(self.nc.Block())


ADA_STEP = 4
ADA_LATE = FT // 2 * ADA_STEP
ADA_EARLY = NA - ADA_LATE
assert ADA_EARLY >= 3 * KT and ADA_EARLY % ADA_STEP == 0


def halve_gate(nc, sem, ada, s):
    gate = ada[:, (3 * s + 2) * KT:(3 * s + 3) * KT]
    nc.vector.tensor_scalar(gate, gate, 0.5, None, ALU.mult).then_inc(sem, 1)


def modulated_gain(dve, nc, sem, ada, sg, gains, s, n):
    scale = ada[:, (3 * s + 1) * KT:(3 * s + 2) * KT]
    nc.vector.tensor_scalar(sg[:, s], scale, 1.0, None, ALU.add).then_inc(sem, 1)
    dve.wait_ge(sem, UP + n + 1)
    nc.vector.tensor_tensor(sg[:, s], sg[:, s], gains[:, s].unsqueeze(2).to_broadcast([P, KT, NCOND]), ALU.mult).then_inc(sem, 1)


def first_norm(nc, d, x, h, ones, ident, c, b_ada, gains, ada, sg):
    ROUNDS = ADA_EARLY // ADA_STEP
    with Phase(nc, "n1") as ph:
        w = ph.sb("w", [P, 2, ADA_STEP, KT, P])
        sq = ph.sb("sq", [P, 2, TOK])
        rstd = ph.sb("rstd", [P, TOK])
        smp = ph.sb("smp", [P, KT, NB])
        eps = ph.sb("eps", [P, 1])
        ps = ph.ps("ps", [P, NCH, 512])
        pa = [ph.ps(f"pa{q}", [P, ADA_STEP, NCOND]) for q in range(2)]
        p9 = [ph.ps(f"p9{q}", [NCOND, ADA_STEP, P]) for q in range(2)]
        row = ph.sb("row", [NCOND, 2, ADA_STEP, P])
        copied = ph.sem("copied")
        w_in = [ph.sem(f"w_in{q}") for q in range(2)]
        x_in = [ph.sem(f"x_in{k}") for k in range(KT)]
        turned = ph.sem("turned")
        c_in, c_act, mm, evac, fix, ones_set, squared, summed, root, inv, scaled, modded, smp_mod, eps_set = (
            ph.sem(n) for n in ("c_in", "c_act", "mm", "evac", "fix", "ones_set", "squared", "summed", "root", "inv", "scaled",
                                "modded", "smp_mod", "eps_set"))
        block = ph.block()

        def load(sp, r):
            src = d["w_ada"][r * ADA_STEP:(r + 1) * ADA_STEP].rearrange("t p k m -> p t k m")
            sp.dma_start(w[:, r % 2].rearrange("p t k m -> p t (k m)"), src.rearrange("p t k m -> p t (k m)")).then_inc(w_in[r % 2], 16)

        @block.sync
        def _(sp):
            for k in range(KT):
                sp.dma_start(x[:, k], d["x"][:, k]).then_inc(x_in[k], 16)
            for r in range(ROUNDS):
                if r >= 2:
                    sp.wait_ge(mm, UP + r - 1)
                load(sp, r)

        @block.gpsimd
        def _(pool):
            nc.gpsimd.memset(ones[:], 1.0).then_inc(ones_set, 1)

        @block.scalar
        def _(act):
            act.dma_start(c[:], d["c"]).then_inc(c_in, 16)
            act.dma_start(b_ada[:], d["b_ada"]).then_inc(c_in, 16)
            act.dma_start(gains[:], d["gains"]).then_inc(c_in, 16)
            act.dma_start(ident[:], d["ident"]).then_inc(c_in, 16)
            act.wait_ge(c_in, UP + 64)
            nc.scalar.activation(c[:], c[:], ACT.Silu).then_inc(c_act, 1)
            for k in range(KT):
                act.wait_ge(x_in[k], UP + 16)
                if k >= 2:
                    act.wait_ge(summed, UP + k - 1)
                nc.scalar.activation(sq[:, k % 2], x[:, k], ACT.Square).then_inc(squared, 1)
            act.wait_ge(summed, UP + KT)
            act.wait_ge(eps_set, UP + 1)
            nc.scalar.activation(rstd[:].rearrange("p (n c) -> p n c", n=NCH), ps[:, :, 0:NC], ACT.Sqrt,
                                 scale=1.0 / DM, bias=eps[:]).then_inc(root, 1)
            act.wait_ge(fix, UP + 2)
            for k in range(KT):
                act.wait_ge(scaled, UP + k + 1)
                nc.scalar.activation(h[:, k, 0:SEQ], h[:, k, 0:SEQ], ACT.Identity,
                                     scale=sg[:, 0, k, 0:1], bias=ada[:, k, 0:1]).then_inc(modded, 1)
            act.wait_ge(modded, UP + KT)

        @block.tensor
        def _(pe):
            pe.wait_ge(ones_set, UP + 1)
            for k in range(KT):
                pe.wait_ge(squared, UP + k + 1)
                for n in range(NCH):
                    m = nc.tensor.matmul(ps[:, n, 0:NC], ones[:], sq[:, k % 2, n * NC:(n + 1) * NC],
                                         start=k == 0, stop=k == KT - 1)
                m.then_inc(summed, 1)
            pe.wait_ge(c_act, UP + 1)

            def turn(r):
                pe.wait_ge(copied, UP + r + 1)
                if r >= 2:
                    pe.wait_ge(evac, UP + r - 1)
                for t in range(ADA_STEP):
                    m = nc.tensor.transpose(pa[r % 2][:, t], row[:, r % 2, t], ident[0:NCOND, 0:NCOND])
                m.then_inc(turned, 1)

            for r in range(ROUNDS):
                pe.wait_ge(w_in[r % 2], UP + 16 * (r // 2 + 1))
                if r >= 2:
                    pe.wait_ge(copied, UP + r - 1)
                for k in range(KT):
                    m = nc.tensor.matmul(p9[r % 2][:], c[:, k], w[:, r % 2, :, k], start=k == 0, stop=k == KT - 1)
                m.then_inc(mm, 1)
                if r >= 1:
                    turn(r - 1)
            turn(ROUNDS - 1)

        @block.vector
        def _(dve):
            nc.vector.memset(eps[:], EPS).then_inc(eps_set, 1)
            dve.wait_ge(root, UP + 1)
            nc.vector.reciprocal(rstd[:], rstd[:]).then_inc(inv, 1)
            dve.wait_ge(inv, UP + 1)
            for k in range(KT):
                nc.vector.tensor_tensor(h[:, k], x[:, k], rstd[:], ALU.mult).then_inc(scaled, 1)
            dve.wait_ge(c_in, UP + 64)

            def copy(r):
                dve.wait_ge(mm, UP + r + 1)
                if r >= 2:
                    dve.wait_ge(turned, UP + r - 1)
                nc.vector.tensor_copy(row[:, r % 2], p9[r % 2][:]).then_inc(copied, 1)

            copy(0)
            for r in range(ROUNDS):
                if r + 1 < ROUNDS:
                    copy(r + 1)
                dve.wait_ge(turned, UP + r + 1)
                at = slice(r * ADA_STEP, (r + 1) * ADA_STEP)
                nc.vector.tensor_tensor(ada[:, at], pa[r % 2][:], b_ada[:, at].unsqueeze(2).to_broadcast([P, ADA_STEP, NCOND]),
                                        ALU.add).then_inc(evac, 1)
                if (r + 1) * ADA_STEP == 2 * KT:
                    dve.wait_ge(evac, UP + r + 1)
                    modulated_gain(dve, nc, fix, ada, sg, gains, 0, 0)
            dve.wait_ge(evac, UP + ROUNDS)
            halve_gate(nc, fix, ada, 0)
            dve.wait_ge(fix, UP + 3)
            dve.wait_ge(scaled, UP + KT)
            nc.vector.tensor_tensor(smp[:], h[:, :, SEQ:TOK], sg[:, 0, :, 1:NCOND], ALU.mult).then_inc(smp_mod, 1)
            dve.wait_ge(smp_mod, UP + 1)
            nc.vector.tensor_tensor(h[:, :, SEQ:TOK], smp[:], ada[:, 0:KT, 1:NCOND], ALU.add).then_inc(smp_mod, 1)
            dve.wait_ge(smp_mod, UP + 2)


def norm_mod(nc, name, x, h, ones, ada, sg, s, store=None):
    with Phase(nc, name) as ph:
        sq = ph.sb("sq", [P, 2, TOK])
        rstd = ph.sb("rstd", [P, TOK])
        smp = ph.sb("smp", [P, KT, NB])
        eps = ph.sb("eps", [P, 1])
        ps = ph.ps("ps", [P, NCH, 512])
        squared, summed, root, inv, scaled, modded, smp_mod, eps_set, saved = (
            ph.sem(n) for n in ("squared", "summed", "root", "inv", "scaled", "modded", "smp_mod", "eps_set", "saved"))
        block = ph.block()

        @block.sync
        def _(sp):
            if store is not None:
                sp.dma_start(store, x[:]).then_inc(saved, 16)
                sp.wait_ge(saved, UP + 16)

        @block.scalar
        def _(act):
            for k in range(KT):
                if k >= 2:
                    act.wait_ge(summed, UP + k - 1)
                nc.scalar.activation(sq[:, k % 2], x[:, k], ACT.Square).then_inc(squared, 1)
            act.wait_ge(summed, UP + KT)
            act.wait_ge(eps_set, UP + 1)
            nc.scalar.activation(rstd[:].rearrange("p (n c) -> p n c", n=NCH), ps[:, :, 0:NC], ACT.Sqrt,
                                 scale=1.0 / DM, bias=eps[:]).then_inc(root, 1)
            for k in range(KT):
                act.wait_ge(scaled, UP + k + 1)
                nc.scalar.activation(h[:, k, 0:SEQ], h[:, k, 0:SEQ], ACT.Identity,
                                     scale=sg[:, s, k, 0:1], bias=ada[:, 3 * s * KT + k, 0:1]).then_inc(modded, 1)
            act.wait_ge(modded, UP + KT)

        @block.tensor
        def _(pe):
            for k in range(KT):
                pe.wait_ge(squared, UP + k + 1)
                for n in range(NCH):
                    m = nc.tensor.matmul(ps[:, n, 0:NC], ones[:], sq[:, k % 2, n * NC:(n + 1) * NC],
                                         start=k == 0, stop=k == KT - 1)
                m.then_inc(summed, 1)

        @block.vector
        def _(dve):
            nc.vector.memset(eps[:], EPS).then_inc(eps_set, 1)
            dve.wait_ge(root, UP + 1)
            nc.vector.reciprocal(rstd[:], rstd[:]).then_inc(inv, 1)
            dve.wait_ge(inv, UP + 1)
            for k in range(KT):
                nc.vector.tensor_tensor(h[:, k], x[:, k], rstd[:], ALU.mult).then_inc(scaled, 1)
            dve.wait_ge(scaled, UP + KT)
            nc.vector.tensor_tensor(smp[:], h[:, :, SEQ:TOK], sg[:, s, :, 1:NCOND], ALU.mult).then_inc(smp_mod, 1)
            dve.wait_ge(smp_mod, UP + 1)
            nc.vector.tensor_tensor(h[:, :, SEQ:TOK], smp[:], ada[:, 3 * s * KT:(3 * s + 1) * KT, 1:NCOND],
                                    ALU.add).then_inc(smp_mod, 1)
            dve.wait_ge(smp_mod, UP + 2)


def ffn(nc, name, w_in_d, w_out_d, x, h, ada, s, late=None):
    with Phase(nc, name) as ph:
        a = ph.sb("a", [P, FT, TOK])
        w = ph.sb("w", [P, 2, 2 * KT * P])
        wo = ph.sb("wo", [P, 2, FT // 2, P])
        g = ph.sb("g", [P, NCH, NC])
        smp = ph.sb("smp", [P, 2, NB])
        ps = [ph.ps(f"ps{n}", [P, 2, 512]) for n in range(NCH)]
        w_in = [ph.sem(f"w_in{q}") for q in range(2)]
        wo_in = [ph.sem(f"wo_in{q}") for q in range(2)]
        mm, silued, acted, wo_used, added, smped = (
            ph.sem(n) for n in ("mm", "silued", "acted", "wo_used", "added", "smped"))
        wv = w[:].rearrange("p q (u k m) -> p q u k m", u=2, k=KT)
        if late is not None:
            wa = ph.sb("wa", [P, ADA_STEP, KT, P])
            pa = ph.ps("pa", [P, ADA_STEP, NCOND])
            wa_in, ma, evac, fix = (ph.sem(n) for n in ("wa_in", "ma", "evac", "fix"))
        block = ph.block()
        HK = FT // 2
        if late is not None:
            d, c, b_ada, gains, sg = late

        def load_ada(sp, i):
            at = bass.ds(ADA_EARLY + ADA_STEP * i, ADA_STEP)
            sp.dma_start(wa[:].rearrange("p t k m -> p t (k m)"), d["w_ada"][at].rearrange("t p k m -> p t (k m)")).then_inc(wa_in, 16)

        @block.sync
        def _(sp):
            if late is not None:
                load_ada(sp, 0)
            for q in range(2):
                sp.dma_start(w[:, q], w_in_d[q]).then_inc(w_in[q], 16)
            for q in range(2):
                sp.dma_start(wo[:, q], w_out_d[q]).then_inc(wo_in[q], 16)
            with sp.Fori(1, FT // 2) as i:
                for q in range(2):
                    sp.wait_ge(mm, UP + NCH * (2 * (i - 1) + q + 1))
                    sp.dma_start(w[:, q], w_in_d[2 * i + q]).then_inc(w_in[q], 16)
                if late is not None:
                    sp.wait_ge(ma, UP + i)
                    load_ada(sp, i)
            with sp.Fori(1, KT) as i:
                for q in range(2):
                    sp.wait_ge(wo_used, UP + 2 * (i - 1) + q + 1)
                    sp.dma_start(wo[:, q], w_out_d[2 * i + q]).then_inc(wo_in[q], 16)

        @block.tensor
        def _(pe):
            with pe.Fori(0, FT // 2) as i:
                for q in range(2):
                    pe.wait_ge(w_in[q], UP + 16 * (i + 1))
                    for n in range(NCH):
                        pe.wait_ge(acted, UP + 2 * NCH * i + (n + 1 if q else 0))
                        for u in range(2):
                            for k in range(KT):
                                m = nc.tensor.matmul(ps[n][:, u, 0:NC], wv[:, q, u, k], h[:, k, n * NC:(n + 1) * NC],
                                                     start=k == 0, stop=k == KT - 1)
                        m.then_inc(mm, 1)
                if late is not None:
                    pe.wait_ge(wa_in, UP + 16 * (i + 1))
                    pe.wait_ge(evac, UP + i)
                    for t in range(ADA_STEP):
                        for k in range(KT):
                            m = nc.tensor.matmul(pa[:, t], wa[:, t, k], c[:, k], start=k == 0, stop=k == KT - 1)
                    m.then_inc(ma, 1)
            pe.wait_ge(acted, UP + FT * NCH)
            with pe.Fori(0, KT // 2) as i:
                for q in range(2):
                    pe.wait_ge(added, UP + 2 * i)
                    for hf in range(2):
                        pe.wait_ge(wo_in[hf], UP + 32 * i + 16 * (q + 1))
                        for n in range(NCH):
                            for k in range(HK):
                                m = nc.tensor.matmul(ps[n][:, q, 0:NC], wo[:, hf, k], a[:, hf * HK + k, n * NC:(n + 1) * NC],
                                                     start=hf == 0 and k == 0, stop=hf == 1 and k == HK - 1)
                        m.then_inc(wo_used, 1)

        @block.scalar
        def _(act):
            with act.Fori(0, FT) as i:
                for n in range(NCH):
                    act.wait_ge(mm, UP + NCH * i + n + 1)
                    act.wait_ge(acted, UP + NCH * i)
                    nc.scalar.activation(g[:, n], ps[n][:, 0, 0:NC], ACT.Silu).then_inc(silued, 1)

        @block.vector
        def _(dve):
            with dve.Fori(0, FT // 2) as i:
                for q in range(2):
                    for n in range(NCH):
                        dve.wait_ge(silued, UP + NCH * (2 * i + q) + n + 1)
                        nc.vector.tensor_tensor(a[:, 2 * i + q, n * NC:(n + 1) * NC], g[:, n], ps[n][:, 1, 0:NC],
                                                ALU.mult).then_inc(acted, 1)
                if late is not None:
                    dve.wait_ge(ma, UP + i + 1)
                    at = bass.ds(ADA_EARLY + ADA_STEP * i, ADA_STEP)
                    nc.vector.tensor_tensor(ada[:, at], pa[:], b_ada[:, at].unsqueeze(2).to_broadcast([P, ADA_STEP, NCOND]),
                                            ALU.add).then_inc(evac, 1)
            if late is not None:
                dve.wait_ge(evac, UP + FT // 2)
                modulated_gain(dve, nc, fix, ada, sg, gains, 1, 0)
                modulated_gain(dve, nc, fix, ada, sg, gains, 2, 2)
                halve_gate(nc, fix, ada, 2)
            gate = (3 * s + 2) * KT
            with dve.Fori(0, KT // 2) as i:
                for q in range(2):
                    t = 2 * i + q
                    dve.wait_ge(wo_used, UP + 4 * i + 2 * q + 2)
                    nc.vector.tensor_tensor(smp[:, q], ps[2][:, q, LASTP:NC], ada[:, gate + t, 1:NCOND],
                                            ALU.mult).then_inc(smped, 1)
                    for n in range(NCH):
                        c = NC if n < NCH - 1 else LASTP
                        v = nc.vector.scalar_tensor_tensor(
                            out=x[:, t, n * NC:n * NC + c], in0=ps[n][:, q, 0:c], scalar=ada[:, bass.ds(gate + t, 1), 0:1].rearrange("p a b -> p (a b)"),
                            in1=x[:, t, n * NC:n * NC + c], op0=ALU.mult, op1=ALU.add)
                    dve.wait_ge(smped, UP + 2 * i + q + 1)
                    nc.vector.tensor_tensor(x[:, t, SEQ:TOK], x[:, t, SEQ:TOK], smp[:, q], ALU.add).then_inc(added, 1)
            dve.wait_ge(added, UP + KT)


def load_tiles(eng, slots, w_in, used, per, src, n):
    for q in range(2):
        eng.dma_start(slots[:, q], src[q]).then_inc(w_in[q], 16)
    with eng.Fori(1, n // 2) as i:
        for q in range(2):
            eng.wait_ge(used, UP + per * (2 * (i - 1) + q + 1))
            eng.dma_start(slots[:, q], src[2 * i + q]).then_inc(w_in[q], 16)
    if n % 2:
        eng.wait_ge(used, UP + per * (n - 2))
        eng.dma_start(slots[:, 0], src[n - 1]).then_inc(w_in[0], 16)


def project_tiles(pe, nc, slots, ps, rhs, w_in, mm, read, n, kt=KT, made=None):
    def tile(i, q):
        pe.wait_ge(w_in[q], UP + 16 * (i + 1))
        for c in range(NCH):
            if c == 0:
                pe.wait_ge(read[q], UP + NCH * i)
            if made is not None and q == 0:
                pe.wait_ge(made[0], UP + made[1] * (c + 1))
            for k in range(kt):
                m = nc.tensor.matmul(ps[q][:, c, 0:NC], slots[:, q, k], rhs[:, k, c * NC:(c + 1) * NC],
                                     start=k == 0, stop=k == kt - 1)
            m.then_inc(mm, 1)

    with pe.Fori(0, n // 2) as i:
        for q in range(2):
            tile(i, q)
    if n % 2:
        tile(n // 2, 0)


def copy_tiles(act, nc, dst, ps, mm, read, n):
    def tile(i, q):
        for c in range(NCH):
            act.wait_ge(mm, UP + NCH * (2 * i + q) + c + 1)
            nc.scalar.activation(dst[:, 2 * i + q, c * NC:(c + 1) * NC], ps[q][:, c, 0:NC], ACT.Copy).then_inc(read[q], 1)

    with act.Fori(0, n // 2) as i:
        for q in range(2):
            tile(i, q)
    if n % 2:
        tile(n // 2, 0)


def project_attention(nc, d, o, scr, paged, h, pj, tok):
    with Phase(nc, "pja") as ph:
        w = ph.sb("w", [P, 2, KT, P])
        wt = ph.sb("wt", [P, KT, VW])
        ps = [ph.ps(f"ps{q}", [P, NCH, 512]) for q in range(2)]
        pt = ph.ps("pt", [P, 2, 512])
        tab = ph.sb("tab", [P, 2], I32)
        tabf = ph.sb("tabf", [P, 2])
        rows = ph.sb("rows", [P, 2, 2], U32)
        pages = ph.sb("pages", [P, 2, ID * PAGE // 2])
        tab_in, tabbed = ph.sem("tab_in"), ph.sem("tabbed")
        w_in = [ph.sem(f"w_in{q}") for q in range(2)]
        read = [ph.sem(f"read{q}") for q in range(2)]
        mm, wt_in, tmm, tread, saved, qk_saved = (ph.sem(n) for n in ("mm", "wt_in", "tmm", "tread", "saved", "qk_saved"))
        block = ph.block()

        @block.sync
        def _(sp):
            with nc.allow_non_contiguous_dma(reason="256 page numbers"):
                sp.dma_start(tab[:], d["page_table"].rearrange("o (c p) -> p (o c)", c=2)).then_inc(tab_in, 16)
            sp.dma_start(wt[:], d["w_tok"]).then_inc(wt_in, 16)
            load_tiles(sp, w, w_in, mm, NCH, d["w_att"], AT)
            sp.wait_ge(read[0], UP + NCH * (AT - AT // 2))
            sp.wait_ge(read[1], UP + NCH * (AT // 2))
            sp.wait_ge(tread, UP + TB + 1)
            sp.dma_start(o["k"], pj[:, KT0:KT0 + 2]).then_inc(saved, 16)
            sp.dma_start(o["kidx"], pj[0:ID, KI0]).then_inc(saved, 16)
            sp.dma_start(o["v_p"], tok[:, 0:TB, 0:NKV * HD]).then_inc(saved, 16)
            sp.dma_start(o["v_s"], tok[0:NB, TB, 0:NKV * HD]).then_inc(saved, 16)
            sp.wait_ge(saved, UP + 64)

        @block.gpsimd
        def _(pool):
            pool.wait_ge(tabbed, UP + 5)
            n = 0
            for f in range(2):
                for c in range(2):
                    if n >= 2:
                        pool.wait_ge(paged, 16 * (2 * n - 2))
                    pool.indirect_dma_start(pages[:, c], None, d["cache_kidx"], bass.IndirectOffsetOnAxis(rows[:, f, c:c + 1], 0)).then_inc(paged, 16)
                    n += 1
                    pool.wait_ge(paged, 16 * (2 * n - 1))
                    pool.dma_start(scr["kidx"][c * P:(c + 1) * P, f], pages[:, c]).then_inc(paged, 16)
            pool.wait_ge(paged, 16 * 2 * n)

        @block.tensor
        def _(pe):
            project_tiles(pe, nc, w, ps, h, w_in, mm, read, AT)
            pe.wait_ge(wt_in, UP + 16)
            for t in range(TB + 1):
                rows = P if t < TB else NB
                if t >= 2:
                    pe.wait_ge(tread, UP + t - 1)
                for k in range(KT):
                    m = nc.tensor.matmul(pt[0:rows, t % 2, 0:VW], h[:, k, t * P:t * P + rows], wt[:, k],
                                         start=k == 0, stop=k == KT - 1)
                m.then_inc(tmm, 1)

        @block.scalar
        def _(act):
            copy_tiles(act, nc, pj, ps, mm, read, AT)
            act.wait_ge(read[0], UP + NCH * (AT - AT // 2))
            act.wait_ge(read[1], UP + NCH * (AT // 2))
            act.dma_start(scr["qk"], pj[:, 0:QI0]).then_inc(qk_saved, 16)
            act.wait_ge(qk_saved, UP + 16)

        @block.vector
        def _(dve):
            dve.wait_ge(tab_in, UP + 16)
            nc.vector.tensor_copy(tabf[:], tab[:]).then_inc(tabbed, 1)
            for f in range(2):
                dve.wait_ge(tabbed, UP + 1 + 2 * f)
                nc.vector.tensor_scalar(tabf[:], tabf[:], 2.0 if f == 0 else 1.0, 0.0 if f == 0 else 1.0, ALU.mult, ALU.add).then_inc(tabbed, 1)
                dve.wait_ge(tabbed, UP + 2 + 2 * f)
                nc.vector.tensor_copy(rows[:, f], tabf[:]).then_inc(tabbed, 1)
            for t in range(TB + 1):
                rows_t = P if t < TB else NB
                dve.wait_ge(tmm, UP + t + 1)
                nc.vector.tensor_copy(tok[0:rows_t, t], pt[0:rows_t, t % 2, 0:VW]).then_inc(tread, 1)


def mask_at(b):
    return P * (b * (b + 1) // 2)


FIRST = TOPK // P
CHOSEN = range(FIRST, TB)


def index_scores(nc, d, scr, pj, tok, ones, ident, mask):
    with Phase(nc, "sel") as ph:
        r = ph.sb("r", [P, 2, SEQ])
        wis = ph.sb("wis", [P, TB, NIH])
        ps = ph.ps("ps", [P, 2, SEQ])
        mm, relu, acc, zeroed, causal, scored, masked, free = (
            ph.sem(n) for n in ("mm", "relu", "acc", "zeroed", "causal", "scored", "masked", "free"))
        HP = NPAGE // 2
        kx = ph.sb("kx", [P, 2, HP, PAGE])
        qx = ph.sb("qx", [P, 2, NIH, NB])
        hot = ph.sb("hot", [P, 2])
        prod = ph.sb("prod", [P, 4, NB])
        wid = ph.sb("wid", [NB, NB, NIH])
        wib = ph.sb("wib", [P, NB, NIH])
        t = ph.sb("t", [P, HP * 2, NIH])
        tn = ph.sb("tn", [NB, NIH])
        snew = ph.sb("snew", [NB, 1])
        sc = ph.sb("sc", [P, NB, NPAGE])
        st = ph.sb("st", [P, 2, P])
        pW = ph.ps("pW", [P, 512])
        pS = [ph.ps(f"pS{q}", [P, 512]) for q in range(2)]
        k_in = [ph.sem(f"k_in{q}") for q in range(2)]
        small, prodd, widd, smm, tmp, summed, ch_s, turned, moved, stored, newd, qzero = (
            ph.sem(n) for n in ("small", "prodd", "widd", "smm", "tmp", "summed", "ch", "turned", "moved", "stored", "newd", "qzero"))
        block = ph.block()
        SC = float((NIH * ID) ** -0.5)
        pN = pW[0:NB, NB * NIH:NB * NIH + NIH]
        pT = pW[:, 0:2 * P].rearrange("p (c s) -> p c s", c=2)
        pSv = [p[:, 0:NPAGE * NIH].rearrange("p (i u h) -> p i u h", i=HP, u=2) for p in pS]

        @block.sync
        def _(sp):
            sp.dma_start(hot[:], d["half"]).then_inc(small, 16)
            sp.wait_ge(qzero, UP + 1)
            for half in range(2):
                for u in range(2):
                    sp.dma_start(qx[half * ID:(half + 1) * ID, half].rearrange("p (t u) b -> p u t b", u=2)[:, u],
                                 pj[u * ID:(u + 1) * ID, QI0:QI0 + 4, SEQ:TOK]).then_inc(small, 16)
            for b in range(NB):
                if b >= 2:
                    sp.wait_ge(smm, UP + b - 1)
                for half in range(2):
                    src = scr["kidx"][b * NPAGE + half * HP:b * NPAGE + (half + 1) * HP].rearrange("i f (d s) -> (f d) i s", s=PAGE)
                    sp.dma_start(kx[half * ID:(half + 1) * ID, b % 2], src).then_inc(k_in[b % 2], 16)
            sp.wait_ge(moved, UP + 1)
            sp.dma_start(by_page(scr["score"]), st[:]).then_inc(stored, 16)
            sp.dma_start(scr["snew"], snew[:]).then_inc(stored, 16)
            sp.wait_ge(stored, UP + 32)

        @block.tensor
        def _(pe):
            pe.wait_ge(small, UP + 80)
            pe.wait_ge(prodd, UP + 1)
            for u in range(4):
                m = nc.tensor.matmul(pN[:, 2 * u:2 * u + 2], prod[:, u], hot[:], start=True, stop=True)
            pe.wait_ge(widd, UP + 1)
            nc.tensor.matmul(pW[:, 0:NB * NIH], ones[0:NB, :], wid[:].rearrange("p b h -> p (b h)"),
                             start=True, stop=True).then_inc(newd, 1)

            def sample(b):
                pe.wait_ge(k_in[b % 2], UP + 32 * (b // 2 + 1))
                if b >= 2:
                    pe.wait_ge(tmp, UP + b - 1)
                for i in range(HP):
                    m = nc.tensor.matmul(pSv[b % 2][:, i], kx[:, b % 2, i], qx[:, :, :, b], start=True, stop=True)
                m.then_inc(smm, 1)

            n = 0
            for i, b in enumerate(CHOSEN):
                for hd in range(NIH):
                    lo = 64 * (hd % 2)
                    if n >= 2:
                        pe.wait_ge(relu, UP + n - 1)
                    for c in range(0, (b + 1) * P, 512):
                        e = min(c + 512, (b + 1) * P)
                        m = nc.tensor.matmul(ps[:, n % 2, c:e], pj[lo:lo + ID, QI0 + hd // 2, b * P:(b + 1) * P],
                                             pj[lo:lo + ID, KI0, c:e], start=True, stop=True)
                    m.then_inc(mm, 1)
                    n += 1
                sample(i)
            for b in range(len(CHOSEN), NB):
                sample(b)
            pe.wait_ge(summed, UP + NB)
            for c in range(2):
                m = nc.tensor.transpose(pT[:, c], sc[:, 4 * c:4 * c + 4].rearrange("p b i -> p (b i)"), ident[:])
            m.then_inc(turned, 1)

        @block.scalar
        def _(act):
            n = 0
            for b in CHOSEN:
                for hd in range(NIH):
                    act.wait_ge(mm, UP + n + 1)
                    if n >= 2:
                        act.wait_ge(acc, UP + n - 1)
                    nc.scalar.activation(r[:, n % 2, 0:(b + 1) * P], ps[:, n % 2, 0:(b + 1) * P], ACT.Relu).then_inc(relu, 1)
                    n += 1

        @block.gpsimd
        def _(pool):
            nc.gpsimd.memset(qx[:], 0.0).then_inc(qzero, 1)
            nc.gpsimd.memset(mask[:, 0:mask_at(FIRST)], 0.0).then_inc(zeroed, 1)
            pool.wait_ge(zeroed, UP + 1)
            for b in range(FIRST):
                part = mask[:, mask_at(b) + b * P:mask_at(b + 1)]
                nc.gpsimd.affine_select(out=part, in_=part, compare_op=ALU.is_ge, fill=-BIG, base=0,
                                        pattern=[[-1, P]], channel_multiplier=1).then_inc(masked, 1)
            for i, b in enumerate(CHOSEN):
                pool.wait_ge(scored, UP + i + 1)
                part = mask[:, mask_at(b) + b * P:mask_at(b + 1)]
                nc.gpsimd.affine_select(out=part, in_=part, compare_op=ALU.is_ge, fill=CAUSAL, base=0,
                                        pattern=[[-1, P]], channel_multiplier=1).then_inc(causal, 1)

        @block.vector
        def _(dve):
            ch = Chain(dve, ch_s)
            nc.vector.tensor_scalar(wis[:], tok[:, 0:TB, NKV * HD:NKV * HD + NIH], SC, None, ALU.mult).then_inc(free, 1)
            nc.vector.tensor_tensor(prod[:], pj[:, QI0:QI0 + 4, SEQ:TOK],
                                    pj[:, KI0, SEQ:TOK].unsqueeze(1).to_broadcast([P, 4, NB]), ALU.mult).then_inc(prodd, 1)
            wi = tok[0:NB, TB, NKV * HD:NKV * HD + NIH]
            nc.vector.scalar_tensor_tensor(out=wid[:], in0=wi.unsqueeze(1).to_broadcast([NB, NB, NIH]), scalar=SC,
                                           in1=ident[0:NB, 0:NB].unsqueeze(2).to_broadcast([NB, NB, NIH]),
                                           op0=ALU.mult, op1=ALU.mult).then_inc(widd, 1)
            dve.wait_ge(small, UP + 80)
            dve.wait_ge(newd, UP + 1)
            ch.link(nc.vector.tensor_copy(wib[:].rearrange("p b h -> p (b h)"), pW[:, 0:NB * NIH]))
            ch.link(nc.vector.scalar_tensor_tensor(out=tn[:], in0=pN, scalar=0.0, in1=wi, op0=ALU.max, op1=ALU.mult))
            ch.link(nc.vector.tensor_reduce(snew[:], tn[:], AX, ALU.add))
            ch.link(nc.vector.tensor_scalar(snew[:], snew[:], SC, None, ALU.mult))
            dve.wait_ge(free, UP + 1)

            def sample(b):
                dve.wait_ge(smm, UP + b + 1)
                if b:
                    dve.wait_ge(summed, UP + b)
                nc.vector.scalar_tensor_tensor(out=t[:], in0=pSv[b % 2].rearrange("p i u h -> p (i u) h"), scalar=0.0,
                                               in1=wib[:, b].unsqueeze(1).to_broadcast([P, NPAGE, NIH]),
                                               op0=ALU.max, op1=ALU.mult).then_inc(tmp, 1)
                dve.wait_ge(tmp, UP + b + 1)
                nc.vector.tensor_reduce(sc[:, b].rearrange("p (u i) -> p i u", u=2), t[:].rearrange("p (i u) h -> p i u h", u=2), AX,
                                        ALU.add).then_inc(summed, 1)

            n = 0
            for i, b in enumerate(CHOSEN):
                s = mask[:, mask_at(b):mask_at(b + 1)]
                for hd in range(NIH):
                    dve.wait_ge(relu, UP + n + 1)
                    if hd == 0:
                        v = nc.vector.tensor_scalar(s, r[:, n % 2, 0:(b + 1) * P], wis[:, b, 0:1], None, ALU.mult)
                    else:
                        dve.wait_ge(acc, UP + n)
                        v = nc.vector.scalar_tensor_tensor(out=s, in0=r[:, n % 2, 0:(b + 1) * P], scalar=wis[:, b, hd:hd + 1],
                                                           in1=s, op0=ALU.mult, op1=ALU.add)
                    v.then_inc(acc, 1)
                    n += 1
                dve.wait_ge(acc, UP + n)
                dve.sem_inc(scored, 1)
                sample(i)
            for b in range(len(CHOSEN), NB):
                sample(b)
            dve.wait_ge(turned, UP + 1)
            nc.vector.tensor_copy(st[:], pT[:]).then_inc(moved, 1)


ROUNDS = TOPK // 8
SHARE = ROUNDS // SG
PROMPT_ROUNDS = SHARE - KT // 2


def top_round(dve, nc, rows, m8, found, tick, before):
    dve.wait_ge(found, UP + before)
    dve.sem_inc(tick, 1)
    for i, s in enumerate(rows):
        nc.vector.max(m8[0:s.shape[0], i], s).then_inc(found, 1)
    dve.wait_ge(found, UP + before + len(rows))
    dve.sem_inc(tick, 1)
    for i, s in enumerate(rows):
        nc.vector.match_replace(s, m8[0:s.shape[0], i], s, TAKEN).then_inc(found, 1)


def top_rounds(dve, nc, rows, m8, found, tick, before, rounds):
    with dve.Fori(0, rounds) as j:
        top_round(dve, nc, rows, m8, found, tick, before + 2 * len(rows) * j)
    return before + 2 * len(rows) * rounds


def chosen_rows(mask):
    return [mask[:, mask_at(b):mask_at(b + 1)] for b in CHOSEN]


def attend(nc, d, scr, h, kT, qs, tok, mask, bias, ident, att):
    with Phase(nc, "att") as ph:
        q = ph.sb("q", [P, 2, P])
        L = ph.sb("L", [P, 2, 2, SEQ])
        ET = ph.sb("ET", [P, 2, SEQ])
        nm = ph.sb("nm", [P, 2, 2])
        den = ph.sb("den", [P, 2, 2])
        rd = ph.sb("rd", [P, 2])
        pair = ph.sb("pair", [P, P])
        pS = ph.ps("pS", [P, 2, SEQ])
        pT = ph.ps("pT", [P, 2, 512])
        pO = ph.ps("pO", [P, 512])
        pG = ph.ps("pG", [P, 512])
        qb = ph.sb("qb", [P, 2, NH // 2, P])
        w = ph.sb("w", [P, 2, KT, P])
        g_raw = ph.sb("g_raw", [P, 2, NCH, NC])
        staged, mm, logit, rmax, exped, trans, copied, pv, scaled, recip, turned = (
            ph.sem(n) for n in ("staged", "mm", "logit", "rmax", "exped", "trans", "copied", "pv", "scaled", "recip",
                                "turned"))
        k_in, qs_in, gmm, gread, g_saved, w_in0, w_in1 = (
            ph.sem(n) for n in ("k_in", "qs_in", "gmm", "gread", "g_saved", "w_in0", "w_in1"))
        q_in = [ph.sem(f"q_in{b}") for b in range(2)]
        w_in = (w_in0, w_in1)
        block = ph.block()
        PAIRS = NH // 2
        G = NH // NKV

        assert G - 1 == NCH
        FILL = KT // 2

        @block.sync
        def _(sp):
            def load_q(b):
                sp.dma_start(qb[:, b % 2], scr["qk"][:, QT0:QT0 + NH // 2, b * P:(b + 1) * P]).then_inc(q_in[b % 2], 16)

            sp.dma_start(kT[:], scr["qk"][:, KT0:KT0 + 2]).then_inc(k_in, 16)
            load_q(0)
            load_q(1)
            for q in range(2):
                sp.dma_start(w[:, q], d["w_ga"][q]).then_inc(w_in[q], 16)
            sp.dma_start(qs[:], scr["qk"][:, QT0:QT0 + NH // 2, SEQ:TOK]).then_inc(qs_in, 16)
            for b in range(TB):
                if b < FILL:
                    for q in range(2):
                        sp.wait_ge(gmm, UP + 2 * NCH * b + 2 * (NCH - 1) + q + 1)
                        if b + 1 < FILL:
                            sp.dma_start(w[:, q], d["w_ga"][2 * (b + 1) + q]).then_inc(w_in[q], 16)
                    sp.wait_ge(gread, UP + 2 * NCH * (b + 1))
                    for q in range(2):
                        sp.dma_start(scr["ga"][:, 2 * b + q], g_raw[:, q].rearrange("p c n -> p (c n)")).then_inc(g_saved, 16)
                if b + 2 < TB:
                    sp.wait_ge(staged, UP + PAIRS * (b + 1))
                    load_q(b + 2)
            sp.wait_ge(g_saved, UP + 16 * KT)
            sp.wait_ge(qs_in, UP + 16)

        PC = 4

        def pieces(b):
            return [(u, c, min(c + PC, b + 1)) for u in range(2) for c in range(0, b + 1, PC)]

        def pieces_before(b):
            return sum(PAIRS * len(pieces(a)) for a in range(b))

        def before(b):
            return sum(PAIRS * (len(pieces(a)) + 1) for a in range(b))

        def loops(eng, body):
            for b in range(TB):
                with eng.Fori(0, G - 1) as g:
                    for m in range(2):
                        body(b * PAIRS + 2 * g + m, b, m, g, (b, g + 1))
                for m in range(2):
                    body(b * PAIRS + 2 * (G - 1) + m, b, m, G - 1, (b + 1, 0) if b + 1 < TB else None)

        @block.gpsimd
        def _(pool):
            def stage(b, m, g):
                pool.wait_ge(q_in[b % 2], UP + 16 * (b // 2 + 1))
                nc.gpsimd.tensor_copy(q[:, m], qb[:, b % 2, m * G + g]).then_inc(staged, 1)

            def body(t, b, m, g, nxt):
                if nxt is not None:
                    pool.wait_ge(mm, UP + 2 * t + 2)
                    stage(nxt[0], m, nxt[1])

            stage(0, 0, 0)
            stage(0, 1, 0)
            loops(pool, body)

        @block.tensor
        def _(pe):
            def logits(t, b, m):
                W = (b + 1) * P
                pe.wait_ge(staged, UP + t + 1)
                for u in range(2):
                    if isinstance(t, int) and t == 0:
                        pass
                    else:
                        pe.wait_ge(logit, UP + 4 * (t - 1) + 2 * u + 1)
                    for c in range(0, W, 512):
                        e = min(c + 512, W)
                        x = nc.tensor.matmul(pS[:, u, c:e], q[64 * u:64 * u + 64, m],
                                             kT[64 * u:64 * u + 64, m, c:e], start=True, stop=True)
                    x.then_inc(mm, 1)

            def body(t, b, m, g, nxt):
                ps = pieces(b)
                first = before(b) + (len(ps) + 1) * (2 * g + m)
                odd = (len(ps) + 1) * m

                def turn(i):
                    u, c0, c1 = ps[i]
                    pe.wait_ge(exped, UP + 2 * t + u + 1)
                    pe.wait_ge(copied, UP + first + i)
                    for c in range(c0, c1):
                        x = nc.tensor.transpose(pT[:, (odd + i) % 2, (c - c0) * P:(c - c0 + 1) * P], L[:, m, u, c * P:(c + 1) * P], ident[:])
                    x.then_inc(trans, 1)

                turn(0)
                turn(1)
                for i, (u, c0, c1) in enumerate(ps):
                    pe.wait_ge(copied, UP + first + i + 2)
                    if i == 0:
                        pe.wait_ge(scaled, UP + t)
                    for c in range(c0, c1):
                        x = nc.tensor.matmul(pO[:, u * HD:(u + 1) * HD], ET[:, u, c * P:(c + 1) * P],
                                             tok[:, c, (2 * m + u) * HD:(2 * m + u + 1) * HD], start=c == 0, stop=c == b)
                    x.then_inc(pv, 1)
                    if i + 2 < len(ps):
                        turn(i + 2)
                if nxt is not None:
                    logits(t + 2, nxt[0], m)
                if b < FILL and nxt is not None and nxt[0] == b:
                    pe.wait_ge(w_in[m], UP + 16 * (b + 1))
                    pe.wait_ge(gread, UP + 2 * NCH * b + 2 * g + m)
                    for k in range(KT):
                        x = nc.tensor.matmul(pG[:, 0:NC], w[:, m, k], h[:, k, bass.ds(g * NC, NC)], start=k == 0, stop=k == KT - 1)
                    x.then_inc(gmm, 1)
                pe.wait_ge(scaled, UP + t + 1)
                pe.wait_ge(copied, UP + first + len(ps))
                nc.tensor.transpose(pT[:, (odd + len(ps)) % 2, 0:P], pair[:], ident[:]).then_inc(turned, 1)

            pe.wait_ge(k_in, UP + 16)
            logits(0, 0, 0)
            logits(1, 0, 1)
            loops(pe, body)

        @block.scalar
        def _(act):
            def exps(t, b, m):
                W = (b + 1) * P
                for u in range(2):
                    act.wait_ge(rmax, UP + 2 * t + u + 1)
                    nc.scalar.activation(L[:, m, u, 0:W], L[:, m, u, 0:W], ACT.Exp, bias=nm[:, m, u:u + 1],
                                         accum_out=den[:, m, u:u + 1]).then_inc(exped, 1)

            def body(t, b, m, g, nxt):
                ps = pieces(b)
                first = pieces_before(b) + len(ps) * (2 * g + m)
                odd = (len(ps) + 1) * m
                act.wait_ge(pv, UP + first)
                for i, (u, c0, c1) in enumerate(ps):
                    act.wait_ge(trans, UP + first + i + 1)
                    nc.scalar.activation(ET[:, u, c0 * P:c1 * P], pT[:, (odd + i) % 2, 0:(c1 - c0) * P], ACT.Copy).then_inc(copied, 1)
                if m == 0:
                    exps(t + 1, b, 1)
                elif nxt is not None:
                    exps(t + 1, nxt[0], 0)
                if b < FILL and nxt is not None and nxt[0] == b:
                    act.wait_ge(gmm, UP + 2 * NCH * b + 2 * g + m + 1)
                    act.wait_ge(g_saved, UP + 32 * b)
                    nc.scalar.activation(g_raw[:, m, g], pG[:, 0:NC], ACT.Copy).then_inc(gread, 1)
                act.wait_ge(turned, UP + t + 1)
                nc.scalar.activation(att[:, m * G + g, b * P:(b + 1) * P], pT[:, (odd + len(ps)) % 2, 0:P], ACT.Copy).then_inc(copied, 1)

            act.sem_inc(copied, 1)
            exps(0, 0, 0)
            loops(act, body)

        @block.vector
        def _(dve):
            def logits(t, b, m, g):
                W = (b + 1) * P
                lo = max(W - WIN, 0)
                if isinstance(t, int):
                    r = t - b * PAIRS
                    if t >= 2:
                        dve.wait_ge(trans, UP + pieces_before(b) + (len(pieces(b)) * (r - 1) if r else -len(pieces(b - 1))))
                else:
                    dve.wait_ge(trans, UP + pieces_before(b) + len(pieces(b)) * (2 * g + m - 1))
                for u in range(2):
                    dve.wait_ge(mm, UP + 2 * t + u + 1)
                    l = L[:, m, u]
                    nc.vector.scalar_tensor_tensor(out=l[:, 0:W], in0=pS[:, u, 0:W], scalar=float(HD ** -0.5),
                                                   in1=mask[:, mask_at(b):mask_at(b + 1)], op0=ALU.mult,
                                                   op1=ALU.add).then_inc(logit, 1)
                    dve.wait_ge(logit, UP + 4 * t + 2 * u + 1)
                    nc.vector.tensor_tensor(l[:, lo:W], l[:, lo:W], bias[:, 2 * (m * G + g) + u, WIN - (W - lo):WIN],
                                            ALU.add).then_inc(logit, 1)
                    dve.wait_ge(logit, UP + 4 * t + 2 * u + 2)
                    nc.vector.tensor_reduce(nm[:, m, u:u + 1], l[:, 0:W], AX, ALU.max, negate=True).then_inc(rmax, 1)

            def body(t, b, m, g, nxt):
                if m == 0:
                    logits(t + 1, b, 1, g)
                elif nxt is not None:
                    logits(t + 1, nxt[0], 0, nxt[1])
                dve.wait_ge(turned, UP + t)
                dve.wait_ge(exped, UP + 2 * t + 2)
                nc.vector.reciprocal(rd[:], den[:, m]).then_inc(recip, 1)
                dve.wait_ge(recip, UP + t + 1)
                dve.wait_ge(pv, UP + pieces_before(b) + len(pieces(b)) * (2 * g + m + 1))
                nc.vector.tensor_tensor(pair[:].rearrange("p (u d) -> p u d", u=2),
                                        pO[:, 0:2 * HD].rearrange("p (u d) -> p u d", u=2),
                                        rd[:].unsqueeze(2).to_broadcast([P, 2, HD]), ALU.mult).then_inc(scaled, 1)

            logits(0, 0, 0, 0)
            loops(dve, body)


def tables(nc, d, s, bias):
    with Phase(nc, "tab") as ph:
        hot = ph.sb("hot", [NBUCKET, 512])
        rb = ph.sb("rb", [NBUCKET, NH])
        byh = ph.sb("byh", [NH, 512])
        rows = ph.sb("rows", [P, 2, NH])
        flip = ph.sb("flip", [P, P])
        up = ph.sb("up", [P, NH, WIN])
        pf = ph.ps("pf", [P, 4, 2 * WIN])
        ps = ph.ps("ps", [P, 512])
        pr = ph.ps("pr", [P, 2, NH])
        flipped, loaded, mm, moved, sub, stored, back = (
            ph.sem(n) for n in ("flipped", "loaded", "mm", "moved", "sub", "stored", "back"))
        block = ph.block()

        @block.sync
        def _(sp):
            sp.dma_start(hot[:], d["hot"]).then_inc(loaded, 16)
            sp.dma_start(rb[:], d["rel_bias"]).then_inc(loaded, 16)
            sp.dma_start(flip[:], d["flip"]).then_inc(loaded, 16)
            sp.wait_ge(sub, UP + 1)
            sp.dma_start(s["byh"], byh[:]).then_inc(stored, 16)
            sp.wait_ge(moved, UP + 2)
            sp.dma_start(s["brow"].rearrange("(c p) h -> p c h", c=2), rows[:]).then_inc(stored, 16)
            sp.wait_ge(stored, UP + 32)
            win = bass.AP(s["byh"].tensor, 0, [[1, P], [512, NH], [1, WIN]])
            sp.dma_start(up[:], win).then_inc(back, 16)
            sp.wait_ge(back, UP + 16)

        @block.tensor
        def _(pe):
            pe.wait_ge(loaded, UP + 48)
            nc.tensor.matmul(ps[0:NH, :], rb[:], hot[:], start=True, stop=True).then_inc(mm, 1)
            for c in range(2):
                nc.tensor.matmul(pr[:, c], hot[:, c * P:(c + 1) * P], rb[:], start=True, stop=True).then_inc(mm, 1)
            pe.wait_ge(back, UP + 16)
            for n in range(NH // 2):
                if n >= 4:
                    pe.wait_ge(flipped, UP + n - 3)
                nc.tensor.matmul(pf[:, n % 4], flip[:], up[:, 2 * n:2 * n + 2].rearrange("p h j -> p (h j)"),
                                 start=True, stop=True).then_inc(mm, 1)

        @block.vector
        def _(dve):
            dve.wait_ge(mm, UP + 3)
            nc.vector.tensor_copy(byh[:], ps[0:NH, :]).then_inc(moved, 1)
            nc.vector.tensor_copy(rows[:], pr[:]).then_inc(moved, 1)
            dve.wait_ge(moved, UP + 2)
            nc.vector.tensor_scalar(byh[:], byh[:], ps[0:NH, 0:1], None, ALU.subtract).then_inc(sub, 1)
            for n in range(NH // 2):
                dve.wait_ge(mm, UP + 4 + n)
                nc.vector.tensor_copy(bias[:, 2 * n:2 * n + 2].rearrange("p h j -> p (h j)"), pf[:, n % 4]).then_inc(flipped, 1)


def mix_out(nc, d, x_d, x, A, ada):
    with Phase(nc, "mo") as ph:
        w = ph.sb("w", [P, 2, KT, P])
        smp = ph.sb("smp", [P, 2, NB])
        ps = [ph.ps(f"ps{q}", [P, NCH, 512]) for q in range(2)]
        w_in = [ph.sem(f"w_in{q}") for q in range(2)]
        read = [ph.sem(f"read{q}") for q in range(2)]
        mm, x_in, smped = (ph.sem(n) for n in ("mm", "x_in", "smped"))
        block = ph.block()
        gate = 5 * KT

        @block.sync
        def _(sp):
            load_tiles(sp, w, w_in, mm, NCH, d["w_out"], KT)

        @block.scalar
        def _(act):
            act.dma_start(x[:], x_d).then_inc(x_in, 16)

        @block.tensor
        def _(pe):
            project_tiles(pe, nc, w, ps, A, w_in, mm, read, KT)

        @block.vector
        def _(dve):
            dve.wait_ge(x_in, UP + 16)
            with dve.Fori(0, KT // 2) as i:
                for q in range(2):
                    t = 2 * i + q
                    dve.wait_ge(mm, UP + NCH * (2 * i + q + 1))
                    nc.vector.tensor_tensor(smp[:, q], ps[q][:, 2, LASTP:NC], ada[:, gate + t, 1:NCOND],
                                            ALU.mult).then_inc(smped, 1)
                    for n in range(NCH):
                        c = NC if n < NCH - 1 else LASTP
                        v = nc.vector.scalar_tensor_tensor(
                            out=x[:, t, n * NC:n * NC + c], in0=ps[q][:, n, 0:c],
                            scalar=ada[:, bass.ds(gate + t, 1), 0:1].rearrange("p a b -> p (a b)"),
                            in1=x[:, t, n * NC:n * NC + c], op0=ALU.mult, op1=ALU.add)
                        if n < NCH - 1:
                            v.then_inc(read[q], 1)
                    dve.wait_ge(smped, UP + 2 * i + q + 1)
                    nc.vector.tensor_tensor(x[:, t, SEQ:TOK], x[:, t, SEQ:TOK], smp[:, q], ALU.add).then_inc(read[q], 1)
            for q in range(2):
                dve.wait_ge(read[q], UP + NCH * KT // 2)


def time_steps(nc, d, o, tok, dt, dtA, ea, te, etot, upper, constants, S):
    with Phase(nc, "ts") as ph:
        rows = ph.sb("rows", [P, 2, SH])
        t = {n: ph.sb(n, [P, TB + 1, SH]) for n in ("v", "e", "u", "l", "r")}
        ps = ph.ps("ps", [P, 2, 512])
        r_in, negabs, exped, logged, ch_s, mm, ex, zero = (ph.sem(n) for n in ("r_in", "negabs", "exped", "logged", "ch", "mm", "ex", "zero"))
        ones = ph.sb("ones", [P, P])
        others, zeroed = ph.sem("others"), ph.sem("zeroed")
        block = ph.block()
        v, e, u, l, r = (t[n] for n in ("v", "e", "u", "l", "r"))
        raw = tok[:, :, NKV * HD + NIH:VW]
        bc = lambda row: rows[:, row].unsqueeze(1).to_broadcast([P, TB, SH])

        @block.sync
        def _(sp):
            sp.dma_start(rows[:, 0], d["dt_bias"]).then_inc(r_in, 16)
            sp.dma_start(rows[:, 1], d["a_log"]).then_inc(r_in, 16)
            sp.dma_start(upper[:], d["upper"]).then_inc(r_in, 16)
            for dst, src in constants:
                sp.dma_start(dst[:], d[src]).then_inc(others, 16)
            sp.dma_start(o["conv_old"], d["conv_old"]).then_inc(others, 16)
            sp.wait_ge(others, UP + 16 * (len(constants) + 1))

        @block.scalar
        def _(act):
            act.wait_ge(r_in, UP + 48)
            nc.scalar.activation(rows[:, 1], rows[:, 1], ACT.Exp).then_inc(exped, 1)
            act.wait_ge(negabs, UP + 1)
            nc.scalar.activation(e[:], e[:], ACT.Exp).then_inc(exped, 1)
            act.wait_ge(negabs, UP + 2)
            nc.scalar.activation(l[:], u[:], ACT.Ln).then_inc(logged, 1)
            act.wait_ge(ex, UP + 1)
            f = lambda a: a[:].rearrange("p c h -> p (c h)")
            nc.scalar.activation(f(ea), ps[:, 0, 0:TB * SH], ACT.Exp).then_inc(exped, 1)
            nc.scalar.activation(f(etot), ps[:, 1, 0:TB * SH], ACT.Exp).then_inc(exped, 1)
            nc.scalar.activation(te[:], te[:], ACT.Exp).then_inc(exped, 1)
            act.wait_ge(exped, UP + 5)

        @block.tensor
        def _(pe):
            pe.wait_ge(mm, UP + 1)
            f = dtA[:, 0:TB].rearrange("p c h -> p (c h)")
            nc.tensor.matmul(ps[:, 0, 0:TB * SH], upper[:], f, start=True, stop=True)
            nc.tensor.matmul(ps[:, 1, 0:TB * SH], ones[:], f, start=True, stop=True).then_inc(mm, 1)

        @block.gpsimd
        def _(pool):
            nc.gpsimd.memset(ones[:], 1.0).then_inc(zero, 1)
            nc.gpsimd.memset(S[:], 0.0).then_inc(zeroed, 1)
            pool.wait_ge(zeroed, UP + 1)

        @block.vector
        def _(dve):
            ch = Chain(dve, ch_s)
            dve.wait_ge(r_in, UP + 48)
            ch.link(nc.vector.memset(v[:, TB], 0.0))
            ch.link(nc.vector.tensor_tensor(v[:, 0:TB], raw[:, 0:TB], bc(0), ALU.add))
            ch.link(nc.vector.tensor_tensor(v[0:NB, TB], raw[0:NB, TB], rows[0:NB, 0], ALU.add))
            nc.vector.scalar_tensor_tensor(out=e[:], in0=v[:], scalar=-1.0, in1=v[:], op0=ALU.mult, op1=ALU.min).then_inc(negabs, 1)
            dve.wait_ge(exped, UP + 2)
            ch.link(nc.vector.tensor_scalar(u[:], e[:], 1.0, None, ALU.add))
            dve.sem_inc(negabs, 1)
            ch.link(nc.vector.tensor_scalar(r[:], u[:], -1.0, None, ALU.add))
            dve.wait_ge(logged, UP + 1)
            ch.link(nc.vector.tensor_scalar(u[:], r[:], 0.0, None, ALU.is_equal))
            ch.link(nc.vector.tensor_tensor(r[:], r[:], u[:], ALU.add))
            ch.link(nc.vector.reciprocal(r[:], r[:]))
            ch.link(nc.vector.tensor_tensor(l[:], l[:], r[:], ALU.mult))
            ch.link(nc.vector.tensor_tensor(l[:], l[:], u[:], ALU.add))
            ch.link(nc.vector.tensor_tensor(l[:], l[:], e[:], ALU.mult))
            ch.link(nc.vector.scalar_tensor_tensor(out=dt[:], in0=v[:], scalar=0.0, in1=l[:], op0=ALU.max, op1=ALU.add))
            ch.link(nc.vector.scalar_tensor_tensor(out=dtA[:, 0:TB], in0=dt[:, 0:TB], scalar=-1.0, in1=bc(1),
                                                   op0=ALU.mult, op1=ALU.mult))
            ch.link(nc.vector.scalar_tensor_tensor(out=dtA[:, TB], in0=dt[:, TB], scalar=-1.0, in1=rows[:, 1],
                                                   op0=ALU.mult, op1=ALU.mult))
            dve.wait_ge(zero, UP + 1)
            dve.sem_inc(mm, 1)
            dve.wait_ge(mm, UP + 2)
            f = lambda a: a[:].rearrange("p c h -> p (c h)")
            ch.link(nc.vector.tensor_copy(f(te), ps[:, 1, 0:TB * SH]))
            ch.link(nc.vector.tensor_tensor(f(te), f(te), ps[:, 0, 0:TB * SH], ALU.subtract))
            dve.sem_inc(ex, 1)


def ssd_project(nc, arena, banks, start, d, o, scr, g, h, xb, xc, zs, cw, cb, y, mask):
    with Phase(nc, "sp", arena, start, banks=banks) as ph:
        w = ph.sb("w", [P, 2, KT, P])
        cv = ph.sb("cv", [P, 2, SEQ])
        st = ph.sb("st", [P, XT, CW - 1, NB])
        sm = ph.sb("sm", [P, 2, XT, NB])
        m8 = ph.sb("m8", [P, len(CHOSEN) + 1, 8])
        top = y[0:NB].rearrange("p a b -> p (a b)")[:, 0:PAST + 1]
        top_in, found, tick = ph.sem("top_in"), ph.sem("found"), ph.sem("tick")
        ps = [ph.ps(f"ps{q}", [P, NCH, 512]) for q in range(2)]
        w_in = [ph.sem(f"w_in{q}") for q in range(2)]
        read = [ph.sem(f"read{q}") for q in range(2)]
        mm, st_in, pad, tap, conv, act_done, smp, saved = (
            ph.sem(n) for n in ("mm", "st_in", "pad", "tap", "conv", "act_done", "smp", "saved"))
        block = ph.block()
        PAD = CW - 1

        @block.sync
        def _(sp):
            sp.dma_start(top[:, 0:PAST], scr["score"]).then_inc(top_in, 16)
            sp.dma_start(top[:, PAST:PAST + 1], scr["snew"]).then_inc(top_in, 16)
            load_tiles(sp, w, w_in, mm, NCH, d["w_ssd"][g], XT + 4)
            for q in range(2):
                sp.wait_ge(read[q], UP + NCH * XT // 2)
            sp.dma_start(o["conv_p"][g], xb[:, :, SEQ:SEQ + PAD]).then_inc(saved, 16)
            sp.dma_start(o["conv_s"][g], xb[:, :, PAD + SEQ:PAD + TOK]).then_inc(saved, 16)
            sp.wait_ge(found, UP + 2 * (len(CHOSEN) * PROMPT_ROUNDS + SHARE))
            sp.dma_start(scr["score"], top[:, 0:PAST]).then_inc(saved, 16)
            sp.dma_start(scr["snew"], top[:, PAST:PAST + 1]).then_inc(saved, 16)
            sp.wait_ge(saved, UP + 64)

        @block.gpsimd
        def _(pool):
            nc.gpsimd.memset(xb[:, :, 0:PAD], 0.0).then_inc(pad, 1)

        @block.tensor
        def _(pe):
            project_tiles(pe, nc, w, ps, h, w_in, mm, read, XT + 4)

        @block.scalar
        def _(act):
            act.dma_start(st[:], d["state_conv"][g]).then_inc(st_in, 16)

            def copy(dst, i, before=0, func=ACT.Copy):
                for q in range(2):
                    for c in range(NCH):
                        act.wait_ge(mm, UP + NCH * (before + 2 * i + q) + c + 1)
                        nc.scalar.activation(dst[:, 2 * i + q, c * NC:(c + 1) * NC], ps[q][:, c, 0:NC], func).then_inc(read[q], 1)

            def silu(i):
                for q in range(2):
                    t = 2 * i + q
                    act.wait_ge(conv, UP + t + 1)
                    nc.scalar.activation(xc[:, t, 0:SEQ], cv[:, q], ACT.Silu,
                                         bias=cb[:, bass.ds(g * XT + t, 1)]).then_inc(act_done, 1)

            raw = xb[:, :, PAD:PAD + TOK]
            copy(raw, 0)
            copy(raw, 1)
            silu(0)
            copy(raw, 2)
            silu(1)
            copy(zs, 0, XT, ACT.Silu)
            silu(2)
            copy(zs, 1, XT, ACT.Silu)
            act.wait_ge(smp, UP + 2 * CW)
            nc.scalar.activation(xc[:, :, SEQ:TOK], sm[:, 0], ACT.Silu).then_inc(act_done, 1)
            act.wait_ge(act_done, UP + XT + 1)

        @block.vector
        def _(dve):

            def convolve(i):
                for q in range(2):
                    t = 2 * i + q
                    dve.wait_ge(read[q], UP + NCH * (i + 1))
                    dve.wait_ge(act_done, UP + 2 * i)
                    for k in range(CW):
                        src, wk = xb[:, t, k:k + SEQ], cw[:, bass.ds(g * XT + t, 1), k:k + 1].rearrange("p a b -> p (a b)")
                        if k == 0:
                            v = nc.vector.tensor_scalar(cv[:, q], src, wk, None, ALU.mult)
                        else:
                            v = nc.vector.scalar_tensor_tensor(out=cv[:, q], in0=src, scalar=wk, in1=cv[:, q],
                                                               op0=ALU.mult, op1=ALU.add)
                        if k < CW - 1:
                            v.then_inc(tap, 1)
                            dve.wait_ge(tap, UP + (CW - 1) * t + k + 1)
                        else:
                            v.then_inc(conv, 1)

            n = top_rounds(dve, nc, chosen_rows(mask), m8, found, tick, 0, PROMPT_ROUNDS)
            dve.wait_ge(pad, UP + 1)
            convolve(0)
            dve.wait_ge(top_in, UP + 32)
            n = top_rounds(dve, nc, [top], m8, found, tick, n, SHARE // 4)
            convolve(1)
            n = top_rounds(dve, nc, [top], m8, found, tick, n, SHARE // 4)
            convolve(2)
            dve.wait_ge(st_in, UP + 16)
            for k in range(CW):
                src = st[:, :, k] if k < CW - 1 else xb[:, :, PAD + SEQ:PAD + TOK]
                wk = cw[:, bass.ds(g * XT, XT), k:k + 1].to_broadcast([P, XT, NB])
                nc.vector.tensor_tensor(sm[:, 0 if k == 0 else 1], src, wk, ALU.mult).then_inc(smp, 1)
                dve.wait_ge(smp, UP + 2 * k + 1)
                other = sm[:, 1] if k else cb[:, bass.ds(g * XT, XT)].unsqueeze(2).to_broadcast([P, XT, NB])
                nc.vector.tensor_tensor(sm[:, 0], sm[:, 0], other, ALU.add).then_inc(smp, 1)
                dve.wait_ge(smp, UP + 2 * k + 2)
            top_rounds(dve, nc, [top], m8, found, tick, n, SHARE - SHARE // 4 * 2)


def ssd_scan(nc, arena, banks, o, g, xc, y, dt, dtA, ea, te, etot, upper, below, ident, hT):
    R, PD = SH // SG, DI // SH
    GW = R * PD
    with Phase(nc, "sc", arena, banks=banks) as ph:
        st = ph.sb("st", [P, 2, XT, P])
        lower = ph.sb("lower", [P, 2, R, P])
        xdt = ph.sb("xdt", [P, 2, GW])
        xw = ph.sb("xw", [P, GW])
        bt = ph.sb("bt", [P, 2, P])
        cbm = ph.sb("cbm", [P, 2, P])
        E = ph.sb("E", [P, 2, R, P])
        yt = ph.sb("yt", [P, GW])
        pX, pB, pY, pO, pH, pT = (ph.ps(n, [P, 512]) for n in ("pX", "pB", "pY", "pO", "pH", "pT"))
        pS = ph.ps("pS", [P, R, P])
        names = ("staged", "segs", "turned", "seg", "x_dt", "x_w", "b_t", "cb_m", "decay", "M", "ydiag", "yoff", "hup",
                 "y1", "y2", "h1", "h2", "yturn", "ysaved", "saved")
        (staged, segs, turned, seg, x_dt, x_w, b_t, cb_m, decay, M, ydiag, yoff, hup, y1, y2, h1, h2, yturn, ysaved,
         saved) = (ph.sem(n) for n in names)
        block = ph.block()
        heads = bass.ds(g * R, R)
        wide = lambda a, c: a[:, c, heads].unsqueeze(2).to_broadcast([P, R, PD])
        v3 = lambda a: a.rearrange("p (r d) -> p r d", r=R)


        def turns(eng, turn):
            with eng.Fori(0, TB // 2 - 1) as i:
                for s in range(2):
                    turn(2 * i + s, s)

        @block.gpsimd
        def _(pool):
            def enter(c, s):
                if not isinstance(c, int):
                    pool.wait_ge(seg, UP + c - 1)
                nc.gpsimd.tensor_tensor(lower[:, s], below[:].unsqueeze(1).to_broadcast([P, R, P]),
                                        dtA[:, c, heads].unsqueeze(2).to_broadcast([P, R, P]), ALU.mult).then_inc(segs, 1)

            def weigh(c, s):
                pool.wait_ge(x_dt, UP + c + 1)
                pool.wait_ge(hup, UP + c)
                nc.gpsimd.tensor_tensor(v3(xw[:]), v3(xdt[:, s]), wide(te, c), ALU.mult).then_inc(x_w, 1)

            def turn(c, s):
                enter(c + 2, s)
                weigh(c + 1, 1 - s)

            enter(0, 0)
            enter(1, 1)
            weigh(0, 0)
            turns(pool, turn)
            weigh(TB - 1, 1)

        @block.tensor
        def _(pe):
            def enter(c, s):
                pe.wait_ge(staged, UP + c + 1)
                pe.wait_ge(x_dt, UP + c)
                pe.wait_ge(cb_m, UP + c)
                for t in range(4):
                    nc.tensor.transpose(pX[:, t * P:(t + 1) * P], st[:, s, t], ident[:])
                nc.tensor.transpose(pB[:, 0:P], st[:, s, 4], ident[:])
                nc.tensor.matmul(pB[:, P:2 * P], st[:, s, 4], st[:, s, 5], start=True, stop=True).then_inc(turned, 1)
                pe.wait_ge(segs, UP + c + 1)
                pe.wait_ge(decay, UP + c)
                for r in range(R):
                    m = nc.tensor.matmul(pS[:, r], lower[:, s, r], upper[:], start=True, stop=True)
                m.then_inc(seg, 1)

            def through(c, s):
                pe.wait_ge(h2, UP + c + 1)
                pe.wait_ge(y1, UP + c)
                nc.tensor.matmul(pO[:], st[:, s, 5], hT[:], start=True, stop=True).then_inc(yoff, 1)
                pe.wait_ge(b_t, UP + c + 1)
                pe.wait_ge(x_w, UP + c + 1)
                nc.tensor.matmul(pH[:], bt[:, s], xw[:], start=True, stop=True).then_inc(hup, 1)
                pe.wait_ge(M, UP + c + 1)
                pe.wait_ge(y2, UP + c)
                for r in range(R):
                    m = nc.tensor.matmul(pY[:, r * PD:(r + 1) * PD], E[:, s, r], xdt[:, s, r * PD:(r + 1) * PD], start=True, stop=True)
                m.then_inc(ydiag, 1)

            def back(c):
                pe.wait_ge(y2, UP + c + 1)
                pe.wait_ge(ysaved, UP + c)
                for t in range(4):
                    m = nc.tensor.transpose(pT[:, t * P:(t + 1) * P], yt[:, t * P:(t + 1) * P], ident[:])
                m.then_inc(yturn, 1)

            def turn(c, s):
                enter(c + 2, s)
                back(c)
                through(c + 1, 1 - s)

            enter(0, 0)
            enter(1, 1)
            through(0, 0)
            turns(pe, turn)
            back(TB - 2)
            through(TB - 1, 1)
            back(TB - 1)

        @block.scalar
        def _(act):
            def stage(c, s):
                if not isinstance(c, int):
                    act.wait_ge(yoff, UP + c - 1)
                nc.scalar.activation(st[:, s], xc[:, :, bass.ds(c * P, P)], ACT.Copy).then_inc(staged, 1)

            def enter(c, s):
                act.wait_ge(seg, UP + c + 1)
                if not isinstance(c, int):
                    act.wait_ge(ydiag, UP + c - 1)
                nc.scalar.activation(E[:, s].rearrange("p r l -> p (r l)"), pS[:].rearrange("p r l -> p (r l)"), ACT.Exp).then_inc(decay, 1)

            def save(c):
                act.wait_ge(yturn, UP + c + 1)
                nc.scalar.activation(y[:, 0:4, bass.ds(c * P, P)], pT[:].rearrange("p (t l) -> p t l", t=4), ACT.Copy).then_inc(ysaved, 1)

            def turn(c, s):
                stage(c + 2, s)
                enter(c + 2, s)
                save(c)

            stage(0, 0)
            stage(1, 1)
            enter(0, 0)
            enter(1, 1)
            turns(act, turn)
            save(TB - 2)
            save(TB - 1)
            act.wait_ge(ysaved, UP + TB)

        @block.sync
        def _(sp):
            sp.wait_ge(h2, UP + TB + 1)
            sp.dma_start(o["ssm_p"][g], hT[:]).then_inc(saved, 16)
            sp.wait_ge(saved, UP + 16)

        @block.vector
        def _(dve):
            def enter(c, s):
                dve.wait_ge(turned, UP + c + 1)
                if not isinstance(c, int):
                    dve.wait_ge(ydiag, UP + c - 1)
                    dve.wait_ge(x_w, UP + c - 1)
                    dve.wait_ge(hup, UP + c - 1)
                nc.vector.tensor_tensor(v3(xdt[:, s]), v3(pX[:]), wide(dt, c), ALU.mult).then_inc(x_dt, 1)
                nc.vector.tensor_copy(bt[:, s], pB[:, 0:P]).then_inc(b_t, 1)
                nc.vector.tensor_tensor(cbm[:, s], pB[:, P:2 * P], upper[:], ALU.mult).then_inc(cb_m, 1)

            def decays(c, s):
                dve.wait_ge(decay, UP + c + 1)
                dve.wait_ge(cb_m, UP + c + 1)
                nc.vector.tensor_tensor(E[:, s], E[:, s], cbm[:, s].unsqueeze(1).to_broadcast([P, R, P]), ALU.mult).then_inc(M, 1)

            def through(c):
                dve.wait_ge(yoff, UP + c + 1)
                dve.wait_ge(yturn, UP + c)
                nc.vector.tensor_tensor(v3(yt[:]), v3(pO[:]), wide(ea, c), ALU.mult).then_inc(y1, 1)
                dve.wait_ge(h2, UP + c + 1)
                nc.vector.tensor_tensor(v3(hT[:]), v3(hT[:]), wide(etot, c), ALU.mult).then_inc(h1, 1)
                dve.wait_ge(h1, UP + c + 1)
                dve.wait_ge(hup, UP + c + 1)
                nc.vector.tensor_tensor(hT[:], hT[:], pH[:], ALU.add).then_inc(h2, 1)
                dve.wait_ge(y1, UP + c + 1)
                dve.wait_ge(ydiag, UP + c + 1)
                nc.vector.tensor_tensor(yt[:], yt[:], pY[:], ALU.add).then_inc(y2, 1)

            def turn(c, s):
                decays(c + 1, 1 - s)
                enter(c + 2, s)
                through(c + 1)

            nc.vector.memset(hT[:], 0.0).then_inc(h2, 1)
            enter(0, 0)
            decays(0, 0)
            enter(1, 1)
            through(0)
            turns(dve, turn)
            decays(TB - 1, 1)
            through(TB - 1)


def ssd_sample(nc, arena, banks, d, o, g, xc, y, dt, dtA, ones, ident, kept):
    R, PD = SH // SG, DI // SH
    HP = R // 2
    with Phase(nc, "ss", arena, banks=banks) as ph:
        H = ph.sb("H", [P, HP, NB, DS])
        T = ph.sb("T", [P, NB, DS])
        xs = ph.sb("xs", [NB, XT * P])
        dA = ph.sb("dA", [NB, R])
        dAx = ph.sb("dAx", [NB, R * PD])
        dAf = ph.sb("dAf", [P, HP, NB])
        eye = ph.sb("eye", [NB, 2, NB, DS])
        pX = ph.ps("pX", [NB, 2, 512])
        pA = ph.ps("pA", [P, HP, NB])
        pC = ph.ps("pC", [P, NB, DS])
        pU = ph.ps("pU", [P, NB, DS])
        H_in, turned, moved, exped, dAturn, ch_s, diag, mmc, mmu, upd = (
            ph.sem(n) for n in ("H_in", "turned", "moved", "exped", "dAturn", "ch", "diag", "mmc", "mmu", "upd"))
        block = ph.block()
        heads = bass.ds(g * R, R)
        chunks = lambda a: a.rearrange("p b n -> p (b n)")

        @block.sync
        def _(sp):
            sp.dma_start(H[:].rearrange("p q b n -> p (q b n)"), d["state_ssm"][g]).then_inc(H_in, 16)
            sp.wait_ge(upd, UP + HP)
            sp.dma_start(o["ssm_s"][g], H[:].rearrange("p q b n -> p (q b n)")).then_inc(kept, 16)

        @block.scalar
        def _(act):
            nc.scalar.activation(dA[:], dtA[0:NB, TB, heads], ACT.Exp).then_inc(exped, 1)

        @block.tensor
        def _(pe):
            for t in range(XT):
                m = nc.tensor.transpose(pX[:, t // 4, (t % 4) * P:(t % 4 + 1) * P], xc[:, t, SEQ:TOK], ident[:])
            m.then_inc(turned, 1)
            pe.wait_ge(moved, UP + 2)
            for t in range(HP):
                m = nc.tensor.transpose(pA[:, t], dAx[:, t * P:(t + 1) * P], ident[0:NB, 0:NB])
            m.then_inc(dAturn, 1)
            pe.wait_ge(diag, UP + 1)
            for c in range(2):
                m = nc.tensor.matmul(chunks(pC[:])[:, c * 512:(c + 1) * 512], ones[0:NB, :],
                                     chunks(eye[:, 1])[:, c * 512:(c + 1) * 512], start=True, stop=True)
            m.then_inc(mmc, 1)
            for t in range(HP):
                pe.wait_ge(upd, UP + t) if t else None
                for c in range(2):
                    m = nc.tensor.matmul(chunks(pU[:])[:, c * 512:(c + 1) * 512], xs[:, t * P:(t + 1) * P],
                                         chunks(eye[:, 0])[:, c * 512:(c + 1) * 512], start=True, stop=True)
                m.then_inc(mmu, 1)

        @block.vector
        def _(dve):
            ch = Chain(dve, ch_s)
            dve.wait_ge(exped, UP + 1)
            nc.vector.tensor_copy(dAx[:].rearrange("b (r p) -> b r p", r=R), dA[:].unsqueeze(2).to_broadcast([NB, R, PD])).then_inc(moved, 1)
            dve.wait_ge(turned, UP + 1)
            nc.vector.tensor_copy(xs[:], pX[:].rearrange("b a n -> b (a n)")[:, 0:XT * P]).then_inc(moved, 1)
            dve.wait_ge(moved, UP + 2)
            xv = xs[:, 0:R * PD].rearrange("b (r p) -> b r p", r=R)
            ch.link(nc.vector.tensor_tensor(xv, xv, dt[0:NB, TB, heads].unsqueeze(2).to_broadcast([NB, R, PD]), ALU.mult))
            for j in range(2):
                ch.link(nc.vector.tensor_tensor(eye[:, j], xs[:, (4 + j) * P:(5 + j) * P].unsqueeze(1).to_broadcast([NB, NB, DS]),
                                                ident[0:NB, 0:NB].unsqueeze(2).to_broadcast([NB, NB, DS]), ALU.mult))
            dve.sem_inc(diag, 1)
            dve.wait_ge(dAturn, UP + 1)
            ch.link(nc.vector.tensor_copy(dAf[:], pA[:]))
            dve.wait_ge(H_in, UP + 16)
            dve.wait_ge(mmc, UP + 1)
            for t in range(HP):
                ch.link(nc.vector.tensor_tensor(H[:, t], H[:, t], dAf[:, t].unsqueeze(2).to_broadcast([P, NB, DS]), ALU.mult))
                dve.wait_ge(mmu, UP + t + 1)
                nc.vector.tensor_tensor(H[:, t], H[:, t], pU[:], ALU.add).then_inc(upd, 1)
                dve.wait_ge(upd, UP + t + 1)
                ch.link(nc.vector.tensor_tensor(T[:], H[:, t], pC[:], ALU.mult))
                ch.link(nc.vector.tensor_reduce(y[:, t, SEQ:TOK], T[:], AX, ALU.add))


def ssd_out(nc, arena, banks, start, kept, d, g, xc, zs, y, ones, dskip, nssd, S, mask):
    GT = 4
    with Phase(nc, "so", arena, start, banks=banks) as ph:
        w = ph.sb("w", [P, 2, GT, P])
        sq = ph.sb("sq", [P, 2, TOK])
        rstd = ph.sb("rstd", [P, TOK])
        eps = ph.sb("eps", [P, 1])
        m8 = ph.sb("m8", [P, len(CHOSEN), 8])
        found, tick = ph.sem("found"), ph.sem("tick")
        ps = [ph.ps(f"ps{q}", [P, NCH, 512]) for q in range(2)]
        w_in = [ph.sem(f"w_in{q}") for q in range(2)]
        read = [ph.sem(f"read{q}") for q in range(2)]
        eps_set, skip, gated, squared, summed, root, inv, scaled, mm = (
            ph.sem(n) for n in ("eps_set", "skip", "gated", "squared", "summed", "root", "inv", "scaled", "mm"))
        block = ph.block()

        @block.sync
        def _(sp):
            sp.wait_ge(kept, 16 * (g + 1))
            load_tiles(sp, w, w_in, mm, NCH, d["w_so"][g], KT)

        @block.scalar
        def _(act):
            for t in range(GT):
                act.wait_ge(gated, UP + t + 1)
                if t >= 2:
                    act.wait_ge(summed, UP + t - 1)
                nc.scalar.activation(sq[:, t % 2], y[:, t], ACT.Square).then_inc(squared, 1)
            act.wait_ge(summed, UP + GT)
            act.wait_ge(eps_set, UP + 1)
            nc.scalar.activation(rstd[:].rearrange("p (n c) -> p n c", n=NCH), ps[1][:, :, 0:NC], ACT.Sqrt,
                                 scale=1.0 / (GT * P), bias=eps[:]).then_inc(root, 1)

        @block.tensor
        def _(pe):
            for t in range(GT):
                pe.wait_ge(squared, UP + t + 1)
                for n in range(NCH):
                    m = nc.tensor.matmul(ps[1][:, n, 0:NC], ones[:], sq[:, t % 2, n * NC:(n + 1) * NC],
                                         start=t == 0, stop=t == GT - 1)
                m.then_inc(summed, 1)
            project_tiles(pe, nc, w, ps, y, w_in, mm, read, KT, kt=GT, made=(scaled, GT))

        @block.vector
        def _(dve):
            nc.vector.memset(eps[:], EPS).then_inc(eps_set, 1)
            for t in range(GT):
                nc.vector.scalar_tensor_tensor(out=y[:, t], in0=xc[:, t], scalar=dskip[:, bass.ds(g * GT + t, 1)], in1=y[:, t],
                                               op0=ALU.mult, op1=ALU.add).then_inc(skip, 1)
                dve.wait_ge(skip, UP + t + 1)
                nc.vector.tensor_tensor(y[:, t], y[:, t], zs[:, t], ALU.mult).then_inc(gated, 1)
            dve.wait_ge(root, UP + 1)
            dve.wait_ge(gated, UP + GT)
            for c in range(NCH):
                at = slice(c * NC, (c + 1) * NC)
                nc.vector.reciprocal(rstd[:, at], rstd[:, at]).then_inc(inv, 1)
                dve.wait_ge(inv, UP + c + 1)
                for t in range(GT):
                    nc.vector.scalar_tensor_tensor(out=y[:, t, at], in0=y[:, t, at], scalar=nssd[:, bass.ds(g * GT + t, 1)],
                                                   in1=rstd[:, at], op0=ALU.mult, op1=ALU.mult).then_inc(scaled, 1)
            with dve.Fori(0, KT // 2) as i:
                top_round(dve, nc, chosen_rows(mask), m8, found, tick, 2 * len(CHOSEN) * i)
                for q in range(2):
                    for c in range(NCH):
                        dve.wait_ge(mm, UP + NCH * (2 * i + q) + c + 1)
                        part = S[:, 2 * i + q, c * NC:(c + 1) * NC]
                        nc.vector.tensor_tensor(part, part, ps[q][:, c, 0:NC], ALU.add).then_inc(read[q], 1)
            for q in range(2):
                dve.wait_ge(read[q], UP + NCH * KT // 2)


def final_norm(nc, o, x, y, ones, gain_d):
    with Phase(nc, "fn") as ph:
        sq = ph.sb("sq", [P, 2, TOK])
        rstd = ph.sb("rstd", [P, TOK])
        eps = ph.sb("eps", [P, 1])
        gain = ph.sb("gain", [P, KT])
        ps = ph.ps("ps", [P, NCH, 512])
        gain_in, eps_set, squared, summed, root, inv, scaled, saved = (
            ph.sem(n) for n in ("gain_in", "eps_set", "squared", "summed", "root", "inv", "scaled", "saved"))
        block = ph.block()

        @block.sync
        def _(sp):
            sp.dma_start(gain[:], gain_d).then_inc(gain_in, 16)
            for k in range(KT):
                sp.wait_ge(scaled, UP + k + 1)
                sp.dma_start(o["y"][:, k], y[:, k]).then_inc(saved, 16)
            sp.wait_ge(saved, UP + 16 * KT)

        @block.scalar
        def _(act):
            for k in range(KT):
                if k >= 2:
                    act.wait_ge(summed, UP + k - 1)
                nc.scalar.activation(sq[:, k % 2], x[:, k], ACT.Square).then_inc(squared, 1)
            act.wait_ge(summed, UP + KT)
            act.wait_ge(eps_set, UP + 1)
            nc.scalar.activation(rstd[:].rearrange("p (n c) -> p n c", n=NCH), ps[:, :, 0:NC], ACT.Sqrt,
                                 scale=1.0 / DM, bias=eps[:]).then_inc(root, 1)

        @block.tensor
        def _(pe):
            for k in range(KT):
                pe.wait_ge(squared, UP + k + 1)
                for n in range(NCH):
                    m = nc.tensor.matmul(ps[:, n, 0:NC], ones[:], sq[:, k % 2, n * NC:(n + 1) * NC],
                                         start=k == 0, stop=k == KT - 1)
                m.then_inc(summed, 1)

        @block.vector
        def _(dve):
            nc.vector.memset(eps[:], EPS).then_inc(eps_set, 1)
            dve.wait_ge(root, UP + 1)
            nc.vector.reciprocal(rstd[:], rstd[:]).then_inc(inv, 1)
            dve.wait_ge(inv, UP + 1)
            dve.wait_ge(gain_in, UP + 16)
            for k in range(KT):
                nc.vector.scalar_tensor_tensor(out=y[:, k], in0=x[:, k], scalar=gain[:, k:k + 1], in1=rstd[:],
                                               op0=ALU.mult, op1=ALU.mult).then_inc(scaled, 1)


def ssd_branch(nc, d, o, scr, kept, h, tok, ones, ident, S, mask):
    with ExitStack() as c:
        sb = lambda n, s: c.enter_context(nc.sbuf_tensor(n, s, F32))
        dt, dtA = sb("dt", [P, TB + 1, SH]), sb("dtA", [P, TB + 1, SH])
        ea, te, etot = (sb(n, [P, TB, SH]) for n in ("ea", "te", "etot"))
        upper, below = sb("upper", [P, P]), sb("below", [P, P])
        cw, cb = sb("cw", [P, SG * XT, CW]), sb("cb", [P, SG * XT])
        dskip, nssd = sb("dskip", [P, DI // P]), sb("nssd", [P, DI // P])
        hT = sb("hT", [P, DI // SG])
        constants = ((below, "below"), (cw, "conv_w"), (cb, "conv_b"), (dskip, "d_skip"), (nssd, "norm_ssd"))
        time_steps(nc, d, o, tok, dt, dtA, ea, te, etot, upper, constants, S)
        xc, zs, y = sb("xc", [P, XT, TOK]), sb("zs", [P, 4, TOK]), sb("y", [P, 4, TOK])
        arena = sb("arena", [P, 10602])
        banks = c.enter_context(nc.psum_tensor("banks", [P, 8 * 512], F32))
        start, xb = carve(arena, 0, [P, XT, CW - 1 + TOK])
        with nc.Fori(0, SG) as g:
            ssd_project(nc, arena, banks, start, d, o, scr, g, h, xb, xc, zs, cw, cb, y, mask)
            ssd_scan(nc, arena, banks, o, g, xc, y, dt, dtA, ea, te, etot, upper, below, ident, hT)
            ssd_sample(nc, arena, banks, d, o, g, xc, y, dt, dtA, ones, ident, kept)
            ssd_out(nc, arena, banks, SH // SG // 2 * NB * DS, kept, d, g, xc, zs, y, ones, dskip, nssd, S, mask)


def by_page(a):
    return a.rearrange("(c b) (i s) -> (b i) c s", c=2, s=PAGE)


def gate_and_gather(nc, d, scr, h, S, mask, ident, gathered, cnt, seln, kvb, brows, spare):
    RING = 2 * NPAGE
    with Phase(nc, "gg") as ph:
        w = ph.sb("w", [P, 2, KT, P])
        g = spare[:].rearrange("p q (c n) -> p q c n", c=NCH)
        pt = ph.sb("pt", [P, 2, P])
        page_pos = ph.sb("page_pos", [P, NB * NPAGE])
        iota = ph.sb("iota", [P, TOPK], F16)
        vals = ph.sb("vals", [P, NB * NPAGE, 3], F16)
        tab = ph.sb("tab", [P, NB * NPAGE], I32)
        hots = ph.sb("hots", [P, RING, TOPK], F16)
        ent = ph.sb("ent", [P, NB, 2, 3])
        where = ph.sb("where", [P, 3, NB, 2])
        row = ph.sb("row", [P, NB, 2], U32)
        brow = ph.sb("brow", [P, NB, 2], U32)
        sel, pos = kvb[0:NB, 0:PAST + 1], kvb[0:NB, PAST + 1:2 * PAST + 1]
        kv = kv_view(kvb)
        ps = ph.ps("ps", [P, NCH, 512])
        pT = ph.ps("pT", [P, 2, P])
        pE = [[ph.ps(f"pE{q}{f}", [P, 512]) for f in range(2)] for q in range(2)]
        w_in = [ph.sem(f"w_in{q}") for q in range(2)]
        gmm, gread, mult, ranked, stored, s_saved, masked, back = (
            ph.sem(n) for n in ("gmm", "gread", "mult", "ranked", "stored", "s_saved", "masked", "back"))
        loaded, top_in, turned, valsd, hotd, used, read, ch_s, ready = (
            ph.sem(n) for n in ("loaded", "top_in", "turned", "valsd", "hotd", "used", "read", "ch", "ready"))
        block = ph.block()
        BEFORE = 2

        @block.sync
        def _(sp):
            sp.dma_start(sel[:, 0:PAST], scr["score"]).then_inc(top_in, 16)
            sp.dma_start(sel[:, PAST:PAST + 1], scr["snew"]).then_inc(top_in, 16)
            load_tiles(sp, w, w_in, gmm, NCH, d["w_gs"], KT)
            sp.wait_ge(mult, UP + KT // 2)
            sp.dma_start(scr["S"][:, 0:KT // 2], S[:, 0:KT // 2]).then_inc(s_saved, 16)
            sp.wait_ge(mult, UP + KT)
            sp.dma_start(scr["S"][:, KT // 2:KT], S[:, KT // 2:KT]).then_inc(s_saved, 16)
            sp.wait_ge(s_saved, UP + 32)

        @block.scalar
        def _(act):
            def gate(t):
                if t >= 2:
                    act.wait_ge(mult, UP + t - 1)
                for c in range(NCH):
                    act.wait_ge(gmm, UP + NCH * t + c + 1)
                    nc.scalar.activation(g[:, t % 2, c], ps[:, c, 0:NC], ACT.Sigmoid).then_inc(gread, 1)

            act.dma_start(iota[:], d["iota"]).then_inc(loaded, 16)
            act.dma_start(vals[:], d["slots"]).then_inc(loaded, 16)
            act.dma_start(tab[:], d["page_table"].to_broadcast([P, NB * NPAGE])).then_inc(loaded, 16)
            gate(0)
            gate(1)
            act.wait_ge(ranked, UP + 1)
            act.dma_start(scr["pos"], pos).then_inc(stored, 16)
            act.wait_ge(stored, UP + 16)
            act.dma_start(pt[:], by_page(scr["pos"])).then_inc(back, 16)
            for t in range(BEFORE, KT):
                gate(t)
            act.wait_ge(back, UP + 16)

        @block.tensor
        def _(pe):
            def gate(i, q):
                pe.wait_ge(w_in[q], UP + 16 * (i + 1))
                for c in range(NCH):
                    if not (isinstance(i, int) and i == 0 and q == 0):
                        pe.wait_ge(gread, UP + NCH * (2 * i + q - 1) + c + 1)
                    for k in range(KT):
                        m = nc.tensor.matmul(ps[:, c, 0:NC], w[:, q, k], h[:, k, c * NC:(c + 1) * NC],
                                             start=k == 0, stop=k == KT - 1)
                    m.then_inc(gmm, 1)

            gate(0, 0)
            gate(0, 1)
            pe.wait_ge(back, UP + 16)
            for c in range(2):
                m = nc.tensor.transpose(pT[:, c], pt[:, c], ident[:])
            m.then_inc(turned, 1)
            pe.wait_ge(valsd, UP + 1)
            with pe.Fori(0, NB // 4) as i:
                for q in range(2):
                    gate(BEFORE // 2 + i, q)
                    for r in range(2):
                        b = 4 * i + 2 * q + r
                        pe.wait_ge(read, UP + 4 * i + 2 * q)
                        pe.wait_ge(hotd, UP + NPAGE * (b + 1))
                        for p in range(NPAGE):
                            for f in range(2):
                                m = nc.tensor.matmul(pE[r][f][:, 0:3], hots[:, r * NPAGE + p, f * P:(f + 1) * P],
                                                     vals[:, b * NPAGE + p], start=p == 0, stop=p == NPAGE - 1)
                        m.then_inc(used, 1)
            gate(KT // 2 - 1, 0)
            gate(KT // 2 - 1, 1)

        @block.vector
        def _(dve):
            ch = Chain(dve, ch_s)

            def gate(t, q):
                dve.wait_ge(gread, UP + NCH * (t + 1))
                nc.vector.tensor_tensor(S[:, t], S[:, t], g[:, q].rearrange("p c n -> p (c n)"), ALU.mult).then_inc(mult, 1)

            dve.wait_ge(top_in, UP + 32)
            ch.link(nc.vector.tensor_scalar(sel, sel, -3.2e38, None, ALU.is_lt))
            ch.link(nc.vector.tensor_tensor_scan(pos, sel[:, 0:PAST], sel[:, 0:PAST], 0.0, ALU.add, ALU.max))
            ch.link(nc.vector.tensor_copy(cnt[:], pos[:, PAST - 1:PAST]))
            ch.link(nc.vector.tensor_copy(seln[:], sel[:, PAST:PAST + 1]))
            ch.link(nc.vector.tensor_tensor(pos, pos, sel[:, 0:PAST], ALU.mult))
            ch.link(nc.vector.tensor_scalar(pos, pos, -1.0, None, ALU.add))
            dve.sem_inc(ranked, 1)
            gate(0, 0)
            dve.wait_ge(loaded, UP + 48)
            nc.vector.tensor_copy(vals[:, :, 1], tab[:]).then_inc(valsd, 1)
            gate(1, 1)
            part = mask[:, mask_at(FIRST):mask_at(TB)]
            nc.vector.tensor_scalar(part, part, -3.2e38, -BIG, ALU.is_gt, ALU.mult).then_inc(masked, 1)
            dve.wait_ge(turned, UP + 1)
            ch.link(nc.vector.tensor_copy(page_pos[:], pT[:].rearrange("p c n -> p (c n)")))
            def one_hots(b):
                if b >= 2:
                    dve.wait_ge(used, UP + b - 1)
                for p in range(NPAGE):
                    nc.vector.tensor_scalar(hots[:, b % 2 * NPAGE + p], iota[:], page_pos[:, b * NPAGE + p:b * NPAGE + p + 1], None,
                                            ALU.is_equal).then_inc(hotd, 1)

            def rows(j):
                for b in (2 * j, 2 * j + 1):
                    dve.wait_ge(used, UP + b + 1)
                    for f in range(2):
                        v = nc.vector.tensor_copy(ent[:, b, f], pE[b % 2][f][:, 0:3])
                    v.then_inc(read, 1)
                dve.wait_ge(read, UP + 2 * j + 2)
                two = slice(2 * j, 2 * j + 2)
                off, page, log = (ent[:, two, :, n] for n in range(3))
                at, rel = where[:, 0, two], where[:, 1, two]
                ch.link(nc.vector.scalar_tensor_tensor(out=at, in0=page, scalar=float(PAGE), in1=off, op0=ALU.mult, op1=ALU.add))
                ch.link(nc.vector.scalar_tensor_tensor(out=rel, in0=log, scalar=float(PAGE), in1=off, op0=ALU.mult, op1=ALU.add))
                ch.link(nc.vector.tensor_scalar(rel, rel, float(WIN - 1 - PAST), 0.0, ALU.add, ALU.max))
                ch.link(nc.vector.tensor_copy(row[:, two], at))
                ch.link(nc.vector.tensor_copy(brow[:, two], rel))
                dve.sem_inc(ready, 1)

            for j in range(NB // 2):
                one_hots(2 * j)
                if j:
                    gate(BEFORE + j - 1, (j - 1) % 2)
                    rows(j - 1)
                one_hots(2 * j + 1)
            gate(BEFORE + NB // 2 - 1, 1)
            rows(NB // 2 - 1)
            gate(KT - 2, 0)
            gate(KT - 1, 1)

        @block.gpsimd
        def _(pool):
            pool.wait_ge(stored, UP + 16)
            n = 0
            for b in range(NB):
                pool.wait_ge(ready, UP + b // 2 + 1)
                for f in range(2):
                    at = bass.IndirectOffsetOnAxis(row[:, b, f:f + 1], 0)
                    for j, src in enumerate((d["cache_k"], d["cache_v"])):
                        pool.indirect_dma_start(kv[:, b, f, j], None, src, at).then_inc(gathered, 16)
                    pool.indirect_dma_start(brows[:, b, f], None, scr["brow"],
                                            bass.IndirectOffsetOnAxis(brow[:, b, f:f + 1], 0)).then_inc(gathered, 16)
                    n += 48
            pool.wait_ge(gathered, n)


def kv_view(kvb):
    return kvb[:, 0:NB * 4 * NKV * HD].rearrange("p (b f j c) -> p b f j c", b=NB, f=2, j=2)


def sample_attend_and_out(nc, d, scr, kT, qs, tok, ones, ident, cnt, seln, kvb, brows, att, A, spare):
    UNITS = [(t, c) for t in range(KT) for c in range(NCH - 1)] + [(t, NCH - 1) for t in reversed(range(KT))]
    SLOTS = KT // 2
    RING, BANKS = 4, 3
    NS = TOPK + 1
    F = 2 * HD
    kv = kv_view(kvb)
    with Phase(nc, "s4") as ph:
        hot = ph.sb("hot", [P, 2])
        qt = ph.sb("qt", [NB, DM])
        qm = ph.sb("qm", [NB, 2, DM])
        prod = ph.sb("prod", [P, DM])
        pn = ph.sb("pn", [P, KT, NB])
        Lg = ph.sb("Lg", [P, NB, 2, NH])
        Ln = ph.sb("Ln", [NB, NH])
        bn = ph.sb("bn", [NB, NH])
        lack = ph.sb("lack", [NB, 1])
        cd = ph.sb("cd", [NB, NB])
        cb = ph.sb("cb", [P, NB])
        slot = ph.sb("slot", [P, 2])
        mb = ph.sb("mb", [P, NB, 2])
        LL = ph.sb("LL", [NH, NB, NS])
        nm = ph.sb("nm", [NH, NB])
        den = ph.sb("den", [NH, NB])
        rd = ph.sb("rd", [NH, NB])
        PT = ph.sb("PT", [P, NB, 2, NH])
        wn = ph.sb("wn", [NB, NH])
        wd = ph.sb("wd", [NB, NB, NH])
        pq = ph.ps("pq", [P, 2, DM])
        pm = ph.ps("pm", [P, 512])
        w = spare[:, 0:SLOTS * KT * P].rearrange("p (q k m) -> p q k m", q=SLOTS, k=KT)
        gs = ph.sb("gs", [P, RING, 2, NC])
        pU = [ph.ps(f"pU{q}", [P, 512]) for q in range(BANKS)]
        w_in = [ph.sem(f"w_in{q}") for q in range(SLOTS)]
        g_in = [ph.sem(f"g_in{q}") for q in range(RING)]
        umm, gated, mixed, added, attd = (ph.sem(n) for n in ("umm", "gated", "mixed", "added", "attd"))
        pL = pq[0:NH].rearrange("h a (b j) -> h (a b) j", b=NB // 2)
        small, ch_s, qturn, qmd, qb, lread, pnd, nlog, cdd, lready, lturn, mx, ex, pready, pturn, ptd, od = (
            ph.sem(n) for n in ("small", "ch", "qturn", "qmd", "qb", "lread", "pnd", "nlog", "cdd", "lready", "lturn",
                                "mx", "ex", "pready", "pturn", "ptd", "od"))
        block = ph.block()

        @block.sync
        def _(sp):
            sp.dma_start(hot[:], d["half"]).then_inc(small, 16)
            sp.dma_start(slot[:], d["slot"]).then_inc(small, 16)
            sp.dma_start(bn[:], scr["brow"][WIN - 1:WIN, :].to_broadcast([NB, NH])).then_inc(small, 16)
            for t in range(KT):
                if t >= SLOTS:
                    sp.wait_ge(umm, UP + (NCH - 1) * (t - SLOTS + 1))
                sp.dma_start(w[:, t % SLOTS], d["w_ao"][t]).then_inc(w_in[t % SLOTS], 16)
            for t in reversed(range(SLOTS)):
                sp.wait_ge(umm, UP + UNITS.index((t + SLOTS, NCH - 1)) + 1)
                sp.dma_start(w[:, t], d["w_ao"][t]).then_inc(w_in[t], 16)
            sp.wait_ge(small, UP + 48)

        @block.tensor
        def _(pe):
            def unit(u):
                t, c = UNITS[u]
                loads = 2 if t >= SLOTS else 1 if c < NCH - 1 else 3
                pe.wait_ge(w_in[t % SLOTS], UP + 16 * loads)
                if u >= BANKS:
                    pe.wait_ge(mixed, UP + u - BANKS + 1)
                for k in range(KT):
                    m = nc.tensor.matmul(pU[u % BANKS][:, 0:NC], w[:, t % SLOTS, k], att[:, k, c * NC:(c + 1) * NC],
                                         start=k == 0, stop=k == KT - 1)
                m.then_inc(umm, 1)

            for t in range(KT):
                m = nc.tensor.transpose(pq[0:NB, 1, t * P:(t + 1) * P], qs[:, t], ident[:])
            m.then_inc(qturn, 1)
            unit(0)
            pe.wait_ge(small, UP + 48)
            pe.wait_ge(pnd, UP + 1)
            for t in range(KT):
                m = nc.tensor.matmul(pm[0:NB, 2 * t:2 * t + 2], pn[:, t], hot[:], start=True, stop=True)
            pe.wait_ge(cdd, UP + 1)
            nc.tensor.matmul(pm[:, 16:16 + NB], ones[0:NB, :], cd[:], start=True, stop=True).then_inc(nlog, 1)
            unit(1)
            for b in range(NB):
                pe.wait_ge(qmd, UP + b + 1)
                if b >= 2:
                    pe.wait_ge(lread, UP + b - 1)
                for c in range(2):
                    m = nc.tensor.matmul(pq[:, b % 2, c * 512:(c + 1) * 512], ones[0:NB, :], qm[:, b % 2, c * 512:(c + 1) * 512],
                                         start=True, stop=True)
                m.then_inc(qb, 1)
                unit(2 + b)
            pe.wait_ge(lready, UP + 1)
            for b in range(NB):
                for f in range(2):
                    nc.tensor.transpose(pL[:, b, f * P:(f + 1) * P], Lg[:, b, f], ident[:])
            nc.tensor.transpose(pm[0:NH, 64:64 + NB], Ln[:], ident[0:NB, 0:NB]).then_inc(lturn, 1)
            unit(10)
            unit(11)
            pe.wait_ge(pready, UP + 1)
            for b in range(NB):
                for f in range(2):
                    at = (2 * b + f) * NH
                    nc.tensor.transpose(pq[:, 0, at:at + NH], LL[:, b, f * P:(f + 1) * P], ident[0:NH, 0:NH])
            nc.tensor.transpose(pq[0:NB, 1, 0:NH], LL[:, :, TOPK], ident[0:NH, 0:NH]).then_inc(pturn, 1)
            unit(12)
            pe.wait_ge(ptd, UP + 1)
            for b in range(NB):
                for m in range(2):
                    out = pm[:, 128 + (2 * b + m) * NH:128 + (2 * b + m + 1) * NH]
                    for f in range(2):
                        nc.tensor.matmul(out, kv[:, b, f, 1, m * F:(m + 1) * F], PT[:, b, f], start=f == 0, stop=False)
                    x = nc.tensor.matmul(out, tok[0:NB, TB, m * F:(m + 1) * F], wd[:, b], start=False, stop=True)
            x.then_inc(od, 1)
            for u in (13, 14, 15):
                unit(u)
            pe.wait_ge(attd, UP + 1)
            for u in range(16, len(UNITS)):
                unit(u)

        @block.scalar
        def _(act):
            def load(u):
                t, c = UNITS[u]
                if u >= RING:
                    act.wait_ge(added, UP + u - RING + 1)
                for j, n in enumerate(("ga", "S")):
                    act.dma_start(gs[:, u % RING, j], scr[n][:, t, c * NC:(c + 1) * NC]).then_inc(g_in[u % RING], 16)

            def gate(u):
                act.wait_ge(g_in[u % RING], UP + 32 * (u // RING + 1))
                nc.scalar.activation(gs[:, u % RING, 0], gs[:, u % RING, 0], ACT.Sigmoid).then_inc(gated, 1)

            for u in range(RING - 1):
                load(u)
            for u in range(len(UNITS)):
                if u + RING - 1 < len(UNITS):
                    load(u + RING - 1)
                gate(u)
                if u == 11:
                    act.wait_ge(mx, UP + 1)
                    for b in range(NB):
                        nc.scalar.activation(LL[:, b], LL[:, b], ACT.Exp, bias=nm[:, b:b + 1], accum_out=den[:, b:b + 1]).then_inc(ex, 1)

        @block.vector
        def _(dve):
            ch = Chain(dve, ch_s)

            def take(u):
                t, c = UNITS[u]
                part = A[:, t, c * NC:(c + 1) * NC]
                dve.wait_ge(gated, UP + u + 1)
                dve.wait_ge(umm, UP + u + 1)
                nc.vector.tensor_tensor(part, gs[:, u % RING, 0], pU[u % BANKS][:, 0:NC], ALU.mult).then_inc(mixed, 1)
                dve.wait_ge(mixed, UP + u + 1)
                nc.vector.tensor_tensor(part, part, gs[:, u % RING, 1], ALU.add).then_inc(added, 1)

            def mask_query(b):
                if b >= 2:
                    dve.wait_ge(qb, UP + b - 1)
                nc.vector.tensor_scalar(qm[:, b % 2], qt[:], ident[0:NB, b:b + 1], None, ALU.mult).then_inc(qmd, 1)

            nc.vector.tensor_tensor(pn[:].rearrange("p (m g) b -> p m g b", m=2),
                                    qs[:].rearrange("p (m g) b -> p m g b", m=2),
                                    kT[:, :, SEQ:TOK].unsqueeze(2).to_broadcast([P, 2, 4, NB]), ALU.mult).then_inc(pnd, 1)
            ch.link(nc.vector.tensor_tensor(cd[:], cnt[:].to_broadcast([NB, NB]), ident[0:NB, 0:NB], ALU.mult))
            dve.sem_inc(cdd, 1)
            dve.wait_ge(qturn, UP + 1)
            ch.link(nc.vector.tensor_copy(qt[:], pq[0:NB, 1]))
            mask_query(0)
            take(0)
            dve.wait_ge(nlog, UP + 1)
            dve.wait_ge(small, UP + 48)
            ch.link(nc.vector.scalar_tensor_tensor(out=Ln[:], in0=pm[0:NB, 0:NH], scalar=float(HD ** -0.5), in1=bn[:],
                                                   op0=ALU.mult, op1=ALU.add))
            ch.link(nc.vector.tensor_copy(cb[:], pm[:, 16:16 + NB]))
            ch.link(nc.vector.tensor_scalar(lack[:], seln[:], 1.0, BIG, ALU.subtract, ALU.mult))
            ch.link(nc.vector.tensor_scalar(Ln[:], Ln[:], lack[:], None, ALU.add))
            ch.link(nc.vector.tensor_tensor(mb[:], slot[:].unsqueeze(1).to_broadcast([P, NB, 2]),
                                            cb[:].unsqueeze(2).to_broadcast([P, NB, 2]), ALU.is_ge))
            ch.link(nc.vector.tensor_scalar(mb[:], mb[:], -BIG, None, ALU.mult))
            take(1)
            for b in range(NB):
                if b + 1 < NB:
                    mask_query(b + 1)
                dve.wait_ge(qb, UP + b + 1)
                for f in range(2):
                    k4 = kv[:, b, f, 0].rearrange("p (m c) -> p m c", m=2).unsqueeze(2).to_broadcast([P, 2, 4, F])
                    x = nc.vector.tensor_tensor(prod[:].rearrange("p (m g c) -> p m g c", m=2, g=4), k4,
                                                pq[:, b % 2].rearrange("p (m g c) -> p m g c", m=2, g=4), ALU.mult)
                    ch.link(x)
                    ch.link(nc.vector.tensor_reduce(Lg[:, b, f], prod[:].rearrange("p (h c) -> p h c", c=HD), AX, ALU.add))
                dve.sem_inc(lread, 1)
                take(2 + b)
            fl = lambda a: a[:].rearrange("p b f h -> p (b f) h")
            ch.link(nc.vector.scalar_tensor_tensor(out=fl(Lg), in0=fl(Lg), scalar=float(HD ** -0.5), in1=fl(brows),
                                                   op0=ALU.mult, op1=ALU.add))
            ch.link(nc.vector.tensor_tensor(fl(Lg), fl(Lg), mb[:].rearrange("p b f -> p (b f)").unsqueeze(2).to_broadcast([P, 2 * NB, NH]),
                                            ALU.add))
            dve.sem_inc(lready, 1)
            dve.wait_ge(lturn, UP + 1)
            ch.link(nc.vector.tensor_copy(LL[:, :, 0:TOPK], pL[:]))
            ch.link(nc.vector.tensor_copy(LL[:, :, TOPK], pm[0:NH, 64:64 + NB]))
            nc.vector.tensor_reduce(nm[:], LL[:], AX, ALU.max, negate=True).then_inc(mx, 1)
            take(10)
            take(11)
            dve.wait_ge(ex, UP + NB)
            ch.link(nc.vector.reciprocal(rd[:], den[:]))
            ch.link(nc.vector.tensor_tensor(LL[:], LL[:], rd[:].unsqueeze(2).to_broadcast([NH, NB, NS]), ALU.mult))
            dve.sem_inc(pready, 1)
            dve.wait_ge(pturn, UP + 1)
            ch.link(nc.vector.tensor_copy(PT[:].rearrange("p b f h -> p (b f h)"), pq[:, 0, 0:2 * NB * NH]))
            ch.link(nc.vector.tensor_copy(wn[:], pq[0:NB, 1, 0:NH]))
            ch.link(nc.vector.tensor_tensor(wd[:], wn[:].unsqueeze(1).to_broadcast([NB, NB, NH]),
                                            ident[0:NB, 0:NB].unsqueeze(2).to_broadcast([NB, NB, NH]), ALU.mult))
            dve.sem_inc(ptd, 1)
            take(12)
            dve.wait_ge(od, UP + 1)
            ov = pm[:, 128:128 + 2 * NB * NH].rearrange("p (b m h) -> p m h b", b=NB, m=2)
            for m in range(2):
                for u in range(2):
                    r = slice(u * HD, (u + 1) * HD)
                    ch.link(nc.vector.tensor_copy(att[r, 4 * m:4 * m + 4, SEQ:TOK], ov[r, m, 8 * m + u:8 * m + 8:2]))
            dve.sem_inc(attd, 1)
            for u in range(13, len(UNITS)):
                take(u)
            dve.wait_ge(added, UP + len(UNITS))


def program(nc, d, o):
    dram = lambda n, s: nc.dram_tensor(f"scr_{n}", s, F32).ap()
    scr = {"byh": dram("byh", [NH, 512]), "brow": dram("brow", [WIN, NH]), "x": dram("x", [P, KT, TOK]),
           "S": dram("S", [P, KT, TOK]), "ga": dram("ga", [P, KT, TOK]),
           "qk": dram("qk", [P, QI0, TOK]), "snew": dram("snew", [NB, 1]), "score": dram("score", [NB, PAST]),
           "pos": dram("pos", [NB, PAST]), "kidx": dram("kidx", [NB * NPAGE, 2, ID * PAGE // 2])}
    with ExitStack() as ctx:
        def buf(c, n, s, t=F32):
            return c.enter_context(nc.sbuf_tensor(n, s, t))

        gathered, paged, kept = (ctx.enter_context(nc.semaphore(n)) for n in ("gathered", "paged", "kept"))
        Phase.share(nc, ctx, 32)
        ada, sg = buf(ctx, "ada", [P, NA, NCOND]), buf(ctx, "sg", [P, 3, KT, NCOND])
        ones, ident = buf(ctx, "ones", [P, P]), buf(ctx, "ident", [P, P])
        h = buf(ctx, "h", [P, KT, TOK])
        with ExitStack() as c1:
            x = buf(c1, "x", [P, KT, TOK])
            c, b_ada, gains = buf(c1, "c", [P, KT, NCOND]), buf(c1, "b_ada", [P, NA]), buf(c1, "gains", [P, 3, KT])
            first_norm(nc, d, x, h, ones, ident, c, b_ada, gains, ada, sg)
            ffn(nc, "f1", d["w_f1i"], d["w_f1o"], x, h, ada, 0, late=(d, c, b_ada, gains, sg))
            norm_mod(nc, "n2", x, h, ones, ada, sg, 1, store=scr["x"])
        with ExitStack() as c2:
            tok = buf(c2, "tok", [P, TB + 1, VW])
            mask = buf(c2, "mask", [P, mask_at(TB)])
            cnt, seln = (buf(c2, n, [NB, 1]) for n in ("cnt", "seln"))
            with ExitStack() as c3:
                pj = buf(c3, "pj", [P, AT, TOK])
                project_attention(nc, d, o, scr, paged, h, pj, tok)
                index_scores(nc, d, scr, pj, tok, ones, ident, mask)
            S = buf(c2, "S", [P, KT, TOK])
            ssd_branch(nc, d, o, scr, kept, h, tok, ones, ident, S, mask)
            att = S
            kvb = buf(c2, "kvb", [P, 2 * (PAST + 1)])
            brows = buf(c2, "brows", [P, NB, 2, NH])
            kT, qs = buf(c2, "kT", [P, 2, TOK]), buf(c2, "qs", [P, NH // 2, NB])
            with ExitStack() as c3:
                bias = buf(c3, "bias", [P, NH, WIN])
                tables(nc, d, scr, bias)
                gate_and_gather(nc, d, scr, h, S, mask, ident, gathered, cnt, seln, kvb, brows, kT)
                attend(nc, d, scr, h, kT, qs, tok, mask, bias, ident, att)
            sample_attend_and_out(nc, d, scr, kT, qs, tok, ones, ident, cnt, seln, kvb, brows, att, h, mask)
        x = buf(ctx, "x3", [P, KT, TOK])
        mix_out(nc, d, scr["x"], x, h, ada)
        norm_mod(nc, "n3", x, h, ones, ada, sg, 2)
        ffn(nc, "f2", d["w_f2i"], d["w_f2o"], x, h, ada, 2)
        final_norm(nc, o, x, h, ones, d["norm_final"])


def tiled(w, cols):
    k, m = w.shape
    return np.ascontiguousarray(w.reshape(k // P, P, m // cols, cols).transpose(2, 1, 0, 3))


def fmajor(a):
    r, f = a.shape
    return np.ascontiguousarray(a.T.reshape(f // P, P, r).transpose(1, 0, 2))


def layout(i):
    a = {}
    a["x"] = fmajor(np.concatenate([i["x_prompt"][0], i["x_sample"][:, 0]], 0))
    a["c"] = fmajor(np.concatenate([i["c_prompt"], i["c_sample"]], 0))
    a["w_ada"] = tiled(i["w_ada"][0], P)
    a["b_ada"] = np.ascontiguousarray(i["b_ada"][0].reshape(NA, P).T)
    gains = np.stack([i["norm_ffn1"][0], i["norm_mix"][0], i["norm_ffn2"][0]])
    a["gains"] = np.ascontiguousarray(gains.reshape(3, KT, P).transpose(2, 0, 1))
    for n in (1, 2):
        wi = tiled(i[f"w_ffn{n}_in"][0], P)
        a[f"w_f{n}i"] = np.ascontiguousarray(np.stack([wi[:FT], wi[FT:]], 2)).reshape(FT, P, 2 * KT * P)
        wo = tiled(i[f"w_ffn{n}_out"][0], P)
        a[f"w_f{n}o"] = np.ascontiguousarray(wo.reshape(KT, P, 2, FT // 2, P).transpose(0, 2, 1, 3, 4)).reshape(2 * KT, P, FT // 2, P)
    cut = np.cumsum([0, NH * HD, NKV * HD, NKV * HD, NIH * ID, ID, NIH, DI, CONVD, SH, DM, DM])
    q, k, v, qi, ki, wi, z, xbc, dt, ga, gs = (i["w_in"][0][:, cut[n]:cut[n + 1]] for n in range(11))
    q = q[:, HEADCOLS]
    a["w_att"] = tiled(np.concatenate([q, k, qi, ki, ki], 1), P)
    wt = np.concatenate([v, wi, dt], 1)
    a["w_tok"] = np.ascontiguousarray(wt.reshape(KT, P, VW).transpose(1, 0, 2))
    a["w_ao"] = tiled(i["w_attn_out"][0][HEADCOLS], P)
    a["w_ga"] = tiled(ga, P)
    a["w_gs"] = tiled(gs, P)
    a["w_out"] = tiled(i["w_out"][0], P)
    xt, zt = tiled(xbc, P)[ORDER].reshape(SG, XT, P, KT, P), tiled(z, P).reshape(SG, 4, P, KT, P)
    a["w_ssd"] = np.concatenate([xt, zt], 1)
    a["w_so"] = np.ascontiguousarray(i["w_ssd_out"][0].reshape(SG, 4, P, KT, P).transpose(0, 3, 2, 1, 4))
    ctile = lambda v: v.reshape(v.shape[:-1] + (CONVD // P, P))[..., ORDER, :]
    a["conv_w"] = np.ascontiguousarray(ctile(i["conv_w"][0]).transpose(2, 1, 0))
    a["conv_b"] = np.ascontiguousarray(ctile(i["conv_b"][0]).T)
    sc = i["state_conv"][0]
    a["state_conv"] = np.ascontiguousarray(ctile(sc).reshape(NB, CW - 1, SG, XT, P).transpose(2, 4, 3, 1, 0))
    a["conv_old"] = np.ascontiguousarray(sc[:, 1:])
    a["dt_bias"] = np.ascontiguousarray(np.broadcast_to(i["dt_bias"][0], (P, SH)))
    a["a_log"] = np.ascontiguousarray(np.broadcast_to(i["a_log"][0], (P, SH)))
    a["upper"] = np.triu(np.ones((P, P), np.float32))
    a["below"] = np.tril(np.ones((P, P), np.float32), -1)
    a["d_skip"] = np.ascontiguousarray(np.repeat(i["d_skip"][0], DI // SH).reshape(DI // P, P).T)
    a["norm_ssd"] = np.ascontiguousarray(i["norm_ssd"][0].reshape(DI // P, P).T)
    a["norm_final"] = np.ascontiguousarray(i["norm_final"].reshape(KT, P).T)
    ssm = i["state_ssm"][0].reshape(NB, SG, 4, P, DS)
    a["state_ssm"] = np.ascontiguousarray(ssm.transpose(1, 3, 2, 0, 4)).reshape(SG, P, 4 * NB * DS)
    a["cache_kidx"] = np.ascontiguousarray(i["cache_kidx"][0].transpose(0, 2, 1)).reshape(2 * NPOOL, ID * PAGE // 2)
    a["cache_k"] = np.ascontiguousarray(i["cache_k"][0].reshape(NPOOL * PAGE, NKV * HD))
    a["cache_v"] = np.ascontiguousarray(i["cache_v"][0].reshape(NPOOL * PAGE, NKV * HD))
    a["page_table"] = np.ascontiguousarray(i["page_table"].reshape(1, NB * NPAGE))
    a["half"] = (np.arange(P)[:, None] // HD == np.arange(2)[None, :]).astype(np.float32)
    a["iota"] = np.ascontiguousarray(np.broadcast_to(np.arange(TOPK, dtype=np.float16), (P, TOPK)))
    slots = np.zeros((P, NB, NPAGE, 3), np.float16)
    slots[..., 0] = np.arange(P)[:, None, None]
    slots[..., 2] = np.arange(NPAGE)
    a["slots"] = slots.reshape(P, NB * NPAGE, 3)
    a["slot"] = (np.arange(P)[:, None] + P * np.arange(2)[None, :]).astype(np.float32)
    a["rel_bias"] = np.ascontiguousarray(i["rel_bias"][:, HEADS])
    a["flip"] = np.ascontiguousarray(np.eye(P, dtype=np.float32)[::-1])
    a["ident"] = np.eye(P, dtype=np.float32)
    dist = np.maximum(255 - np.arange(512), 0)
    far = NBUCKET // 2 + (np.log(np.maximum(dist, 1).astype(np.float32) / (NBUCKET // 2)) / np.log(MAXD / (NBUCKET // 2))
                          * (NBUCKET - NBUCKET // 2)).astype(np.int32)
    bucket = np.where(dist < NBUCKET // 2, dist, np.minimum(far, NBUCKET - 1))
    a["hot"] = (np.arange(NBUCKET)[:, None] == bucket[None, :]).astype(np.float32)
    return a


HEADS = np.array([4 * (2 * m + u) + g for m in range(2) for g in range(4) for u in range(2)])
HEADCOLS = (HEADS[:, None] * HD + np.arange(HD)).reshape(-1)

OUTS = {"k": [P, 2, TOK], "kidx": [ID, TOK], "v_p": [P, TB, NKV * HD], "v_s": [NB, NKV * HD], "y": [P, KT, TOK],
        "conv_p": [SG, P, XT, CW - 1], "conv_s": [SG, P, XT, NB], "conv_old": [NB, CW - 2, CONVD], "ssm_p": [SG, P, DI // SG],
        "ssm_s": [SG, P, 4 * NB * DS]}
ORDER = np.concatenate([np.concatenate([np.arange(4) + 4 * g, [16 + g], [20 + g]]) for g in range(SG)])


def unlay(r):
    y = r["y"].transpose(2, 1, 0).reshape(TOK, DM)
    k = r["k"].transpose(2, 1, 0).reshape(TOK, NKV, HD)
    kidx = r["kidx"].T
    v = r["v_p"].transpose(1, 0, 2).reshape(1, 1, SEQ, NKV, HD)
    back = np.argsort(ORDER)
    conv_p = r["conv_p"].transpose(3, 0, 2, 1).reshape(CW - 1, SG * XT, P)[:, back].reshape(1, 1, CW - 1, CONVD)
    new = r["conv_s"].transpose(3, 0, 2, 1).reshape(NB, SG * XT, P)[:, back].reshape(NB, 1, CONVD)
    conv_s = np.concatenate([r["conv_old"], new], 1)[None]
    R, PD = SH // SG, DI // SH
    ssm_p = r["ssm_p"].reshape(SG, DS, R, PD).transpose(0, 2, 3, 1).reshape(1, 1, SH, PD, DS)
    ssm_s = r["ssm_s"].reshape(SG, 2, PD, R // 2, NB, DS).transpose(4, 0, 3, 1, 2, 5).reshape(1, NB, SH, PD, DS)
    out = (y[:SEQ][None], y[SEQ:][:, None], k[:SEQ][None, None], v, kidx[:SEQ][None, None], ssm_p, conv_p,
           k[SEQ:].reshape(1, NB, 1, NKV, HD), r["v_s"].reshape(1, NB, 1, NKV, HD), kidx[SEQ:].reshape(1, NB, 1, ID),
           ssm_s, conv_s)
    return tuple(np.ascontiguousarray(a) for a in out)


def kernel(**inputs):
    import concourse.bacc as bacc
    from concourse.bass_utils import run_bass_kernel_spmd

    nc = bacc.Bacc("TRN2", target_bir_lowering=False, num_devices=1)
    arrays = layout({n: np.asarray(a) for n, a in inputs.items()})
    d = {n: nc.dram_tensor(f"in_{n}", a.shape, mybir.dt.from_np(a.dtype), kind="ExternalInput").ap() for n, a in arrays.items()}
    o = {n: nc.dram_tensor(f"out_{n}", s, F32, kind="ExternalOutput").ap() for n, s in OUTS.items()}
    program(nc, d, o)
    r = run_bass_kernel_spmd(nc, [{f"in_{n}": a for n, a in arrays.items()}], core_ids=[0])
    return unlay({n: r.results[0][f"out_{n}"] for n in OUTS})
```
